# Optimizing a Trainium2 kernel written in Bass

```python
import math
import jax, jax.numpy as jnp
from jax import lax
import numpy as np

D_MODEL = 1024
BATCH = 1
SEQ = 512
DEPTH = 1

HEAD_DIM = 64
NSA_HEADS = 8
NSA_GROUPS = 2
NSA_HPG = NSA_HEADS // NSA_GROUPS
CMP_LEN = 32
CMP_STRIDE = 16
CMP_HIDDEN = 2 * HEAD_DIM
SLC_BLOCK = 64
SLC_TOPN = 8
WINDOW = 256
FORCE_BONUS = 1.0e4
DIFF_HEADS = 4
FOX_HEADS = 8
N_BRANCH = 3
BRANCH_WIDTH = 512
D_FF = 2816
CONV_W = 3
Q_BLOCK = 128
EPS = 1e-6
NEG = -1.0e30

NSA_Q = NSA_HEADS * HEAD_DIM
NSA_KV = 3 * 2 * NSA_GROUPS * HEAD_DIM
NSA_GATE = 3 * NSA_HEADS
DIFF_Q = DIFF_HEADS * 2 * HEAD_DIM
DIFF_K = DIFF_HEADS * 2 * HEAD_DIM
DIFF_V = DIFF_HEADS * 2 * HEAD_DIM
FOX_Q = FOX_HEADS * HEAD_DIM
FOX_K = FOX_HEADS * HEAD_DIM
FOX_V = FOX_HEADS * HEAD_DIM
FOX_F = FOX_HEADS
MERGE_G = N_BRANCH * D_MODEL
IN_SIZES = (NSA_Q, NSA_KV, NSA_GATE, DIFF_Q, DIFF_K, DIFF_V, FOX_Q, FOX_K, FOX_V, FOX_F, MERGE_G)
D_IN = NSA_Q + NSA_KV + NSA_GATE + DIFF_Q + DIFF_K + DIFF_V + FOX_Q + FOX_K + FOX_V + FOX_F + MERGE_G

kernel_name = "hybrid_nsa_diff_fox_convffn"

def rms_norm(x, g):
    xf = x.astype(jnp.float32)
    y = xf * lax.rsqrt(jnp.mean(xf * xf, axis=-1, keepdims=True) + EPS)
    return (y * g.astype(jnp.float32)).astype(x.dtype)

def alibi_slopes(n):
    return jnp.asarray(2.0 ** (-8.0 * np.arange(1, n + 1) / n), jnp.float32)

def masked_softmax(logits, mask):
    p = jax.nn.softmax(jnp.where(mask, logits, NEG), axis=-1)
    return jnp.where(mask, p, 0.0)

def unblock(y):
    y = jnp.moveaxis(y, 0, 1)
    return y.reshape((y.shape[0], y.shape[1] * y.shape[2]) + y.shape[3:])

def compress(raw, pe, w1, w2, idx):
    B = raw.shape[0]
    G, hd = raw.shape[2], raw.shape[3]
    nc, L = idx.shape
    blocks = raw[:, idx] + pe[:, None, :]
    flat = jnp.transpose(blocks, (0, 1, 3, 2, 4)).reshape(B, nc, G, L * hd)
    return jax.nn.gelu(flat @ w1) @ w2

def nsa_attention(q, k_cmp, v_cmp, k_slc, v_slc, k_win, v_win, gate_logits, cmp_end):
    B, S, H, hd = q.shape
    G, R = NSA_GROUPS, NSA_HPG
    nc = k_cmp.shape[1]
    ns = S // SLC_BLOCK
    n_sel = min(SLC_TOPN, ns)
    slopes = alibi_slopes(H).reshape(G, R)
    c_start = jnp.arange(nc) * CMP_STRIDE
    s_start = jnp.arange(ns) * SLC_BLOCK
    overlap = ((c_start[:, None] < s_start[None, :] + SLC_BLOCK)
               & (c_start[:, None] + CMP_LEN > s_start[None, :])).astype(jnp.float32)
    kb = jnp.transpose(k_slc.reshape(B, ns, SLC_BLOCK, G, hd), (0, 3, 1, 2, 4))
    vb = jnp.transpose(v_slc.reshape(B, ns, SLC_BLOCK, G, hd), (0, 3, 1, 2, 4))
    pad = ((0, 0), (WINDOW, 0), (0, 0), (0, 0))
    kw_pad = jnp.pad(k_win, pad)
    vw_pad = jnp.pad(v_win, pad)
    gather = jax.vmap(jax.vmap(lambda blocks, ix: blocks[ix]))
    blk_ids = jnp.arange(ns)
    sl = slopes[None, :, :, None]

    def chunk(c):
        t0 = c * Q_BLOCK
        tpos = t0 + jnp.arange(Q_BLOCK)
        qg = lax.dynamic_slice_in_dim(q, t0, Q_BLOCK, axis=1).reshape(B, Q_BLOCK, G, R, hd)
        dist_c = tpos[:, None] - cmp_end[None, :]
        s_c = jnp.einsum('btgrd,bngd->bgrtn', qg, k_cmp).astype(jnp.float32)
        s_c = s_c - sl[..., None] * dist_c.astype(jnp.float32)
        p_c = masked_softmax(s_c, dist_c >= 0)
        o_c = jnp.einsum('bgrtn,bngd->btgrd', p_c.astype(v_cmp.dtype), v_cmp)
        imp = jnp.einsum('bgrtn,nj->bgtj', p_c, overlap)
        cur = tpos // SLC_BLOCK
        causal_blk = blk_ids[None, :] <= cur[:, None]
        forced = ((blk_ids[None, :] == 0) | (blk_ids[None, :] == cur[:, None])
                  | (blk_ids[None, :] == cur[:, None] - 1))
        score = jnp.where(causal_blk, jnp.where(forced, imp + FORCE_BONUS, imp), NEG)
        sel = lax.top_k(score, n_sel)[1]
        ks = gather(kb, sel)
        vs = gather(vb, sel)
        spos = sel[..., None] * SLC_BLOCK + jnp.arange(SLC_BLOCK)
        dist_s = (tpos[None, None, :, None, None] - spos)[:, :, None]
        s_s = jnp.einsum('btgrd,bgtnkd->bgrtnk', qg, ks).astype(jnp.float32)
        s_s = s_s - sl[..., None, None] * dist_s.astype(jnp.float32)
        m = n_sel * SLC_BLOCK
        p_s = masked_softmax(s_s.reshape(B, G, R, Q_BLOCK, m),
                             (dist_s >= 0).reshape(B, G, 1, Q_BLOCK, m))
        o_s = jnp.einsum('bgrtm,bgtmd->btgrd', p_s.astype(vs.dtype),
                         vs.reshape(B, G, Q_BLOCK, m, hd))
        kw = lax.dynamic_slice_in_dim(kw_pad, t0, Q_BLOCK + WINDOW, axis=1)
        vw = lax.dynamic_slice_in_dim(vw_pad, t0, Q_BLOCK + WINDOW, axis=1)
        wpos = t0 - WINDOW + jnp.arange(Q_BLOCK + WINDOW)
        dist_w = tpos[:, None] - wpos[None, :]
        mask_w = (wpos[None, :] >= 0) & (dist_w >= 0) & (dist_w < WINDOW)
        s_w = jnp.einsum('btgrd,bsgd->bgrts', qg, kw).astype(jnp.float32)
        s_w = s_w - sl[..., None] * dist_w.astype(jnp.float32)
        p_w = masked_softmax(s_w, mask_w)
        o_w = jnp.einsum('bgrts,bsgd->btgrd', p_w.astype(vw.dtype), vw)
        gc = jax.nn.sigmoid(lax.dynamic_slice_in_dim(gate_logits, t0, Q_BLOCK, axis=1)
                            .reshape(B, Q_BLOCK, 3, G, R, 1))
        o = gc[:, :, 0] * o_c + gc[:, :, 1] * o_s + gc[:, :, 2] * o_w
        return o.reshape(B, Q_BLOCK, H * hd)

    return unblock(lax.map(chunk, jnp.arange(S // Q_BLOCK)))

def diff_attention(q, k, v, lam):
    B, S, H = q.shape[0], q.shape[1], q.shape[2]
    slopes = alibi_slopes(H)[None, :, None, None, None]
    kpos = jnp.arange(S)

    def chunk(c):
        t0 = c * Q_BLOCK
        tpos = t0 + jnp.arange(Q_BLOCK)
        qc = lax.dynamic_slice_in_dim(q, t0, Q_BLOCK, axis=1)
        dist = tpos[:, None] - kpos[None, :]
        s = jnp.einsum('bthcd,bshcd->bhcts', qc, k).astype(jnp.float32)
        s = s - slopes * dist.astype(jnp.float32)
        p = masked_softmax(s, dist >= 0)
        a = p[:, :, 0] - lam * p[:, :, 1]
        return jnp.einsum('bhts,bshe->bthe', a.astype(v.dtype), v)

    return unblock(lax.map(chunk, jnp.arange(S // Q_BLOCK)))

def forgetting_attention(q, k, v, log_f):
    S = q.shape[1]
    F = jnp.transpose(jnp.cumsum(log_f, axis=1), (0, 2, 1))
    kpos = jnp.arange(S)

    def chunk(c):
        t0 = c * Q_BLOCK
        tpos = t0 + jnp.arange(Q_BLOCK)
        qc = lax.dynamic_slice_in_dim(q, t0, Q_BLOCK, axis=1)
        Fc = lax.dynamic_slice_in_dim(F, t0, Q_BLOCK, axis=2)
        s = jnp.einsum('bthd,bshd->bhts', qc, k).astype(jnp.float32)
        s = s + Fc[..., :, None] - F[..., None, :]
        p = masked_softmax(s, tpos[:, None] >= kpos[None, :])
        return jnp.einsum('bhts,bshd->bthd', p.astype(v.dtype), v)

    return unblock(lax.map(chunk, jnp.arange(S // Q_BLOCK)))

def conv_ffn(h, w_up, conv_w, conv_b, w_down):
    S = h.shape[1]
    u, g = jnp.split(h @ w_up, 2, axis=-1)
    up = jnp.pad(u, ((0, 0), (CONV_W - 1, 0), (0, 0)))
    uc = conv_b
    for j in range(CONV_W):
        uc = uc + conv_w[j] * up[:, j:j + S]
    return (jax.nn.gelu(uc) * g) @ w_down

def setup_inputs(seed: int = 0) -> dict:
    key = jax.random.key(seed)
    ks = jax.random.split(key, 24)
    f32 = jnp.float32
    n = lambda k, shape, scale: (jax.random.normal(k, shape, f32) * scale)
    gain = lambda k, shape: 1.0 + 0.02 * jax.random.normal(k, shape, f32)
    L, hd = CMP_LEN, HEAD_DIM
    return {
        "x": jax.random.normal(ks[0], (BATCH, SEQ, D_MODEL), f32),
        "attn_norm_g": gain(ks[1], (DEPTH, D_MODEL)),
        "w_in": n(ks[2], (DEPTH, D_MODEL, D_IN), D_MODEL ** -0.5),
        "nsa_q_g": gain(ks[3], (DEPTH, hd)),
        "nsa_k_g": gain(ks[4], (DEPTH, 3, hd)),
        "cmp_pe": n(ks[5], (DEPTH, 2, L, hd), 0.02),
        "cmp_w1": n(ks[6], (DEPTH, 2, L * hd, CMP_HIDDEN), (L * hd) ** -0.5),
        "cmp_w2": n(ks[7], (DEPTH, 2, CMP_HIDDEN, hd), CMP_HIDDEN ** -0.5),
        "diff_q_g": gain(ks[8], (DEPTH, hd)),
        "diff_k_g": gain(ks[9], (DEPTH, hd)),
        "diff_lam": n(ks[10], (DEPTH, 4, hd), 0.1),
        "diff_subln_g": gain(ks[11], (DEPTH, 2 * hd)),
        "fox_q_g": gain(ks[12], (DEPTH, hd)),
        "fox_k_g": gain(ks[13], (DEPTH, hd)),
        "fox_b": jax.random.uniform(ks[14], (DEPTH, FOX_HEADS), f32, 1.0, 4.0),
        "w_br": n(ks[15], (DEPTH, N_BRANCH, BRANCH_WIDTH, D_MODEL), BRANCH_WIDTH ** -0.5),
        "w_o": n(ks[16], (DEPTH, D_MODEL, D_MODEL), D_MODEL ** -0.5),
        "ffn_norm_g": gain(ks[17], (DEPTH, D_MODEL)),
        "w_up": n(ks[18], (DEPTH, D_MODEL, 2 * D_FF), D_MODEL ** -0.5),
        "conv_w": n(ks[19], (DEPTH, CONV_W, D_FF), CONV_W ** -0.5),
        "conv_b": n(ks[20], (DEPTH, D_FF), 0.02),
        "w_down": n(ks[21], (DEPTH, D_FF, D_MODEL), D_FF ** -0.5),
    }

def reference(x, attn_norm_g, w_in, nsa_q_g, nsa_k_g, cmp_pe, cmp_w1, cmp_w2,
              diff_q_g, diff_k_g, diff_lam, diff_subln_g, fox_q_g, fox_k_g, fox_b,
              w_br, w_o, ffn_norm_g, w_up, conv_w, conv_b, w_down):
    B, S, D = x.shape
    hd = HEAD_DIM
    scale = hd ** -0.5
    split_points = [int(v) for v in np.cumsum(IN_SIZES)[:-1]]
    nc = (S - CMP_LEN) // CMP_STRIDE + 1
    cmp_idx = jnp.arange(nc)[:, None] * CMP_STRIDE + jnp.arange(CMP_LEN)[None, :]
    cmp_end = cmp_idx[:, -1]
    h = x
    for l in range(DEPTH):
        a = rms_norm(h, attn_norm_g[l])
        (nq, nkv, ngate, dq, dk, dv, fq, fk, fv, ff, mg) = jnp.split(a @ w_in[l], split_points, axis=-1)

        qa = rms_norm(nq.reshape(B, S, NSA_HEADS, hd), nsa_q_g[l]) * scale
        kv = nkv.reshape(B, S, 3, 2, NSA_GROUPS, hd)
        k_cmp = rms_norm(compress(kv[:, :, 0, 0], cmp_pe[l, 0], cmp_w1[l, 0], cmp_w2[l, 0], cmp_idx),
                         nsa_k_g[l, 0])
        v_cmp = compress(kv[:, :, 0, 1], cmp_pe[l, 1], cmp_w1[l, 1], cmp_w2[l, 1], cmp_idx)
        k_slc = rms_norm(kv[:, :, 1, 0], nsa_k_g[l, 1])
        k_win = rms_norm(kv[:, :, 2, 0], nsa_k_g[l, 2])
        o_a = nsa_attention(qa, k_cmp, v_cmp, k_slc, kv[:, :, 1, 1], k_win, kv[:, :, 2, 1],
                            ngate.reshape(B, S, 3, NSA_HEADS), cmp_end)

        lam_init = 0.8 - 0.6 * math.exp(-0.3 * l)
        lv = diff_lam[l].astype(jnp.float32)
        lam = jnp.exp(jnp.sum(lv[0] * lv[1])) - jnp.exp(jnp.sum(lv[2] * lv[3])) + lam_init
        qb = rms_norm(dq.reshape(B, S, DIFF_HEADS, 2, hd), diff_q_g[l]) * scale
        kb = rms_norm(dk.reshape(B, S, DIFF_HEADS, 2, hd), diff_k_g[l])
        ob = diff_attention(qb, kb, dv.reshape(B, S, DIFF_HEADS, 2 * hd), lam)
        o_b = (rms_norm(ob, diff_subln_g[l]) * (1.0 - lam_init)).reshape(B, S, BRANCH_WIDTH)

        qc = rms_norm(fq.reshape(B, S, FOX_HEADS, hd), fox_q_g[l]) * scale
        kc = rms_norm(fk.reshape(B, S, FOX_HEADS, hd), fox_k_g[l])
        log_f = jax.nn.log_sigmoid((ff + fox_b[l]).astype(jnp.float32))
        o_c = forgetting_attention(qc, kc, fv.reshape(B, S, FOX_HEADS, hd), log_f).reshape(B, S, BRANCH_WIDTH)

        gates = jax.nn.sigmoid(mg.reshape(B, S, N_BRANCH, D))
        merged = (gates[:, :, 0] * (o_a @ w_br[l, 0]) + gates[:, :, 1] * (o_b @ w_br[l, 1])
                  + gates[:, :, 2] * (o_c @ w_br[l, 2]))
        h = h + merged @ w_o[l]

        h = h + conv_ffn(rms_norm(h, ffn_norm_g[l]), w_up[l], conv_w[l], conv_b[l], w_down[l])
    return h


_drawn_inputs = setup_inputs


def setup_inputs(seed=0):
    import zlib

    import numpy as np

    out = dict(_drawn_inputs(seed))
    spreads = {}
    factors = {'attn_norm_g': 3.057,
     'nsa_q_g': 8.0,
     'nsa_k_g': 8.0,
     'cmp_pe': 8.0,
     'diff_q_g': 7.556,
     'diff_k_g': 6.541,
     'diff_subln_g': 6.041,
     'fox_q_g': 8.0,
     'fox_k_g': 8.0,
     'ffn_norm_g': 3.997,
     'conv_b': 5.638}
    for name, (base, spread) in spreads.items():
        noise = np.random.default_rng([zlib.crc32(name.encode()), seed]).standard_normal(out[name].shape)
        drawn = base * np.exp(spread * noise) if base else spread * noise
        out[name] = __import__('jax').numpy.asarray(drawn.astype(out[name].dtype))
    for name, factor in factors.items():
        out[name] = (out[name] * factor).astype(out[name].dtype)
    return out
```

```python
import concourse.bass as bass
from concourse import mybir
from contextlib import ExitStack

P = 128
S = 512
D = 1024
HD = 64
TT = S // P
KD = D // P
D_FF = 2816
NF = D_FF // P
NCMP = 31
EPS = 1e-6
LAM_INIT = 0.2
BLOCK = 2048

C_ATTN, C_FFN = 0, 8
C_CONVW = 16
C_CONVB = C_CONVW + 3 * NF
C_SUBLN = C_CONVB + NF
C_QG = C_SUBLN + 1
C_KG = C_QG + 3
C_PE = C_KG + 5
C_LAM = C_PE + 32
C_FOXB = C_LAM + 4 * HD
C_END = C_FOXB + 8
K_ID, K_D, K_W, K_M, K_DC, K_SEL, K_VALID, K_U = 0, 128, 640, 1152, 1280, 1408, 2432, 2433
K_END = 3329

NSA, DIFF, FOX = 0, 1, 2
PROJ = {NSA: ["cmp", "nq0", "nq1", "slc", "win", "small"],
        DIFF: ["dq0", "dq1", "dk0", "dk1", "dv0", "dv1"],
        FOX: ["fq0", "fq1", "fk0", "fk1", "fv0", "fv1"]}
BLOCKS = []
for _m in (NSA, DIFF, FOX):
    BLOCKS += [(_m, n) for n in PROJ[_m]] + [(_m, f"gate{n}") for n in range(4)] + [(_m, f"br{n}") for n in range(2)]
BLOCKS += [("wo", n) for n in range(4)]
BI = {n: i for i, n in enumerate(BLOCKS)}
B_UP = len(BLOCKS)
N_UP = D_FF // 256
B_DOWN = B_UP + 2 * N_UP
N_DOWN = NF // 2
N_BLOCKS = B_DOWN + N_DOWN
assert B_UP % 2 == 0

SLOPES8 = [2.0 ** -(h + 1) for h in range(8)]


def units_of(m):
    if m == NSA:
        return [(k, h, 0, i) for h in range(8) for i in range(TT) for k in ("slc", "win")]
    if m == DIFF:
        return [("diff", h, c, i) for h in range(4) for i in range(TT) for c in range(2)]
    return [("fox", h, 0, i) for h in range(8) for i in range(TT)]


def span(u):
    kind, h, c, i = u
    s0 = max(0, i - 2) * P if kind == "win" else 0
    return s0, (i + 1) * P - s0


FILL = 4 * 2 * KD * 3


def fill_range(m, j):
    n = -(-FILL // len(units_of(m)))
    return min(FILL, j * n), min(FILL, (j + 1) * n)


def has_pv(m, j):
    return m != DIFF or j % 2 == 1


def pv_index(m, j):
    return j // 2 if m == DIFF else j


T_LAG, O_LAG = 2, 3


def build(nc, x, wblk, w1, w2, params, consts, out):
    f32, f32r = mybir.dt.float32, mybir.dt.float32r
    ACT, ALU, AX = mybir.ActivationFunctionType, mybir.AluOpType, mybir.AxisListType
    KB = 1024

    place, results = {}, [0] * 8

    def plan(key, bank):
        place[key] = (bank, results[bank])
        results[bank] += 1

    tn = 0

    def plan_t(key):
        nonlocal tn
        plan(key, 4 + tn % 2)
        tn += 1

    def plan_post(m, name):
        for n in T_CHUNKS.get(name, []):
            plan_t(("T", m, name, n))

    T_CHUNKS = {n: [0, 1] for n in ("nq0", "nq1", "slc", "win", "dq0", "dq1", "dk0", "dk1", "fq0", "fq1", "fk0", "fk1")}
    for k in range(KD):
        plan(("N", 0, k), k)
    for m in (NSA, DIFF, FOX):
        prev = None
        for name in PROJ[m]:
            b = BI[(m, name)]
            for half in range(1 if name == "small" else 2):
                plan(("P", m, name, half), (b % 2) * 2 + half)
            if prev:
                plan_post(m, prev)
            prev = name
        plan_post(m, prev)
        if m == NSA:
            for kv in range(2):
                plan(("H", kv), kv)
            plan(("KC",), 2)
            plan(("VC",), 3)
            plan_t(("KCT",))
            for i in range(TT):
                for e in range(2):
                    plan(("SC", i, e), 6 + e)
                plan_t(("TC", i))
                for e in range(2):
                    plan(("OC", i, e), 2 + e)
        if m == FOX:
            plan(("F",), 6)
        U = len(units_of(m))
        for j in range(U + O_LAG):
            if j < U:
                plan(("S", m, j), 6 + j % 2)
                f0, f1 = fill_range(m, j)
                for f in range(f0, f1):
                    if f % (KD * 3) == 0:
                        plan(("G", m, f // (KD * 3)), (f // (KD * 3)) % 2)
            if T_LAG <= j < U + T_LAG and has_pv(m, j - T_LAG):
                plan_t(("A", m, j - T_LAG))
            if j >= O_LAG and has_pv(m, j - O_LAG):
                plan(("O", m, j - O_LAG), 2 + pv_index(m, j - O_LAG) % 2)
        for k in range(4):
            plan_t(("OT", m, k))
        for c in range(KD):
            plan(("B", m, c), c % 4)
    for n in range(4):
        for half in range(2):
            plan(("WO", n, half), (n % 2) * 2 + half)
    for k in range(KD):
        plan(("N", 1, k), k)
    up0 = list(results)
    for b in range(4):
        results[b] += N_UP
    for d in range(KD):
        plan(("Y", d), d)
    for d in range(KD):
        plan(("YT", d), d)

    with ExitStack() as ctx:
        base = -(-nc.sbuf_base // 64) * 64
        used = [0]

        def at(name, shape, dt, off):
            size = 4
            for s in shape[1:]:
                size *= s
            used[0] = max(used[0], off + size)
            return nc.alloc_sbuf_tensor_at(name, shape, dt, offset=base + off)

        aT_h = at("aT_h", [P, KD, S], f32r, 0)
        aT_l = at("aT_l", [P, KD, S], f32r, 16 * KB)
        raw = [at(f"raw{i}", [P, BLOCK], f32, (32 + 8 * i) * KB) for i in range(2)]
        wh = [at(f"wh{i}", [P, BLOCK], f32r, (48 + 8 * i) * KB) for i in range(2)]
        wl = [at(f"wl{i}", [P, BLOCK], f32r, (64 + 8 * i) * KB) for i in range(2)]
        RX = 80 * KB
        x0 = at("x0", [P, TT, D], f32, RX)
        nrm = [at(f"nrm{i}", [P, TT, 256], f32, RX + 4 * KB * i) for i in range(2)]
        prob = at("prob", [P, 6, S], f32, RX)
        probT = at("probT", [P, 2, S], f32, RX + 12 * KB)
        bt = at("bt", [P, 2, S], f32, RX + 12 * KB)
        hid = at("hid", [P, TT, D], f32, RX)
        RA = 96 * KB
        stage = at("stage", [P, K_U], f32, RA)
        xn0 = at("xn0", [P, TT, D], f32, RA + 16 * KB)
        xn1 = at("xn1", [P, TT, D], f32, RA + 48 * KB)
        qk_h = at("qk_h", [P, 8, S], f32r, RA)
        qk_l = at("qk_l", [P, 8, S], f32r, RA + 16 * KB)
        oT_h = at("oT_h", [P, 4, S], f32r, RA)
        oT_l = at("oT_l", [P, 4, S], f32r, RA + 8 * KB)
        mT_h = at("mT_h", [P, KD, S], f32r, RA + 16 * KB)
        mT_l = at("mT_l", [P, KD, S], f32r, RA + 32 * KB)
        V = at("V", [P, TT, S], f32, RA + 32 * KB)
        otok = at("otok", [P, TT, S], f32, RA + 40 * KB)
        gate = at("gate", [P, KD, S], f32, RA + 48 * KB)
        w1_sb = at("w1_sb", [P, 2, 16, P], f32, RA + 48 * KB)
        merged = at("merged", [P, KD, S], f32, RA + 64 * KB)
        RM = RA + 64 * KB
        cx = at("cx", [P, 2, S], f32, RM)
        cpe = at("cpe", [P, 2, 16, 2, 32], f32, RM + 4 * KB)
        pc = at("pc", [P, 2, 2, 4, 32], f32, RM)
        pcT = at("pcT", [P, 2, P], f32, RM + 2 * KB)
        w2_sb = at("w2_sb", [P, 2, HD], f32, RM + 12 * KB)
        chid = at("chid", [P, 2, P], f32, RM + 12 * KB + 512)
        ktok = at("ktok", [HD, 2, HD], f32, RM + 13 * KB + 512)
        ksq = at("ksq", [HD, HD], f32, RM + 14 * KB)
        kc_h = at("kc_h", [P, 2, 32], f32r, RM + 14 * KB + 256)
        kc_l = at("kc_l", [P, 2, 32], f32r, RM + 14 * KB + 512)
        vblk = at("vblk", [P, 4, HD], f32, RM + 15 * KB)
        sq = at("sq", [P, 2, S], f32, RA + 80 * KB)
        RC = RA + 84 * KB
        slopeI = at("slopeI", [P, 8, P], f32r, RC)
        distD = at("distD", [P, S], f32r, RC + 4 * KB)
        distW = at("distW", [P, S], f32r, RC + 6 * KB)
        causal = at("causal", [P, P], f32r, RC + 8 * KB)
        distC = at("distC", [P, TT, 32], f32r, RC + 8 * KB + 512)
        sel = at("sel", [P, 8, P], f32r, RC + 9 * KB)
        later = at("later", [P, 896], f32, RC + 13 * KB)
        fT = at("fT", [P, S], f32r, RC + 16 * KB + 512)
        actT_h = at("actT_h", [P, NF, S], f32r, RA)
        actT_l = at("actT_l", [P, NF, S], f32r, RA + 44 * KB)
        uc = at("uc", [P, 2, S], f32, RA + 88 * KB)
        gl = at("gl", [P, 2, S], f32, RA + 92 * KB)
        av = at("av", [P, 2, S], f32, RA + 96 * KB)
        yT = at("yT", [P, KD, S], f32, 0)
        outt = at("outt", [P, TT, D], f32, 32 * KB)
        RK = RC + 18 * KB + 512
        ident = at("ident", [P, P], f32, RK)
        identr = at("identr", [P, P], f32r, RK + 512)
        par = at("par", [P, C_END], f32, RK + KB)
        RS = RK + KB + -(-4 * C_END // 32) * 32
        so = [RS]

        def small(name, shape, dt=f32):
            t = at(name, shape, dt, so[0])
            n = 4
            for s in shape[1:]:
                n *= s
            so[0] += -(-n // 32) * 32
            return t

        ss = small("ss", [P, TT])
        lnv = small("lnv", [P, 16])
        rstd = small("rstd", [P, 16])
        hss = small("hss", [P, TT, 4])
        nmx = small("nmx", [P, 64])
        lsum = small("lsum", [P, 64])
        rl = small("rl", [P, 64])
        coef = small("coef", [P, 64])
        cmx = small("cmx", [P, 8])
        csum = small("csum", [P, 8])
        crl = small("crl", [P, 8])
        ccoef = small("ccoef", [P, 8])
        smallt = small("smallt", [P, TT, 32])
        gsm = small("gsm", [P, TT, 24])
        logf = small("logf", [P, TT, 8])
        lf1 = small("lf1", [P, TT, 8])
        lf2 = small("lf2", [P, TT, 8])
        lamt = small("lamt", [P, 2])
        lame = small("lame", [P, 2])
        neglam = small("neglam", [P, 1])
        epsc = small("epsc", [P, 1])
        valid = small("valid", [P, 1])
        kss = small("kss", [HD, 1])
        assert base + used[0] <= nc.sbuf_usable_end, (base + used[0], nc.sbuf_usable_end)

        ps = [ctx.enter_context(nc.psum_tensor(f"ps{i}", [P, S], f32)) for i in range(8)]

        def sem(name):
            return ctx.enter_context(nc.semaphore(name))

        psum_full = [sem(f"psum_full{i}") for i in range(8)]
        psum_free = [sem(f"psum_free{i}") for i in range(8)]
        raw_in = [sem(f"raw_in{i}") for i in range(2)]
        hi_ready = sem("hi_ready")
        lo_ready = sem("lo_ready")
        down_used = sem("down_used")
        x_in, par_in, const_in, cw_in, h_in = (sem(n) for n in ("x_in", "par_in", "const_in", "cw_in", "h_in"))
        consts_ready = sem("consts_ready")
        act_link, dve_link = sem("act_link"), sem("dve_link")
        ss_ready = sem("ss_ready")
        xn_ready = sem("xn_ready")
        hi_taken = sem("hi_taken")
        sq_ready = sem("sq_ready")
        hss_ready = sem("hss_ready")
        rstd_ready = sem("rstd_ready")
        max_ready = sem("max_ready")
        comb_ready = sem("comb_ready")
        cexp_ready = sem("cexp_ready")
        small_v, small_a = sem("small_v"), sem("small_a")
        cpe_ready = sem("cpe_ready")
        ksq_ready, kss_ready = sem("ksq_ready"), sem("kss_ready")
        sub_ready = sem("sub_ready")
        conv_step = sem("conv_step")
        gelu_ready, act_hi = sem("gelu_ready"), sem("act_hi")
        act_lo = sem("act_lo")
        merged_ready = sem("merged_ready")
        merged_hi, merged_lo = sem("merged_hi"), sem("merged_lo")
        out_ready, out_done = sem("out_ready"), sem("out_done")

        def free(eng, key):
            b, r = place[key]
            eng.wait_ge(psum_free[b], r + 1)

        def full(eng, key):
            b, r = place[key]
            eng.wait_ge(psum_full[b], r + 1)

        last_result = {}
        for m in (NSA, DIFF, FOX):
            for name in PROJ[m]:
                last_result[BI[(m, name)]] = ("P", m, name, 0 if name == "small" else 1)
            for n in range(4):
                last_result[BI[(m, f"gate{n}")]] = ("G", m, 2 * n + 1)
            for n in range(2):
                last_result[BI[(m, f"br{n}")]] = ("B", m, 4 * n + 3)
        for n in range(4):
            last_result[BI[("wo", n)]] = ("WO", n, 1)

        def bank(key):
            return ps[place[key][0]]

        hi_order = [("N", 0, k) for k in range(KD)]
        for m in (NSA, DIFF, FOX):
            for name in PROJ[m]:
                hi_order += [("T", m, name, c) for c in T_CHUNKS.get(name, [])]
            if m == NSA:
                hi_order += [("KCT",)]
            if m == FOX:
                hi_order += [("F",)]
            hi_order += [("OT", m, k) for k in range(4)]
        hi_order += [("N", 1, k) for k in range(KD)]
        hi_at = {k: n + 1 for n, k in enumerate(hi_order)}

        QK_CHUNK = {"nq0": 0, "nq1": 2, "slc": 4, "win": 6, "dq0": 0, "dq1": 2, "dk0": 4, "dk1": 6,
                    "fq0": 0, "fq1": 2, "fk0": 4, "fk1": 6}
        GAIN = {"nq0": C_QG, "nq1": C_QG, "slc": C_KG + 1, "win": C_KG + 2, "dq0": C_QG + 1, "dq1": C_QG + 1,
                "dk0": C_KG + 3, "dk1": C_KG + 3, "fq0": C_QG + 2, "fq1": C_QG + 2, "fk0": C_KG + 4, "fk1": C_KG + 4}
        NORM_JOBS = [(m, n) for m in (NSA, DIFF, FOX) for n in PROJ[m] if n in T_CHUNKS]
        NORMS = [n for m, n in NORM_JOBS]
        rs_order = [("N", 0)]
        for m in (NSA, DIFF, FOX):
            rs_order += [n for n in PROJ[m] if n in T_CHUNKS]
            if m == NSA:
                rs_order += [("KC",)]
            if m == DIFF:
                rs_order += [("SUB",)]
        rs_order += [("N", 1)]
        rs_at = {k: n + 1 for n, k in enumerate(rs_order)}

        def operands(m, u):
            kind, h, c, i = u
            s0, n = span(u)
            if kind in ("slc", "win"):
                b, qc, kc = 64 * (h % 2), h // 2, (4 if kind == "slc" else 6) + h // 4
            elif kind == "diff":
                b, qc, kc = 64 * c, h, 4 + h
            else:
                b, qc, kc = 64 * (h % 2), h // 2, 4 + h // 2
            return slice(b, b + 64), qc, kc

        def unit_no(m, j):
            return sum(len(units_of(q)) for q in range(m)) + j

        def v_cols(u):
            kind, h, c, i = u
            if kind == "slc":
                return h // 4 * 64, 64
            if kind == "win":
                return 128 + h // 4 * 64, 64
            if kind == "diff":
                return h * P, P
            return h * 64, 64

        block = ctx.enter_context(nc.Block())

        @block.sync
        def _(sp):
            sp.dma_start(x0[:, :, :], x[0].rearrange("(t p) d -> p t d", p=P)).then_inc(x_in, 16)
            sp.dma_start(par[:, :], params).then_inc(par_in, 16)

            def load(b, slot, first):
                if not first:
                    sp.wait_ge(lo_ready, b - 1)
                sp.dma_start(raw[slot][:, :], wblk[bass.ds(b, 1)].rearrange("o p n -> p (o n)")).then_inc(raw_in[slot], 16)

            load(0, 0, True)
            load(1, 1, True)
            sp.dma_start(stage[:, :], consts[:, 0:K_U]).then_inc(const_in, 16)
            sp.dma_start(later[:, :], consts[:, K_U:K_U + 896]).then_inc(const_in, 16)
            sp.dma_start(w1_sb[:, :, :, :], w1).then_inc(cw_in, 16)
            sp.dma_start(w2_sb[:, :, :], w2).then_inc(cw_in, 16)
            with sp.Fori(2, BI[("wo", 2)], 2) as i:
                load(i, 0, False)
                load(i + 1, 1, False)
            sp.wait_ge(merged_ready, 16)
            sp.dma_start(hid[:, :, :], x[0].rearrange("(t p) d -> p t d", p=P)).then_inc(h_in, 16)
            with sp.Fori(BI[("wo", 2)], N_BLOCKS - 1, 2) as i:
                load(i, 0, False)
                load(i + 1, 1, False)
            load(N_BLOCKS - 1, (N_BLOCKS - 1) % 2, False)
            outv = out[0].rearrange("(t p) d -> p t d", p=P)
            for n in range(4):
                sp.wait_ge(out_ready, 2 * n + 2)
                sp.dma_start(outv[:, :, n * 256:(n + 1) * 256], outt[:, :, n * 256:(n + 1) * 256]).then_inc(out_done, 16)
            sp.wait_ge(out_done, 64)

        @block.scalar
        def _(act):
            links = [0]

            def link(ins):
                links[0] += 1
                ins.then_inc(act_link, 1)
                act.wait_ge(act_link, links[0])

            def split_hi(slot, fills):
                act.wait_ge(raw_in[slot], fills * 16)
                nc.scalar.activation(wh[slot][:, :], raw[slot][:, :], ACT.Copy).then_inc(hi_ready, 1)

            def split(b):
                if b >= 2:
                    full(act, last_result[b - 2])
                split_hi(b % 2, b // 2 + 1)

            def take_hi(key, dst, src, scale):
                full(act, key)
                nc.scalar.activation(dst, src, ACT.Copy, scale=scale).then_inc(hi_taken, 1)

            def inv_rms(key, src, n, width):
                link(nc.scalar.activation(lnv[0:src.shape[0], 0:n], src, ACT.Ln, scale=1.0 / width,
                                          bias=epsc[0:src.shape[0], :]))
                nc.scalar.activation(rstd[0:src.shape[0], 0:n], lnv[0:src.shape[0], 0:n], ACT.Exp,
                                     scale=-0.5).then_inc(rstd_ready, 1)

            def norm_tokens(p, src):
                for t in range(TT):
                    if p == 1 and t == 0:
                        for n in (2, 3):
                            for half in range(2):
                                free(act, ("WO", n, half))
                    link(nc.scalar.activation(sq[:, :, :].rearrange("p a n -> p (a n)"), src[:, t, :], ACT.Square,
                                              accum_out=ss[:, t:t + 1]))
                inv_rms(("N", p), ss[:, :], TT, D)
                for k in range(KD):
                    g = (C_ATTN if p == 0 else C_FFN) + k
                    take_hi(("N", p, k), aT_h[:, k, :], bank(("N", p, k))[:, :], par[:, g:g + 1])

            def post(m, name):
                if name in T_CHUNKS:
                    w = P if name in ("slc", "win") else 256
                    n = NORMS.index(name)
                    for half in range(2):
                        full(act, ("P", m, name, half))
                        src = bank(("P", m, name, half))[:, :].rearrange("p (t c) -> p t c", t=2)
                        if name in ("slc", "win"):
                            vc = 0 if name == "slc" else P
                            nc.scalar.activation(V[:, 2 * half:2 * half + 2, vc:vc + P], src[:, :, P:], ACT.Copy)
                        nc.scalar.activation(sq[:, half, 0:2 * w].rearrange("p (t c) -> p t c", t=2), src[:, :, 0:w],
                                             ACT.Square).then_inc(sq_ready, 1)
                    act.wait_ge(hss_ready, 2 * (n + 1) + sub_extra(m))
                    inv_rms(name, hss[:, :, :].rearrange("p t h -> p (t h)"), 16, HD)
                elif name in ("dv0", "dv1", "fv0", "fv1"):
                    vc = 256 * int(name[2])
                    for half in range(2):
                        full(act, ("P", m, name, half))
                        b = place[("P", m, name, half)][0]
                        nc.scalar.activation(V[:, 2 * half:2 * half + 2, vc:vc + 256],
                                             ps[b][:, :].rearrange("p (t c) -> p t c", t=2), ACT.Copy).then_inc(psum_free[b], 1)

            def post_t(m, name):
                for c in T_CHUNKS.get(name, []):
                    g = GAIN[name]
                    take_hi(("T", m, name, c), qk_h[:, QK_CHUNK[name] + c, :], bank(("T", m, name, c))[:, :], par[:, g:g + 1])

            def sub_extra(m):
                return 2 if m == FOX else 0

            act.wait_ge(x_in, 16)
            act.wait_ge(small_v, 1)
            split(0)
            split(1)
            act.wait_ge(par_in, 16)
            norm_tokens(0, x0)

            for m in (NSA, DIFF, FOX):
                units = units_of(m)
                prev = None
                for name in PROJ[m]:
                    b = BI[(m, name)]
                    if prev is not None:
                        split(b + 1)
                        post(m, prev)
                        post_t(m, prev)
                    prev = name
                split(BI[(m, prev)] + 2)
                post(m, prev)
                post_t(m, prev)
                if m == NSA:
                    act.wait_ge(small_v, 2)
                    nc.scalar.activation(gsm[:, :, :], smallt[:, :, 0:24], ACT.Exp, scale=-1.0).then_inc(small_a, 1)
                    link(nc.scalar.activation(lf1[:, :, :], logf[:, :, :], ACT.Abs))
                    link(nc.scalar.activation(lf1[:, :, :], lf1[:, :, :], ACT.Exp, scale=-1.0))
                    nc.scalar.activation(lf2[:, :, :], lf1[:, :, :], ACT.Ln, bias=1.0).then_inc(small_a, 1)
                    act.wait_ge(small_v, 4)
                    nc.scalar.activation(lame[:, :], lamt[:, :], ACT.Exp).then_inc(small_a, 1)
                    full(act, ("H", 0))
                    b = place[("H", 0)][0]
                    nc.scalar.activation(chid[:, 0, 0:64], ps[b][:, 0:64], ACT.Gelu_apprx_tanh).then_inc(psum_free[b], 1)
                    full(act, ("H", 1))
                    b = place[("H", 1)][0]
                    hv = chid[:, 1, :].rearrange("p (g r n) -> p g r n", g=2, r=2)
                    for r in range(2):
                        ins = nc.scalar.activation(hv[:, :, r, :], ps[b][:, 0:64].rearrange("p (g n) -> p g n", g=2),
                                                   ACT.Gelu_apprx_tanh)
                        if r == 1:
                            ins.then_inc(psum_free[b], 1)
                    full(act, ("KC",))
                    nc.scalar.activation(ksq[:, :], bank(("KC",))[0:HD, 0:HD], ACT.Square).then_inc(ksq_ready, 1)
                    act.wait_ge(kss_ready, 1)
                    inv_rms(("KC",), kss[:, :], 1, HD)
                    take_hi(("KCT",), kc_h[:, :, :], bank(("KCT",))[:, 0:64].rearrange("p (g n) -> p g n", g=2),
                            par[:, C_KG:C_KG + 1])
                    for i in range(TT):
                        for e in range(2):
                            free(act, ("SC", i, e))
                        nc.scalar.activation(pc[:, i % 2], pc[:, i % 2], ACT.Exp).then_inc(cexp_ready, 1)
                        b = place[("TC", i)][0]
                        full(act, ("TC", i))
                        if i >= 1:
                            full(act, ("OC", i - 1, 1))
                        nc.scalar.activation(pcT[:, :, :], ps[b][:, 0:256].rearrange("p (e t) -> p e t", e=2),
                                             ACT.Copy).then_inc(psum_free[b], 1)
                if m == FOX:
                    full(act, ("F",))
                    nc.scalar.activation(fT[0:8, :], bank(("F",))[0:8, :], ACT.Copy, scale=-1.0).then_inc(hi_taken, 1)
                U = len(units)
                for j in range(U + O_LAG):
                    if j < U:
                        s0, n = span(units[j])
                        b = place[("S", m, j)][0]
                        act.wait_ge(max_ready, unit_no(m, j) + 1)
                        nc.scalar.activation(prob[:, j % 4, 0:n], ps[b][:, 0:n], ACT.Exp, bias=nmx[:, j:j + 1],
                                             accum_out=lsum[:, j:j + 1]).then_inc(psum_free[b], 1)
                    q = j - T_LAG
                    if 0 <= q < U and has_pv(m, q) and pv_index(m, q) % 2 == 1:
                        s0, n = span(units[q])
                        b = place[("A", m, q)][0]
                        full(act, ("A", m, q))
                        nc.scalar.activation(probT[:, 1, 0:n], ps[b][:, 0:n], ACT.Copy).then_inc(psum_free[b], 1)
                    if j < U:
                        f0, f1 = fill_range(m, j)
                        for f in range(f0, f1):
                            if (f + 1) % (2 * KD * 3) == 0:
                                split(BI[(m, "gate0")] + f // (2 * KD * 3) + 2)
                            if (f + 1) % (KD * 3) == 0:
                                c = f // (KD * 3)
                                full(act, ("G", m, c))
                                if m > NSA:
                                    free(act, ("B", m - 1, c))
                                b = place[("G", m, c)][0]
                                nc.scalar.activation(gate[:, c, :], ps[b][:, :], ACT.Tanh, scale=0.5).then_inc(psum_free[b], 1)
                if m == DIFF:
                    for half in range(2):
                        free(act, ("O", m, U - 1))
                        if half == 0:
                            free(act, ("O", m, U - 3))
                        nc.scalar.activation(sq[:, :, :], otok[:, 2 * half:2 * half + 2, :], ACT.Square).then_inc(sq_ready, 1)
                        if half == 0:
                            act.wait_ge(hss_ready, 2 * len([n for n in NORMS if n[0] in "nswd"]) + 1)
                    act.wait_ge(hss_ready, 2 * len([n for n in NORMS if n[0] in "nswd"]) + 2)
                    inv_rms(("SUB",), hss[:, :, :].rearrange("p t h -> p (t h)"), 16, P)
                for k in range(4):
                    take_hi(("OT", m, k), oT_h[:, k, :], bank(("OT", m, k))[:, :],
                            par[:, C_SUBLN:C_SUBLN + 1] if m == DIFF else 1.0)
                for c in range(KD):
                    if c % 4 == 3:
                        split(BI[(m, f"br{c // 4}")] + 2)
                    if m == FOX:
                        act.wait_ge(merged_ready, KD + c + 1)
                        nc.scalar.activation(mT_h[:, c, :], merged[:, c, :], ACT.Copy, scale=0.5).then_inc(merged_hi, 1)
            for n in range(4):
                split(BI[("wo", n)] + 2)
            norm_tokens(1, hid)

            with act.Fori(0, N_UP) as i:
                for c in range(2):
                    act.wait_ge(psum_free[c], i + (up0[c] + 1))
                    nc.scalar.activation(gl[:, c, :], uc[:, c, :], ACT.Gelu_apprx_tanh).then_inc(gelu_ready, 1)
                    if c == 0:
                        act.wait_ge(psum_full[1], i + (up0[1] + 1))
                        split_hi(0, i + (B_UP // 2 + 2))
                for c in range(2):
                    act.wait_ge(psum_free[2 + c], i + (up0[2 + c] + 1))
                    nc.scalar.activation(actT_h[:, bass.ds(2 * i + c, 1), :].rearrange("p o n -> p (o n)"),
                                         av[:, c, :], ACT.Copy).then_inc(act_hi, 1)
                act.wait_ge(psum_full[3], i + (up0[3] + 1))
                split_hi(1, i + (B_UP // 2 + 2))
            for n in range(2, N_DOWN):
                act.wait_ge(down_used, n - 1)
                split_hi(n % 2, (B_DOWN + n) // 2 + 1)
            for d in range(0, KD, 2):
                full(act, ("Y", d))
                b = place[("Y", d)][0]
                nc.scalar.activation(yT[:, d, :], ps[b][:, :], ACT.Copy).then_inc(psum_free[b], 1)

        @block.vector
        def _(dve):
            links = [0]

            def link(ins):
                links[0] += 1
                ins.then_inc(dve_link, 1)
                dve.wait_ge(dve_link, links[0])

            def split_lo(b, slot):
                dve.wait_ge(hi_ready, b + 1)
                nc.vector.tensor_tensor(wl[slot][:, :], raw[slot][:, :], wh[slot][:, :].bitcast(f32),
                                        ALU.subtract).then_inc(lo_ready, 1)

            def split(b):
                split_lo(b, b % 2)

            def take_lo(key, dst, hi, src, scale):
                dve.wait_ge(hi_taken, hi_at[key])
                b = place[key][0]
                nc.vector.scalar_tensor_tensor(dst, src, scale, hi.bitcast(f32), ALU.mult, ALU.subtract).then_inc(psum_free[b], 1)

            def norm_tokens(p, src, dst):
                dve.wait_ge(rstd_ready, rs_at[("N", p)])
                for t in range(TT):
                    nc.vector.tensor_scalar(dst[:, t, :], src[:, t, :], rstd[:, t:t + 1], None, ALU.mult).then_inc(xn_ready, 1)
                for k in range(KD):
                    g = (C_ATTN if p == 0 else C_FFN) + k
                    take_lo(("N", p, k), aT_l[:, k, :], aT_h[:, k, :], bank(("N", p, k))[:, :], par[:, g:g + 1])

            def head_sums(src, n, heads):
                nc.vector.tensor_reduce(hss[:, 2 * n:2 * n + 2, 0:heads], src, AX.X, ALU.add).then_inc(hss_ready, 1)

            sqn = [0]

            def post(m, name):
                if name in T_CHUNKS:
                    kv = name in ("slc", "win")
                    w = P if kv else 256
                    nh = w // HD
                    q = NORMS.index(name)
                    for half in range(2):
                        sqn[0] += 1
                        dve.wait_ge(sq_ready, sqn[0])
                        head_sums(sq[:, half, 0:2 * w].rearrange("p (t h c) -> p t h c", t=2, c=HD), half, nh)
                    if q >= 2:
                        full(dve, ("T", *NORM_JOBS[q - 2], 1))
                    dve.wait_ge(rstd_ready, rs_at[name])
                    for half in range(2):
                        b = place[("P", m, name, half)][0]
                        src = ps[b][:, :].rearrange("p (t h c) -> p t h c", t=2, c=HD)[:, :, 0:nh, :]
                        r = rstd[:, 8 * half:8 * half + 8].rearrange("p (t h) -> p t h", t=2)[:, :, 0:nh].unsqueeze(3).to_broadcast([P, 2, nh, HD])
                        if kv:
                            dst = nrm[q % 2][:, 2 * half:2 * half + 2, :].rearrange("p t (g r c) -> p t g r c", g=2, r=2)
                            nc.vector.tensor_tensor(dst[:, :, :, 0, :], src, r, ALU.mult)
                            ins = nc.vector.tensor_tensor(dst[:, :, :, 1, :], src, r, ALU.mult)
                        else:
                            dst = nrm[q % 2][:, 2 * half:2 * half + 2, :].rearrange("p t (h c) -> p t h c", c=HD)
                            ins = nc.vector.tensor_tensor(dst, src, r, ALU.mult)
                        ins.then_inc(psum_free[b], 1)
                elif name == "cmp":
                    for kv in range(2):
                        key = ("P", m, name, kv)
                        full(dve, key)
                        b = place[key][0]
                        if kv == 1:
                            dve.wait_ge(cpe_ready, 1)
                        for g in range(2):
                            nc.vector.tensor_copy(cx[0:64, g, :], ps[b][64 * g:64 * g + 64, :])
                            ins = nc.vector.tensor_copy(cx[64:128, g, 0:S - 1], ps[b][64 * g:64 * g + 64, 1:S])
                        ins.then_inc(psum_free[b], 1)
                        free(dve, key)
                        nc.vector.memset(cpe[:, kv, :, :, NCMP:NCMP + 1], 0.0)
                        for g in range(2):
                            pairs = cx[:, g, :].rearrange("p (n r two) -> p two r n", r=8, two=2)[:, 0]
                            for r in range(2):
                                c0 = C_PE + 16 * kv + 8 * r
                                pe_ = par[:, c0:c0 + 8].unsqueeze(2).to_broadcast([P, 8, NCMP])
                                ins = nc.vector.tensor_tensor(cpe[:, kv, 8 * r:8 * r + 8, g, 0:NCMP], pairs[:, :, r:r + NCMP],
                                                              pe_, ALU.add)
                        ins.then_inc(cpe_ready, 1)
                elif name == "small":
                    full(dve, ("P", m, name, 0))
                    b = place[("P", m, name, 0)][0]
                    nc.vector.tensor_copy(smallt[:, :, :], ps[b][:, 0:P].rearrange("p (t c) -> p t c", t=TT)).then_inc(psum_free[b], 1)
                    free(dve, ("P", m, name, 0))

            def post_t(m, name):
                for c in T_CHUNKS.get(name, []):
                    g = GAIN[name]
                    k = QK_CHUNK[name] + c
                    take_lo(("T", m, name, c), qk_l[:, k, :], qk_h[:, k, :], bank(("T", m, name, c))[:, :], par[:, g:g + 1])

            nc.vector.memset(epsc[:, :], EPS).then_inc(small_v, 1)
            dve.wait_ge(par_in, 16)
            link(nc.vector.tensor_scalar(par[:, C_QG:C_QG + 3], par[:, C_QG:C_QG + 3], HD ** -0.5, None, ALU.mult))
            link(nc.vector.tensor_scalar(par[:, C_SUBLN:C_SUBLN + 1], par[:, C_SUBLN:C_SUBLN + 1], 1.0 - LAM_INIT, None, ALU.mult))
            split(0)
            split(1)
            dve.wait_ge(const_in, 32)
            nc.vector.tensor_copy(ident[:, :], stage[:, K_ID:K_ID + P]).then_inc(consts_ready, 1)
            norm_tokens(0, x0, xn0)
            nc.vector.tensor_copy(valid[:, :], stage[:, K_VALID:K_VALID + 1])
            nc.vector.tensor_copy(identr[:, :], stage[:, K_ID:K_ID + P])
            nc.vector.tensor_copy(distD[:, :], stage[:, K_D:K_D + S])
            nc.vector.tensor_copy(distW[:, :], stage[:, K_W:K_W + S])
            nc.vector.tensor_copy(causal[:, :], stage[:, K_M:K_M + P])
            nc.vector.tensor_copy(distC[:, :, :].rearrange("p t n -> p (t n)"), stage[:, K_DC:K_DC + P])
            nc.vector.tensor_copy(sel[:, :, :].rearrange("p h n -> p (h n)"), stage[:, K_SEL:K_SEL + 1024])
            nc.vector.memset(fT[:, :].bitcast(f32), 0.0)
            for h in range(8):
                ins = nc.vector.tensor_scalar(slopeI[:, h, :], stage[:, K_ID:K_ID + P], SLOPES8[h], None, ALU.mult)
            link(ins)

            for m in (NSA, DIFF, FOX):
                units = units_of(m)
                prev = None
                for name in PROJ[m]:
                    b = BI[(m, name)]
                    if prev is not None:
                        split(b + 1)
                        post(m, prev)
                        post_t(m, prev)
                    prev = name
                split(BI[(m, prev)] + 2)
                post(m, prev)
                post_t(m, prev)
                if m == NSA:
                    fb = par[:, C_FOXB:C_FOXB + 8].unsqueeze(1).to_broadcast([P, TT, 8])
                    link(nc.vector.tensor_tensor(logf[:, :, :], smallt[:, :, 24:32], fb, ALU.add))
                    nc.vector.tensor_copy(gsm[:, :, :], smallt[:, :, 0:24]).then_inc(small_v, 1)
                    lv = par[:, C_LAM:C_LAM + 4 * HD].rearrange("p (a b c) -> p a b c", a=2, b=2)
                    lsc = sq[:, 0, 0:P].rearrange("p (a c) -> p a c", a=2)
                    nc.vector.tensor_tensor(lsc, lv[:, :, 0, :], lv[:, :, 1, :], ALU.mult).then_inc(small_v, 1)
                    dve.wait_ge(small_v, 3)
                    nc.vector.tensor_reduce(lamt[:, :], lsc, AX.X, ALU.add).then_inc(small_v, 1)
                    dve.wait_ge(small_a, 1)
                    link(nc.vector.tensor_scalar(gsm[:, :, :], gsm[:, :, :], 1.0, None, ALU.add))
                    link(nc.vector.reciprocal(gsm[:, :, :], gsm[:, :, :]))
                    dve.wait_ge(small_a, 2)
                    link(nc.vector.tensor_scalar(lf1[:, :, :], logf[:, :, :], 0.0, None, ALU.min))
                    nc.vector.tensor_tensor(logf[:, :, :], lf1[:, :, :], lf2[:, :, :], ALU.subtract).then_inc(small_v, 1)
                    dve.wait_ge(small_a, 3)
                    link(nc.vector.scalar_tensor_tensor(neglam[:, :], lame[:, 1:2], -LAM_INIT, lame[:, 0:1], ALU.add, ALU.subtract))
                    dve.wait_ge(ksq_ready, 1)
                    nc.vector.tensor_reduce(kss[:, :], ksq[:, :], AX.X, ALU.add).then_inc(kss_ready, 1)
                    dve.wait_ge(rstd_ready, rs_at[("KC",)])
                    b = place[("KC",)][0]
                    nc.vector.tensor_scalar(ktok[:, 0, :], ps[b][0:HD, 0:HD], rstd[0:HD, 0:1], None, ALU.mult)
                    nc.vector.tensor_scalar(ktok[:, 1, :], ps[b][0:HD, 0:HD], rstd[0:HD, 0:1], None, ALU.mult).then_inc(psum_free[b], 1)
                    link(nc.vector.memset(vblk[:, :, :], 0.0))
                    full(dve, ("VC",))
                    b = place[("VC",)][0]
                    for a in range(4):
                        ins = nc.vector.tensor_copy(vblk[32 * a:32 * a + 32, a, :], ps[b][32 * a:32 * a + 32, 0:HD])
                    ins.then_inc(psum_free[b], 1)
                    take_lo(("KCT",), kc_l[:, :, :], kc_h[:, :, :], bank(("KCT",))[:, 0:64].rearrange("p (g n) -> p g n", g=2),
                            par[:, C_KG:C_KG + 1])
                    for i in range(TT):
                        for e in range(2):
                            full(dve, ("SC", i, e))
                            b = place[("SC", i, e)][0]
                            src = ps[b][:, 0:P].rearrange("p (a n) -> p a n", a=4)
                            link(nc.vector.tensor_reduce(cmx[:, 4 * e:4 * e + 4], src, AX.X, ALU.max))
                            if e == 0 and i >= 2:
                                full(dve, ("TC", i - 2))
                            nc.vector.tensor_tensor(pc[:, i % 2, e], src, cmx[:, 4 * e:4 * e + 4].unsqueeze(2).to_broadcast([P, 4, 32]),
                                                    ALU.subtract).then_inc(psum_free[b], 1)
                        dve.wait_ge(cexp_ready, i + 1)
                        link(nc.vector.tensor_reduce(csum[:, :], pc[:, i % 2].rearrange("p e a n -> p (e a) n"), AX.X, ALU.add))
                        link(nc.vector.reciprocal(crl[:, :], csum[:, :]))
                        if i == 0:
                            link(nc.vector.tensor_scalar(crl[:, :], crl[:, :], valid[:, 0:1], None, ALU.mult))
                        link(nc.vector.tensor_tensor(ccoef[:, :].rearrange("p (e a) -> p e a", e=2), crl[:, :].rearrange("p (e a) -> p e a", e=2),
                                                     gsm[:, i, 0:8].rearrange("p (a e) -> p e a", e=2), ALU.mult))
                        for e in range(2):
                            full(dve, ("OC", i, e))
                            b = place[("OC", i, e)][0]
                            dst = otok[:, i, :].rearrange("p (a e c) -> p e a c", e=2, c=HD)[:, e]
                            cf = ccoef[:, 4 * e:4 * e + 4].unsqueeze(2).to_broadcast([P, 4, HD])
                            nc.vector.tensor_tensor(dst, ps[b][:, 0:256].rearrange("p (a c) -> p a c", a=4), cf, ALU.mult).then_inc(psum_free[b], 1)
                if m == FOX:
                    dve.wait_ge(hi_taken, hi_at[("F",)])
                    b = place[("F",)][0]
                    nc.vector.scalar_tensor_tensor(fT[32:40, :], ps[b][0:8, :], -1.0, fT[0:8, :].bitcast(f32), ALU.mult,
                                                   ALU.subtract).then_inc(psum_free[b], 1)
                U = len(units)
                for j in range(U + O_LAG):
                    if j < U:
                        s0, n = span(units[j])
                        full(dve, ("S", m, j))
                        nc.vector.tensor_reduce(nmx[:, j:j + 1], bank(("S", m, j))[:, 0:n], AX.X, ALU.max, negate=True).then_inc(max_ready, 1)
                    q = j - 1
                    if 0 <= q < U:
                        free(dve, ("S", m, q))
                        kind, h, c, i = units[q]
                        if m == DIFF:
                            if c == 1:
                                free(dve, ("S", m, q - 1))
                                link(nc.vector.reciprocal(rl[:, q - 1:q + 1], lsum[:, q - 1:q + 1]))
                                link(nc.vector.tensor_scalar(coef[:, q:q + 1], rl[:, q:q + 1], neglam[:, 0:1], None, ALU.mult))
                                s0, n = span(units[q])
                                dst = prob[:, 4 + (q // 2) % 2, 0:n]
                                link(nc.vector.tensor_scalar(dst, prob[:, (q - 1) % 4, 0:n], rl[:, q - 1:q], None, ALU.mult))
                                nc.vector.scalar_tensor_tensor(dst, prob[:, q % 4, 0:n], coef[:, q:q + 1], dst, ALU.mult, ALU.add).then_inc(comb_ready, 1)
                        else:
                            link(nc.vector.reciprocal(rl[:, q:q + 1], lsum[:, q:q + 1]))
                            if m == NSA:
                                gi = 8 * (1 if kind == "slc" else 2) + h
                                link(nc.vector.tensor_scalar(coef[:, q:q + 1], rl[:, q:q + 1], gsm[:, i, gi:gi + 1], None, ALU.mult))
                    q = j - T_LAG
                    if 0 <= q < U and has_pv(m, q) and pv_index(m, q) % 2 == 0:
                        s0, n = span(units[q])
                        b = place[("A", m, q)][0]
                        full(dve, ("A", m, q))
                        nc.vector.tensor_copy(probT[:, 0, 0:n], ps[b][:, 0:n]).then_inc(psum_free[b], 1)
                    q = j - O_LAG
                    if 0 <= q < U and has_pv(m, q):
                        kind, h, c, i = units[q]
                        b = place[("O", m, q)][0]
                        full(dve, ("O", m, q))
                        if m == NSA:
                            if kind == "slc":
                                free(dve, ("OC", i, h % 2))
                            else:
                                free(dve, ("O", m, q - 1))
                            dst = otok[:, i, h * HD:(h + 1) * HD]
                            nc.vector.scalar_tensor_tensor(dst, ps[b][:, 0:HD], coef[:, q:q + 1], dst, ALU.mult, ALU.add).then_inc(psum_free[b], 1)
                        elif m == DIFF:
                            nc.vector.tensor_copy(otok[:, i, h * P:(h + 1) * P], ps[b][:, 0:P]).then_inc(psum_free[b], 1)
                        else:
                            nc.vector.tensor_scalar(otok[:, i, h * HD:(h + 1) * HD], ps[b][:, 0:HD], rl[:, q:q + 1], None,
                                                    ALU.mult).then_inc(psum_free[b], 1)
                    if j < U:
                        f0, f1 = fill_range(m, j)
                        for f in range(f0, f1):
                            if (f + 1) % (2 * KD * 3) == 0:
                                split(BI[(m, "gate0")] + f // (2 * KD * 3) + 2)
                if m == DIFF:
                    for half in range(2):
                        sqn[0] += 1
                        dve.wait_ge(sq_ready, sqn[0])
                        head_sums(sq[:, :, :].rearrange("p t (h c) -> p t h c", c=P), half, 4)
                    dve.wait_ge(rstd_ready, rs_at[("SUB",)])
                    v = otok[:, :, :].rearrange("p t (h c) -> p (t h) c", c=P)
                    nc.vector.tensor_tensor(v, v, rstd[:, :].unsqueeze(2).to_broadcast([P, 16, P]), ALU.mult).then_inc(sub_ready, 1)
                for k in range(4):
                    take_lo(("OT", m, k), oT_l[:, k, :], oT_h[:, k, :], bank(("OT", m, k))[:, :],
                            par[:, C_SUBLN:C_SUBLN + 1] if m == DIFF else 1.0)
                for c in range(KD):
                    if c % 4 == 3:
                        split(BI[(m, f"br{c // 4}")] + 2)
                    free(dve, ("G", m, c))
                    full(dve, ("B", m, c))
                    pb = place[("B", m, c)][0]
                    dst = merged[:, c, :] if m == NSA else bt[:, c % 2, :]
                    nc.vector.scalar_tensor_tensor(dst, gate[:, c, :], 1.0, ps[pb][:, :], ALU.add, ALU.mult).then_inc(psum_free[pb], 1)
                    if m > NSA:
                        free(dve, ("B", m, c))
                        free(dve, ("B", NSA, c))
                        if m == FOX:
                            dve.wait_ge(merged_ready, c + 1)
                        nc.vector.tensor_tensor(merged[:, c, :], merged[:, c, :], bt[:, c % 2, :], ALU.add).then_inc(merged_ready, 1)
                    if m == FOX:
                        dve.wait_ge(merged_hi, c + 1)
                        nc.vector.scalar_tensor_tensor(mT_l[:, c, :], merged[:, c, :], 0.5, mT_h[:, c, :].bitcast(f32), ALU.mult,
                                                       ALU.subtract).then_inc(merged_lo, 1)
            dve.wait_ge(h_in, 16)
            for n in range(4):
                for half in range(2):
                    full(dve, ("WO", n, half))
                    b = place[("WO", n, half)][0]
                    dst = hid[:, 2 * half:2 * half + 2, n * 256:(n + 1) * 256]
                    nc.vector.tensor_tensor(dst, ps[b][:, :].rearrange("p (t c) -> p t c", t=2), dst, ALU.add).then_inc(psum_free[b], 1)
                split(BI[("wo", n)] + 2)
            norm_tokens(1, hid, xn1)

            with dve.Fori(0, N_UP) as i:
                for c in range(2):
                    dve.wait_ge(psum_full[c], i + (up0[c] + 1))
                    u = ps[c]

                    def tap(j):
                        return par[:, bass.ds(6 * i + (C_CONVW + 3 * c + j), 1)]

                    nc.vector.tensor_scalar(uc[:, c, :], u[:, :], tap(2), par[:, bass.ds(2 * i + (C_CONVB + c), 1)],
                                            ALU.mult, ALU.add).then_inc(conv_step, 1)
                    dve.wait_ge(conv_step, 4 * i + (2 * c + 1))
                    nc.vector.scalar_tensor_tensor(uc[:, c, 1:S], u[:, 0:S - 1], tap(1), uc[:, c, 1:S], ALU.mult,
                                                   ALU.add).then_inc(conv_step, 1)
                    dve.wait_ge(conv_step, 4 * i + (2 * c + 2))
                    nc.vector.scalar_tensor_tensor(uc[:, c, 2:S], u[:, 0:S - 2], tap(0), uc[:, c, 2:S], ALU.mult,
                                                   ALU.add).then_inc(psum_free[c], 1)
                split_lo(B_UP + 2 * i + 2, 0)
                for c in range(2):
                    dve.wait_ge(psum_full[2 + c], i + (up0[2 + c] + 1))
                    dve.wait_ge(gelu_ready, 2 * i + (c + 1))
                    nc.vector.tensor_tensor(av[:, c, :], gl[:, c, :], ps[2 + c][:, :], ALU.mult).then_inc(psum_free[2 + c], 1)
                for c in range(2):
                    dve.wait_ge(act_hi, 2 * i + (c + 1))
                    k = bass.ds(2 * i + c, 1)
                    nc.vector.tensor_tensor(actT_l[:, k, :].rearrange("p o n -> p (o n)"), av[:, c, :],
                                            actT_h[:, k, :].rearrange("p o n -> p (o n)").bitcast(f32), ALU.subtract).then_inc(act_lo, 1)
                split_lo(B_UP + 2 * i + 3, 1)
            for n in range(2, N_DOWN):
                split(B_DOWN + n)

            def finish(d):
                full(dve, ("YT", d))
                cols = slice(d * P, (d + 1) * P)
                nc.vector.tensor_tensor(outt[:, :, cols], bank(("YT", d))[:, :].rearrange("p (t c) -> p t c", t=TT), hid[:, :, cols],
                                        ALU.add).then_inc(out_ready, 1)

            for d in range(KD):
                if d % 2 == 1:
                    full(dve, ("Y", d))
                    b = place[("Y", d)][0]
                    nc.vector.tensor_copy(yT[:, d, :], ps[b][:, :]).then_inc(psum_free[b], 1)
                if d >= 1:
                    finish(d - 1)
            finish(KD - 1)

        @block.tensor
        def _(pe):
            def begin(key):
                b, r = place[key]
                if r:
                    pe.wait_ge(psum_free[b], r)
                return ps[b]

            def done(key, ins):
                ins.then_inc(psum_full[place[key][0]], 1)

            def passes(dst, a_h, a_l, b_h, b_l, start, stop):
                nc.tensor.matmul(dst, a_h, b_h, start=start, stop=False)
                nc.tensor.matmul(dst, a_h, b_l, start=False, stop=False)
                return nc.tensor.matmul(dst, a_l, b_h, start=False, stop=stop)

            def weights(b, k, cols):
                pe.wait_ge(lo_ready, b + 1)
                return [w[b % 2][:, 0:k * cols].rearrange("p (k c) -> p k c", k=k) for w in (wh, wl)]

            def project(b, keys, cols, tiles):
                h, l = weights(b, KD, cols)
                for n, key in enumerate(keys):
                    bk = begin(key)
                    for t in range(tiles):
                        tt = n * tiles + t
                        rows = slice(tt * P, (tt + 1) * P)
                        for k in range(KD):
                            ins = passes(bk[:, t * cols:(t + 1) * cols], aT_h[:, k, rows], aT_l[:, k, rows], h[:, k], l[:, k],
                                         k == 0, k == KD - 1)
                    done(key, ins)

            def transposes(key, blocks):
                bk = begin(key)
                for n, src in enumerate(blocks):
                    ins = nc.tensor.transpose(bk[:, n * P:(n + 1) * P], src, ident[:, :])
                done(key, ins)

            def norm_transposes(p, xn):
                pe.wait_ge(xn_ready, TT * (p + 1))
                for k in range(KD):
                    transposes(("N", p, k), [xn[:, t, k * P:(k + 1) * P] for t in range(TT)])

            def post_t(m, name):
                if name not in T_CHUNKS:
                    return
                for half in range(2):
                    free(pe, ("P", m, name, half))
                q = NORMS.index(name)
                for c in T_CHUNKS[name]:
                    transposes(("T", m, name, c), [nrm[q % 2][:, t, c * P:(c + 1) * P] for t in range(TT)])

            pe.wait_ge(consts_ready, 1)
            norm_transposes(0, xn0)
            for k in range(KD):
                free(pe, ("N", 0, k))

            for m in (NSA, DIFF, FOX):
                units = units_of(m)
                prev = None
                for name in PROJ[m]:
                    b = BI[(m, name)]
                    if name == "cmp":
                        h, l = weights(b, KD, 256)
                        for n in range(2):
                            key = ("P", m, name, n)
                            bk = begin(key)
                            for k in range(KD):
                                cols = slice(n * P, (n + 1) * P)
                                ins = passes(bk[:, :], h[:, k, cols], l[:, k, cols], aT_h[:, k], aT_l[:, k], k == 0, k == KD - 1)
                            done(key, ins)
                    elif name == "small":
                        project(b, [("P", m, name, 0)], 32, TT)
                    else:
                        project(b, [("P", m, name, n) for n in range(2)], 256, 2)
                    if prev is not None:
                        post_t(m, prev)
                    prev = name
                post_t(m, prev)

                for name in PROJ[m]:
                    for c in T_CHUNKS.get(name, []):
                        free(pe, ("T", m, name, c))
                    if name[1] == "v":
                        free(pe, ("P", m, name, 0))
                        free(pe, ("P", m, name, 1))

                if m == NSA:
                    pe.wait_ge(cw_in, 32)
                    for kv in range(2):
                        pe.wait_ge(cpe_ready, kv + 1)
                        bk = begin(("H", kv))
                        for r in range(16):
                            ins = nc.tensor.matmul(bk[:, 0:64], w1_sb[:, kv, r, :], cpe[:, kv, r], start=r == 0, stop=r == 15)
                        done(("H", kv), ins)
                    free(pe, ("H", 0))
                    bk = begin(("KC",))
                    done(("KC",), nc.tensor.matmul(bk[0:HD, 0:HD], chid[:, 0, 0:64], w2_sb[:, 0, :], start=True, stop=True))
                    free(pe, ("H", 1))
                    bk = begin(("VC",))
                    done(("VC",), nc.tensor.matmul(bk[:, 0:HD], chid[:, 1, :], w2_sb[:, 1, :], start=True, stop=True))
                    free(pe, ("KC",))
                    bk = begin(("KCT",))
                    done(("KCT",), nc.tensor.transpose(bk[:, 0:64], ktok[:, :, :].rearrange("n r c -> n (r c)"), ident[0:HD, 0:HD]))
                    free(pe, ("VC",))
                    free(pe, ("KCT",))
                    for i in range(TT):
                        rows = slice(i * P, (i + 1) * P)
                        for e in range(2):
                            bk = begin(("SC", i, e))
                            hd_ = slice(64 * e, 64 * e + 64)
                            for a in range(4):
                                dst = bk[:, 32 * a:32 * a + 32]
                                nc.tensor.matmul(dst, slopeI[:, 2 * a + e, :], distC[:, i, :], start=True, stop=False)
                                ins = passes(dst, qk_h[hd_, a, rows], qk_l[hd_, a, rows], kc_h[hd_, a // 2], kc_l[hd_, a // 2], False, True)
                            done(("SC", i, e), ins)
                        pe.wait_ge(cexp_ready, i + 1)
                        transposes(("TC", i), [pc[:, i % 2, e].rearrange("p a n -> p (a n)") for e in range(2)])
                        free(pe, ("TC", i))
                        for e in range(2):
                            bk = begin(("OC", i, e))
                            done(("OC", i, e), nc.tensor.matmul(bk[:, 0:256], pcT[:, e, :], vblk[:, :, :].rearrange("p a c -> p (a c)"),
                                                                start=True, stop=True))
                if m == FOX:
                    bk = begin(("F",))
                    pe.wait_ge(small_v, 5)
                    for i in range(TT):
                        ins = nc.tensor.matmul(bk[0:8, :], logf[:, i, :], later[:, 384 - P * i:384 - P * i + S], start=i == 0, stop=i == TT - 1)
                    done(("F",), ins)
                    free(pe, ("F",))

                U = len(units)

                def scores(j):
                    u = units[j]
                    kind, h, c, i = u
                    s0, n = span(u)
                    rows, qc, kc = operands(m, u)
                    bk = begin(("S", m, j))
                    dst = bk[:, 0:n]
                    if kind == "fox":
                        nc.tensor.matmul(dst, sel[:, h, :], fT[:, 0:n], start=True, stop=False)
                        nc.tensor.matmul(bk[:, n - P:n], identr[:, :], causal[:, :], start=False, stop=False)
                    else:
                        dist = distW if kind == "win" else distD
                        sl = h if kind != "diff" else 2 * h + 1
                        c0 = 384 - P * i + s0
                        nc.tensor.matmul(dst, slopeI[:, sl, :], dist[:, c0:c0 + n], start=True, stop=False)
                    t = slice(i * P, (i + 1) * P)
                    done(("S", m, j), passes(dst, qk_h[rows, qc, t], qk_l[rows, qc, t], qk_h[rows, kc, s0:s0 + n], qk_l[rows, kc, s0:s0 + n],
                                             False, True))

                def values(q):
                    u = units[q]
                    s0, n = span(u)
                    v0, vw = v_cols(u)
                    free(pe, ("A", m, q))
                    bk = begin(("O", m, q))
                    for kb in range(n // P):
                        ins = nc.tensor.matmul(bk[:, 0:vw], probT[:, pv_index(m, q) % 2, kb * P:(kb + 1) * P],
                                               V[:, s0 // P + kb, v0:v0 + vw], start=kb == 0, stop=kb == n // P - 1)
                    done(("O", m, q), ins)

                def fill(f):
                    c, k, p = f // 24, f % 24 // 3, f % 3
                    b = BI[(m, f"gate{c // 2}")]
                    h, l = weights(b, KD, 256) if f % 24 == 0 else fill_w[0]
                    fill_w[0] = (h, l)
                    key = ("G", m, c)
                    bk = begin(key) if f % 24 == 0 else ps[place[key][0]]
                    cols = slice(c % 2 * P, c % 2 * P + P)
                    ins = nc.tensor.matmul(bk[:, :], (l if p == 2 else h)[:, k, cols], (aT_l if p == 1 else aT_h)[:, k],
                                           start=f % 24 == 0, stop=f % 24 == 23)
                    if f % 24 == 23:
                        done(key, ins)

                fill_w = [None]
                for j in range(U + O_LAG):
                    if j < U:
                        scores(j)
                        for f in range(*fill_range(m, j)):
                            fill(f)
                    q = j - T_LAG
                    if 0 <= q < U and has_pv(m, q):
                        if m == DIFF:
                            pe.wait_ge(comb_ready, q // 2 + 1)
                        else:
                            free(pe, ("S", m, q))
                        s0, n = span(units[q])
                        slot = 4 + (q // 2) % 2 if m == DIFF else q % 4
                        transposes(("A", m, q), [prob[:, slot, kb * P:(kb + 1) * P] for kb in range(n // P)])
                    q = j - O_LAG
                    if 0 <= q < U and has_pv(m, q):
                        values(q)

                if m == DIFF:
                    pe.wait_ge(sub_ready, 1)
                else:
                    free(pe, ("O", m, U - 1))
                for k in range(4):
                    transposes(("OT", m, k), [otok[:, t, k * P:(k + 1) * P] for t in range(TT)])
                for k in range(4):
                    free(pe, ("OT", m, k))
                for c in range(KD):
                    h, l = weights(BI[(m, f"br{c // 4}")], 4, S)
                    bk = begin(("B", m, c))
                    cols = slice(c % 4 * P, c % 4 * P + P)
                    for k in range(4):
                        ins = passes(bk[:, :], h[:, k, cols], l[:, k, cols], oT_h[:, k], oT_l[:, k], k == 0, k == 3)
                    done(("B", m, c), ins)

            pe.wait_ge(merged_lo, KD)
            for n in range(4):
                h, l = weights(BI[("wo", n)], KD, 256)
                for half in range(2):
                    key = ("WO", n, half)
                    bk = begin(key)
                    for t in range(2):
                        rows = slice((2 * half + t) * P, (2 * half + t + 1) * P)
                        for k in range(KD):
                            ins = passes(bk[:, t * 256:(t + 1) * 256], mT_h[:, k, rows], mT_l[:, k, rows], h[:, k], l[:, k], k == 0, k == KD - 1)
                    done(key, ins)
            norm_transposes(1, xn1)
            for k in range(KD):
                free(pe, ("N", 1, k))

            with pe.Fori(0, N_UP) as i:
                for b in range(2):
                    pe.wait_ge(lo_ready, 2 * i + (B_UP + b + 1))
                    h, l = [w[b][:, :].rearrange("p (k c) -> p k c", k=KD) for w in (wh, wl)]
                    for c in range(2):
                        bk = 2 * b + c
                        pe.wait_ge(psum_free[bk], i + up0[bk])
                        cols = slice(c * P, (c + 1) * P)
                        for k in range(KD):
                            ins = passes(ps[bk][:, :], h[:, k, cols], l[:, k, cols], aT_h[:, k], aT_l[:, k], k == 0, k == KD - 1)
                        ins.then_inc(psum_full[bk], 1)

            def down(n, slot, first, last):
                pe.wait_ge(lo_ready, n + (B_DOWN + 1))
                h, l = [w[slot][:, :].rearrange("p (k c) -> p k c", k=2) for w in (wh, wl)]
                acts = [[t[:, bass.ds(2 * n + k, 1), :].rearrange("p o n -> p (o n)") for t in (actT_h, actT_l)] for k in range(2)]
                for d in range(KD):
                    if first:
                        begin(("Y", d))
                    cols = slice(d * P, (d + 1) * P)
                    for k in range(2):
                        ins = passes(ps[d][:, :], h[:, k, cols], l[:, k, cols], acts[k][0], acts[k][1], first and k == 0, last and k == 1)
                    if last:
                        done(("Y", d), ins)
                if not last:
                    ins.then_inc(down_used, 1)

            pe.wait_ge(act_lo, NF)
            down(0, 0, True, False)
            with pe.Fori(1, N_DOWN - 2, 2) as n:
                down(n, 1, False, False)
                down(n + 1, 0, False, False)
            down(N_DOWN - 2, 1, False, False)
            down(N_DOWN - 1, 0, False, True)
            for d in range(KD):
                free(pe, ("Y", d))
                transposes(("YT", d), [yT[:, d, t * P:(t + 1) * P] for t in range(TT)])


def pack_params(np, a):
    def cols(v):
        return v.reshape(-1, P).T

    def twice(v):
        return np.concatenate([v, v])[:, None]

    conv = a["conv_w"][0].reshape(3, NF, P).transpose(2, 1, 0).reshape(P, 3 * NF)
    pe = [a["cmp_pe"][0, i].reshape(16, P).T for i in range(2)]
    rows = [np.broadcast_to(v.reshape(1, -1), (P, v.size)) for v in (a["diff_lam"][0], a["fox_b"][0])]
    gains = [a["nsa_q_g"][0], a["diff_q_g"][0], a["fox_q_g"][0], a["nsa_k_g"][0, 0], a["nsa_k_g"][0, 1], a["nsa_k_g"][0, 2],
             a["diff_k_g"][0], a["fox_k_g"][0]]
    parts = [cols(a["attn_norm_g"][0]), cols(a["ffn_norm_g"][0]), conv, cols(a["conv_b"][0]), cols(a["diff_subln_g"][0])]
    out = np.concatenate(parts + [twice(g) for g in gains] + pe + rows, axis=1)
    assert out.shape == (P, C_END)
    return np.ascontiguousarray(out)


def pack_constants(np):
    far = -1e30
    c = np.zeros((P, K_END), np.float32)
    p = np.arange(P)[:, None]
    col = np.arange(S)[None, :]
    c[:, K_ID:K_ID + P] = np.eye(P)
    dist = 384 + p - col
    c[:, K_D:K_D + S] = np.where(dist >= 0, -dist, far)
    c[:, K_W:K_W + S] = np.where((dist >= 0) & (dist < 256), -dist, far)
    c[:, K_M:K_M + P] = np.where(np.arange(P)[None, :] <= p, 0.0, far)
    for i in range(TT):
        dc = i * P + p - (16 * np.arange(32)[None, :] + 31)
        c[:, K_DC + 32 * i:K_DC + 32 * i + 32] = np.where(dc >= 0, -dc, far)
    for h in range(8):
        c[h, K_SEL + P * h:K_SEL + P * (h + 1)] = 1.0
        c[32 + h, K_SEL + P * h:K_SEL + P * (h + 1)] = 1.0
    c[:, K_U:K_U + 896] = np.arange(896)[None, :] - 384 >= p
    c[:, K_VALID] = np.arange(P) >= 31
    return c


def pack_weights(np, a):
    w_in, w_br, w_o, w_up, w_down = (a[n][0] for n in ("w_in", "w_br", "w_o", "w_up", "w_down"))
    col = {"nq": 0, "cmp": 512, "slc": 768, "win": 1024, "ngate": 1280, "dq": 1304, "dk": 1816, "dv": 2328,
           "fq": 2840, "fk": 3352, "fv": 3864, "ff": 4376, "mg": 4384}

    def rows_of(w, k):
        return w.reshape(k, P, -1).transpose(1, 0, 2).reshape(P, -1)

    out = np.zeros((N_BLOCKS, P, BLOCK), np.float32)
    for n, (m, name) in enumerate(BLOCKS):
        if m == "wo":
            out[n] = rows_of(w_o[:, 256 * name:256 * name + 256], KD)
        elif name == "small":
            w = np.concatenate([w_in[:, col["ngate"]:col["ngate"] + 24], w_in[:, col["ff"]:col["ff"] + 8]], axis=1)
            out[n][:, 0:KD * 32] = rows_of(w, KD)
        elif name.startswith("gate"):
            c = col["mg"] + D * m + 256 * int(name[4])
            out[n] = rows_of(w_in[:, c:c + 256], KD)
        elif name.startswith("br"):
            h = int(name[2])
            out[n] = rows_of(w_br[m][:, S * h:S * h + S], 4)
        else:
            c = col[name] if name in col else col[name[:2]] + 256 * int(name[2])
            out[n] = rows_of(w_in[:, c:c + 256], KD)
    for i in range(N_UP):
        out[B_UP + 2 * i] = rows_of(w_up[:, 256 * i:256 * i + 256], KD)
        out[B_UP + 2 * i + 1] = rows_of(w_up[:, D_FF + 256 * i:D_FF + 256 * i + 256], KD)
    for n in range(N_DOWN):
        out[B_DOWN + n] = rows_of(w_down[256 * n:256 * n + 256], 2)
    return out


def kernel(**inputs):
    import numpy as np
    import concourse.bacc as bacc
    from concourse.bass_utils import run_bass_kernel_spmd

    a = {k: np.asarray(v) for k, v in inputs.items()}
    arrays = {
        "x": a["x"],
        "wblk": pack_weights(np, a),
        "w1": np.ascontiguousarray(a["cmp_w1"][0].reshape(2, 16, P, P).transpose(2, 0, 1, 3)),
        "w2": np.ascontiguousarray(a["cmp_w2"][0].transpose(1, 0, 2)),
        "params": pack_params(np, a),
        "consts": pack_constants(np),
    }
    nc = bacc.Bacc("TRN2", target_bir_lowering=False, num_devices=1)
    args = [nc.dram_tensor(n, v.shape, mybir.dt.from_np(v.dtype), kind="ExternalInput").ap() for n, v in arrays.items()]
    args.append(nc.dram_tensor("out", (1, S, D), mybir.dt.float32, kind="ExternalOutput").ap())
    build(nc, *args)
    r = run_bass_kernel_spmd(nc, [arrays], core_ids=[0])
    return r.results[0]["out"]
```

```python
import concourse.bass as bass
from concourse import mybir
from contextlib import ExitStack

P = 128
S = 512
D = 1024
HD = 64
TT = S // P
KD = D // P
D_FF = 2816
NF = D_FF // P
NCMP = 31
EPS = 1e-6
LAM_INIT = 0.2
BLOCK = 2048

C_ATTN, C_FFN = 0, 8
C_CONVW = 16
C_CONVB = C_CONVW + 3 * NF
C_SUBLN = C_CONVB + NF
C_QG = C_SUBLN + 1
C_KG = C_QG + 3
C_PE = C_KG + 5
C_LAM = C_PE + 32
C_FOXB = C_LAM + 4 * HD
C_END = C_FOXB + 8
K_ID, K_D, K_W, K_M, K_DC, K_SEL, K_VALID, K_U = 0, 128, 640, 1152, 1280, 1408, 2432, 2433
K_END = 3329

NSA, DIFF, FOX = 0, 1, 2
PROJ = {NSA: ["cmp", "small", "nq0", "nq1", "slc", "win"],
        DIFF: ["dq0", "dq1", "dk0", "dk1", "dv0", "dv1"],
        FOX: ["fq0", "fq1", "fk0", "fk1", "fv0", "fv1"]}
BLOCKS = [(NSA, PROJ[NSA][0])]
for _m in (NSA, DIFF, FOX):
    BLOCKS += [(_m, n) for n in PROJ[_m][1:]] + [(_m, f"gate{n}") for n in range(4)]
    BLOCKS += [(_m + 1, PROJ[_m + 1][0])] if _m < FOX else []
    BLOCKS += [(_m, f"br{n}") for n in range(2)]
BLOCKS += [("wo", n) for n in range(4)]
BI = {n: i for i, n in enumerate(BLOCKS)}
B_UP = len(BLOCKS)
N_UP = D_FF // 256
B_DOWN = B_UP + 2 * N_UP
N_DOWN = NF // 2
N_BLOCKS = B_DOWN + N_DOWN
assert B_UP % 2 == 0

LN_EXP = "natural_log_exp_and_others"
SLOPES8 = [2.0 ** -(h + 1) for h in range(8)]


def units_of(m):
    if m == NSA:
        return [(k, h, 0, i) for i in range(TT) for h in range(8) for k in ("slc", "win")]
    if m == DIFF:
        return [("diff", h, c, i) for i in range(TT) for h in range(4) for c in range(2)]
    return [("fox", h, 0, i) for i in range(TT) for h in range(8)]


def span(u):
    kind, h, c, i = u
    s0 = max(0, i - 2) * P if kind == "win" else 0
    return s0, (i + 1) * P - s0


GATE_STEPS = KD * 3
FILL = KD * GATE_STEPS


def has_pv(m, q):
    return m != DIFF or q % 2 == 1


def pv_index(m, q):
    return q // 2 if m == DIFF else q


def attention_events(m):
    U = len(units_of(m))
    per = U // TT
    t_lag, o_lag = (3, 4) if m == DIFF else (2, 3)
    at = {}

    def put(j, *event):
        at.setdefault(j, []).append(event)

    fills = FILL if m < FOX else FILL - GATE_STEPS
    n = -(-fills // U)
    for j in range(U):
        put(j, "S", j)
        f0, f1 = min(fills, j * n), min(fills, (j + 1) * n)
        put(j, "G", f0, f1)
        for f in range(f0, f1):
            if (f + 1) % (2 * GATE_STEPS) == 0:
                b = BI[(m, "gate0")] + f // (2 * GATE_STEPS) + 2
                for piece in range(4):
                    put(j + 1 + piece, "W", b, piece)
    for q in range(U):
        if has_pv(m, q):
            put(q + 1, "C", q)
            put(q + t_lag, "A", q)
            put(q + o_lag, "O", q)
    if m == NSA:
        put(-1, "SC", 0)
        put(0, "TC", 0)
        put(1, "OC", 0)
        for i in range(1, TT):
            put(per * i - 12, "SC", i)
            put(per * i - 8, "TC", i)
            put(per * i - 6, "OC", i)
    for i in range(TT):
        last = per * (i + 1) - 1 + o_lag
        if m == DIFF:
            put(last, "SUB", i)
            put(last + 1, "SUN", i)
            if i < TT - 1:
                put(last + 3, "OT", i)
        elif i < TT - 1:
            put(last + 1, "OT", i)
    order = {k: n for n, k in enumerate(("SC", "S", "C", "TC", "OC", "G", "A", "O", "SUB", "SUN", "OT", "W"))}
    out = [e for j in sorted(at) for e in sorted(at[j], key=lambda e: order[e[0]])]
    if m == FOX:
        out += [("G", fills, fills + 16), ("OT", TT - 1), ("G", fills + 16, FILL), ("W", BI[(m, "gate3")] + 2, None)]
    else:
        nxt = BI[(m + 1, PROJ[m + 1][0])]
        out += [("P", 0), ("OT", TT - 1), ("P", 1), ("W", nxt + 2, None)]
    return out


def build(nc, x, wblk, w1, w2, params, consts, out):
    f32, f32r = mybir.dt.float32, mybir.dt.float32r
    ACT, ALU, AX = mybir.ActivationFunctionType, mybir.AluOpType, mybir.AxisListType
    KB = 1024

    place, results = {}, [0] * 8

    def plan(key, bank):
        place[key] = (bank, results[bank])
        results[bank] += 1

    turn = 0

    def plan_t(key):
        nonlocal turn
        plan(key, 4 + turn % 2)
        turn += 1

    T_CHUNKS = {n: [0, 1] for n in ("nq0", "nq1", "slc", "win", "dq0", "dq1", "dk0", "dk1", "fq0", "fq1", "fk0", "fk1")}
    EVENTS = {m: attention_events(m) for m in (NSA, DIFF, FOX)}

    def plan_p(m, name):
        for half in range(1 if name == "small" else 2):
            plan(("P", m, name, half), (BI[(m, name)] % 2) * 2 + half)

    for k in range(KD):
        plan(("N", 0, k), k)
    for m in (NSA, DIFF, FOX):
        for n, name in enumerate(PROJ[m]):
            if m == NSA or n > 0:
                plan_p(m, name)
            if n > 0:
                for c in T_CHUNKS.get(PROJ[m][n - 1], []):
                    plan_t(("T", m, PROJ[m][n - 1], c))
            if name == "nq0":
                plan(("H", 0), 6)
                plan(("H", 1), 7)
            if name == "nq1":
                plan(("KC",), 6)
                plan(("VC",), 7)
                plan(("F",), 6)
            if name == "slc":
                plan_t(("KCT",))
        for c in T_CHUNKS.get(PROJ[m][-1], []):
            plan_t(("T", m, PROJ[m][-1], c))
        for e in EVENTS[m]:
            if e[0] == "S":
                plan(("S", m, e[1]), 6 + e[1] % 2)
            elif e[0] == "G":
                for f in range(e[1], e[2]):
                    if f % GATE_STEPS == 0:
                        plan(("G", m, f // GATE_STEPS), f // GATE_STEPS % 2)
            elif e[0] == "A":
                plan_t(("A", m, e[1]))
            elif e[0] == "O":
                plan(("O", m, e[1]), 2 + pv_index(m, e[1]) % 2)
            elif e[0] == "SC":
                plan(("SC", e[1], 0), 6)
                plan(("SC", e[1], 1), 7)
            elif e[0] == "TC":
                plan_t(("TC", e[1]))
            elif e[0] == "OC":
                plan(("OC", e[1], 0), 2)
                plan(("OC", e[1], 1), 3)
            elif e[0] == "OT":
                plan_t(("OT", m, e[1]))
            elif e[0] == "P":
                name = PROJ[m + 1][0]
                plan(("P", m + 1, name, e[1]), (BI[(m + 1, name)] % 2) * 2 + e[1])
        for c in range(KD):
            plan(("B", m, c), (c + 2) % 4)
    for n in range(4):
        for half in range(2):
            plan(("WO", n, half), (n % 2) * 2 + half)
        for k in range(2 * n - 2, 2 * n):
            if k >= 0:
                plan(("N", 1, k), 4 + k % 2)
    plan(("N", 1, 6), 4)
    plan(("N", 1, 7), 5)
    plan(("R",), 6)
    up0 = list(results)
    for b in range(4):
        results[b] += N_UP
    for d in range(KD):
        plan(("Y", d), d)
    for d in range(KD):
        plan(("YT", d), d)

    with ExitStack() as ctx:
        base = -(-nc.sbuf_base // 64) * 64
        used = [0]

        def at(name, shape, dt, off):
            size = 4
            for s in shape[1:]:
                size *= s
            used[0] = max(used[0], off + size)
            return nc.alloc_sbuf_tensor_at(name, shape, dt, offset=base + off)

        aT_h = at("aT_h", [P, KD, S], f32r, 0)
        aT_l = at("aT_l", [P, KD, S], f32r, 16 * KB)
        raw = [at(f"raw{i}", [P, BLOCK], f32, (32 + 8 * i) * KB) for i in range(2)]
        wh = [at(f"wh{i}", [P, BLOCK], f32r, (48 + 8 * i) * KB) for i in range(2)]
        wl = [at(f"wl{i}", [P, BLOCK], f32r, (64 + 8 * i) * KB) for i in range(2)]
        RX = 80 * KB
        x0 = at("x0", [P, TT, D], f32, RX)
        nrm = [at(f"nrm{i}", [P, TT, 256], f32, RX + 4 * KB * i) for i in range(2)]
        prob = at("prob", [P, 6, S], f32, RX)
        probT = at("probT", [P, 2, S], f32, RX + 12 * KB)
        bt = at("bt", [P, 2, S], f32, RX + 12 * KB)
        hid = at("hid", [P, TT, D], f32, RX)
        RA = 96 * KB
        stage = at("stage", [P, K_U], f32, RA)
        xn0 = at("xn0", [P, TT, D], f32, RA + 16 * KB)
        qk_h = at("qk_h", [P, 8, S], f32r, RA)
        qk_l = at("qk_l", [P, 8, S], f32r, RA + 16 * KB)
        oT_h = at("oT_h", [P, 4, S], f32r, RA)
        oT_l = at("oT_l", [P, 4, S], f32r, RA + 8 * KB)
        mT_h = at("mT_h", [P, KD, S], f32r, RA + 16 * KB)
        mT_l = at("mT_l", [P, KD, S], f32r, RA + 32 * KB)
        V = at("V", [P, TT, S], f32, RA + 32 * KB)
        oT = at("oT", [P, 4, S], f32, RA + 40 * KB)
        gate = at("gate", [P, KD, S], f32, RA + 48 * KB)
        w1_sb = at("w1_sb", [P, 2, 16, P], f32, RA + 48 * KB)
        merged = at("merged", [P, KD, S], f32, RA + 64 * KB)
        RM = RA + 64 * KB
        cx = at("cx", [P, 2, S], f32, RM)
        cpe = at("cpe", [P, 2, 16, 2, 32], f32, RM + 4 * KB)
        pc = at("pc", [P, 2, 2, 4, 32], f32, RM)
        pcT = at("pcT", [P, 2, P], f32, RM + 2 * KB)
        w2_sb = at("w2_sb", [P, 2, HD], f32, RM + 12 * KB)
        chid = at("chid", [P, 2, P], f32, RM + 12 * KB + 512)
        ktok = at("ktok", [HD, 2, HD], f32, RM + 13 * KB + 512)
        ksq = at("ksq", [HD, HD], f32, RM + 14 * KB)
        kc_h = at("kc_h", [P, 2, 32], f32r, RM + 14 * KB + 256)
        kc_l = at("kc_l", [P, 2, 32], f32r, RM + 14 * KB + 512)
        vblk = at("vblk", [P, 4, HD], f32, RM + 15 * KB)
        sq = at("sq", [P, 2, S], f32, RA + 80 * KB)
        RC = RA + 84 * KB
        slopeI = at("slopeI", [P, 8, P], f32r, RC)
        distD = at("distD", [P, S], f32r, RC + 4 * KB)
        distW = at("distW", [P, S], f32r, RC + 6 * KB)
        causal = at("causal", [P, P], f32r, RC + 8 * KB)
        distC = at("distC", [P, TT, 32], f32r, RC + 8 * KB + 512)
        sel = at("sel", [P, 8, P], f32r, RC + 9 * KB)
        later = at("later", [P, 896], f32, RC + 13 * KB)
        otok = at("otok", [P, 2, S], f32, RC + 13 * KB)
        fT = at("fT", [P, S], f32r, RC + 17 * KB)
        rstdT = at("rstdT", [P, S], f32, RC + 16 * KB)
        ones = at("ones", [P, P], f32, RC + 18 * KB)
        diag = at("diag", [P, TT, P], f32, RA + 82 * KB)
        actT_h = at("actT_h", [P, NF, S], f32r, RA)
        actT_l = at("actT_l", [P, NF, S], f32r, RA + 44 * KB)
        uc = at("uc", [P, 2, S], f32, RA + 88 * KB)
        gl = at("gl", [P, 2, S], f32, RA + 92 * KB)
        av = at("av", [P, 2, S], f32, RA + 96 * KB)
        yT = at("yT", [P, KD, S], f32, 0)
        outt = at("outt", [P, TT, D], f32, 32 * KB)
        RK = RC + 19 * KB
        ident = at("ident", [P, P], f32, RK)
        identr = at("identr", [P, P], f32r, RK + 512)
        par = at("par", [P, C_END], f32, RK + KB)
        RS = RK + KB + -(-4 * C_END // 32) * 32
        so = [RS]

        def small(name, shape, dt=f32):
            t = at(name, shape, dt, so[0])
            n = 4
            for s in shape[1:]:
                n *= s
            so[0] += -(-n // 32) * 32
            return t

        ss = small("ss", [P, TT])
        sst = small("sst", [P, TT, 4])
        lnv = small("lnv", [P, 16])
        rstd = small("rstd", [P, 16])
        hss = small("hss", [P, TT, 4])
        epsc = small("epsc", [P, 1])
        un = at("un", [P, 2, S], f32, so[0])
        nmx = small("nmx", [P, 64])
        lsum = small("lsum", [P, 64])
        rl = small("rl", [P, 64])
        coef = small("coef", [P, 64])
        cmx = small("cmx", [P, 8])
        csum = small("csum", [P, 8])
        crl = small("crl", [P, 8])
        ccoef = small("ccoef", [P, 8])
        smallt = small("smallt", [P, TT, 32])
        gsm = small("gsm", [P, TT, 24])
        logf = small("logf", [P, TT, 8])
        lf1 = small("lf1", [P, TT, 8])
        lf2 = small("lf2", [P, TT, 8])
        lprod = small("lprod", [P, 2, HD])
        lamt = small("lamt", [P, 2])
        lame = small("lame", [P, 2])
        neglam = small("neglam", [P, 1])
        valid = small("valid", [P, 1])
        kss = small("kss", [HD, 1])
        assert base + used[0] <= nc.sbuf_usable_end, (base + used[0], nc.sbuf_usable_end)

        ps = [ctx.enter_context(nc.psum_tensor(f"ps{i}", [P, S], f32)) for i in range(8)]

        def sem(name):
            return ctx.enter_context(nc.semaphore(name))

        psum_full = [sem(f"psum_full{i}") for i in range(8)]
        psum_free = [sem(f"psum_free{i}") for i in range(8)]
        raw_in = [sem(f"raw_in{i}") for i in range(2)]
        hi_ready = sem("hi_ready")
        lo_ready = sem("lo_ready")
        down_used = sem("down_used")
        x_in = [sem(f"x_in{t}") for t in range(TT)]
        id_in, par_in, const_in, cw_in, h_in = (sem(n) for n in ("id_in", "par_in", "const_in", "cw_in", "h_in"))
        x_sums = sem("x_sums")
        xn_act = sem("xn_act")
        eps_set = sem("eps_set")
        pc_ready = sem("pc_ready")
        oT_hi, oT_lo = sem("oT_hi"), sem("oT_lo")
        sub_sums = sem("sub_sums")
        diag_ready = sem("diag_ready")
        glr_ready = sem("glr_ready")
        act_link, dve_link = sem("act_link"), sem("dve_link")
        xn_ready = sem("xn_ready")
        hi_taken = sem("hi_taken")
        sq_ready = sem("sq_ready")
        hss_ready = sem("hss_ready")
        rstd_ready = sem("rstd_ready")
        max_ready = sem("max_ready")
        comb_ready = sem("comb_ready")
        cexp_ready = sem("cexp_ready")
        small_v, small_a = sem("small_v"), sem("small_a")
        cpe_ready = sem("cpe_ready")
        ksq_ready, kss_ready = sem("ksq_ready"), sem("kss_ready")
        sub_sq = sem("sub_sq")
        sst_ready, sums_ready = sem("sst_ready"), sem("sums_ready")
        conv_done = sem("conv_done")
        sub_ready = sem("sub_ready")
        conv_step = sem("conv_step")
        gelu_ready, act_hi = sem("gelu_ready"), sem("act_hi")
        act_lo = sem("act_lo")
        merged_ready = sem("merged_ready")
        merged_hi, merged_lo = sem("merged_hi"), sem("merged_lo")
        out_ready, out_done = sem("out_ready"), sem("out_done")

        def free(eng, key):
            b, r = place[key]
            eng.wait_ge(psum_free[b], r + 1)

        def full(eng, key):
            b, r = place[key]
            eng.wait_ge(psum_full[b], r + 1)

        last_result = {}
        for m in (NSA, DIFF, FOX):
            for name in PROJ[m]:
                last_result[BI[(m, name)]] = ("P", m, name, 0 if name == "small" else 1)
            for n in range(4):
                last_result[BI[(m, f"gate{n}")]] = ("G", m, 2 * n + 1)
            for n in range(2):
                last_result[BI[(m, f"br{n}")]] = ("B", m, 4 * n + 3)
        for n in range(4):
            last_result[BI[("wo", n)]] = ("WO", n, 1)

        def bank(key):
            return ps[place[key][0]]

        hi_order = [("N", 0, k) for k in range(KD)]
        for m in (NSA, DIFF, FOX):
            for n, name in enumerate(PROJ[m]):
                if n > 0:
                    hi_order += [("T", m, PROJ[m][n - 1], c) for c in T_CHUNKS.get(PROJ[m][n - 1], [])]
                if name == "nq1":
                    hi_order += [("F",)]
                if name == "slc":
                    hi_order += [("KCT",)]
            hi_order += [("T", m, PROJ[m][-1], c) for c in T_CHUNKS.get(PROJ[m][-1], [])]
        hi_order += [("N", 1, k) for k in range(KD)]
        hi_at = {k: n + 1 for n, k in enumerate(hi_order)}

        QK_CHUNK = {"nq0": 0, "nq1": 2, "slc": 4, "win": 6, "dq0": 0, "dq1": 2, "dk0": 4, "dk1": 6,
                    "fq0": 0, "fq1": 2, "fk0": 4, "fk1": 6}
        GAIN = {"nq0": C_QG, "nq1": C_QG, "slc": C_KG + 1, "win": C_KG + 2, "dq0": C_QG + 1, "dq1": C_QG + 1,
                "dk0": C_KG + 3, "dk1": C_KG + 3, "fq0": C_QG + 2, "fq1": C_QG + 2, "fk0": C_KG + 4, "fk1": C_KG + 4}
        NORM_JOBS = [(m, n) for m in (NSA, DIFF, FOX) for n in PROJ[m] if n in T_CHUNKS]
        NORMS = [n for m, n in NORM_JOBS]
        rs_order = [("N", 0), "nq0", ("KC",), "nq1", "slc", "win", "dq0", "dq1", "dk0", "dk1"]
        rs_order += [("SUB", i) for i in range(TT)] + ["fq0", "fq1", "fk0", "fk1", ("N", 1)]
        rs_at = {k: n + 1 for n, k in enumerate(rs_order)}

        def operands(m, u):
            kind, h, c, i = u
            s0, n = span(u)
            if kind in ("slc", "win"):
                b, qc, kc = 64 * (h % 2), h // 2, (4 if kind == "slc" else 6) + h // 4
            elif kind == "diff":
                b, qc, kc = 64 * c, h, 4 + h
            else:
                b, qc, kc = 64 * (h % 2), h // 2, 4 + h // 2
            return slice(b, b + 64), qc, kc

        def unit_no(m, j):
            return sum(len(units_of(q)) for q in range(m)) + j

        def v_cols(u):
            kind, h, c, i = u
            if kind == "slc":
                return h // 4 * 64, 64
            if kind == "win":
                return 128 + h // 4 * 64, 64
            if kind == "diff":
                return h * P, P
            return h * 64, 64

        block = ctx.enter_context(nc.Block())

        @block.sync
        def _(sp):
            xv = x[0].rearrange("(t p) d -> t p d", p=P)
            for t in range(TT):
                sp.dma_start(x0[:, t, :], xv[t]).then_inc(x_in[t], 16)
            sp.dma_start(ident[:, :], consts[:, K_ID:K_ID + P]).then_inc(id_in, 16)

            def load(b, slot, first):
                if not first:
                    sp.wait_ge(lo_ready, b - 1)
                sp.dma_start(raw[slot][:, :], wblk[bass.ds(b, 1)].rearrange("o p n -> p (o n)")).then_inc(raw_in[slot], 16)

            load(0, 0, True)
            sp.dma_start(par[:, :], params).then_inc(par_in, 16)
            load(1, 1, True)
            sp.dma_start(stage[:, :], consts[:, 0:K_U]).then_inc(const_in, 16)
            sp.dma_start(later[:, :], consts[:, K_U:K_U + 896]).then_inc(const_in, 16)
            sp.dma_start(w1_sb[:, :, :, :], w1).then_inc(cw_in, 16)
            sp.dma_start(w2_sb[:, :, :], w2).then_inc(cw_in, 16)
            with sp.Fori(2, BI[("wo", 2)], 2) as i:
                load(i, 0, False)
                load(i + 1, 1, False)
            sp.wait_ge(merged_ready, 2 * KD)
            sp.dma_start(hid[:, :, :], x[0].rearrange("(t p) d -> p t d", p=P)).then_inc(h_in, 16)
            with sp.Fori(BI[("wo", 2)], N_BLOCKS - 1, 2) as i:
                load(i, 0, False)
                load(i + 1, 1, False)
            load(N_BLOCKS - 1, (N_BLOCKS - 1) % 2, False)
            outv = out[0].rearrange("(t p) d -> p t d", p=P)
            for n in range(4):
                sp.wait_ge(out_ready, 2 * n + 2)
                sp.dma_start(outv[:, :, n * 256:(n + 1) * 256], outt[:, :, n * 256:(n + 1) * 256]).then_inc(out_done, 16)
            sp.wait_ge(out_done, 64)

        @block.scalar
        def _(act):
            links = [0]

            def link(ins):
                links[0] += 1
                ins.then_inc(act_link, 1)
                act.wait_ge(act_link, links[0])

            def split_hi(slot, fills):
                act.wait_ge(raw_in[slot], fills * 16)
                nc.scalar.activation(wh[slot][:, :], raw[slot][:, :], ACT.Copy).then_inc(hi_ready, 4)

            def split(b, piece=None):
                if b >= 2 and piece in (None, 0):
                    full(act, last_result[b - 2])
                if piece is None:
                    return split_hi(b % 2, b // 2 + 1)
                if piece == 0:
                    act.wait_ge(raw_in[b % 2], (b // 2 + 1) * 16)
                cols = slice(piece * 512, piece * 512 + 512)
                nc.scalar.activation(wh[b % 2][:, cols], raw[b % 2][:, cols], ACT.Copy).then_inc(hi_ready, 1)

            def take_hi(key, dst, src, scale):
                full(act, key)
                nc.scalar.activation(dst, src, ACT.Copy, scale=scale).then_inc(hi_taken, 1)

            def inv_rms(dst, src, width):
                rows, n = src.shape[0], src.shape[1]
                link(nc.scalar.activation(lnv[0:rows, 0:n], src, ACT.Ln, scale=1.0 / width, bias=epsc[0:rows, :]))
                nc.scalar.activation(dst, lnv[0:rows, 0:n], ACT.Exp, scale=-0.5).then_inc(rstd_ready, 1)

            def post(m, name):
                if name in T_CHUNKS:
                    w = P if name in ("slc", "win") else 256
                    n = NORMS.index(name)
                    for half in range(2):
                        full(act, ("P", m, name, half))
                        src = bank(("P", m, name, half))[:, :].rearrange("p (t c) -> p t c", t=2)
                        if name in ("slc", "win"):
                            vc = 0 if name == "slc" else P
                            nc.scalar.activation(V[:, 2 * half:2 * half + 2, vc:vc + P], src[:, :, P:], ACT.Copy)
                        nc.scalar.activation(sq[:, half, 0:2 * w].rearrange("p (t c) -> p t c", t=2), src[:, :, 0:w],
                                             ACT.Square).then_inc(sq_ready, 1)
                    act.wait_ge(hss_ready, 2 * (n + 1))
                    inv_rms(rstd[:, :], hss[:, :, :].rearrange("p t h -> p (t h)"), HD)
                elif name in ("dv0", "dv1", "fv0", "fv1"):
                    vc = 256 * int(name[2])
                    for half in range(2):
                        full(act, ("P", m, name, half))
                        b = place[("P", m, name, half)][0]
                        nc.scalar.activation(V[:, 2 * half:2 * half + 2, vc:vc + 256],
                                             ps[b][:, :].rearrange("p (t c) -> p t c", t=2), ACT.Copy).then_inc(psum_free[b], 1)
                elif name == "small":
                    free(act, ("P", m, "small", 0))
                    nc.scalar.activation(gsm[:, :, :], smallt[:, :, 0:24], ACT.Exp, scale=-1.0).then_inc(small_a, 1)
                    act.wait_ge(small_v, 1)
                    link(nc.scalar.activation(lf1[:, :, :], logf[:, :, :], ACT.Abs))
                    link(nc.scalar.activation(lf1[:, :, :], lf1[:, :, :], ACT.Exp, scale=-1.0))
                    nc.scalar.activation(lf2[:, :, :], lf1[:, :, :], ACT.Ln, bias=1.0).then_inc(small_a, 1)
                    act.wait_ge(small_v, 3)
                    nc.scalar.activation(lame[:, :], lamt[:, :], ACT.Exp).then_inc(small_a, 1)

            def post_t(m, name):
                for c in T_CHUNKS.get(name, []):
                    g = GAIN[name]
                    take_hi(("T", m, name, c), qk_h[:, QK_CHUNK[name] + c, :], bank(("T", m, name, c))[:, :], par[:, g:g + 1])

            def compression(name):
                if name == "nq0":
                    full(act, ("H", 0))
                    b = place[("H", 0)][0]
                    nc.scalar.activation(chid[:, 0, 0:64], ps[b][:, 0:64], ACT.Gelu_apprx_tanh).then_inc(psum_free[b], 1)
                    full(act, ("H", 1))
                    b = place[("H", 1)][0]
                    hv = chid[:, 1, :].rearrange("p (g r n) -> p g r n", g=2, r=2)
                    for r in range(2):
                        ins = nc.scalar.activation(hv[:, :, r, :], ps[b][:, 0:64].rearrange("p (g n) -> p g n", g=2), ACT.Gelu_apprx_tanh)
                    ins.then_inc(psum_free[b], 1)
                    nc.scalar.preload_act_table_set(LN_EXP)
                elif name == "nq1":
                    full(act, ("KC",))
                    nc.scalar.activation(ksq[:, :], bank(("KC",))[0:HD, 0:HD], ACT.Square).then_inc(ksq_ready, 1)
                    act.wait_ge(kss_ready, 1)
                    inv_rms(rstd[0:HD, 0:1], kss[:, :], HD)
                    full(act, ("F",))
                    nc.scalar.activation(fT[0:8, :], bank(("F",))[0:8, :], ACT.Copy, scale=-1.0).then_inc(hi_taken, 1)
                elif name == "slc":
                    take_hi(("KCT",), kc_h[:, :, :], bank(("KCT",))[:, 0:64].rearrange("p (g n) -> p g n", g=2), par[:, C_KG:C_KG + 1])

            nc.scalar.preload_act_table_set(LN_EXP)
            act.wait_ge(eps_set, 1)
            for t in (0, 2):
                act.wait_ge(x_in[t], 16)
                link(nc.scalar.activation(sq[:, :, :].rearrange("p a n -> p (a n)"), x0[:, t, :], ACT.Square, accum_out=ss[:, t:t + 1]))
            act.wait_ge(x_sums, 2)
            inv_rms(rstd[:, 0:TT], ss[:, :], D)
            act.wait_ge(rstd_ready, 1)
            nc.scalar.activation(xn0[:, 3, :], x0[:, 3, :], ACT.Copy, scale=rstd[:, 3:4]).then_inc(xn_act, 1)
            split(0)
            act.wait_ge(par_in, 16)
            for k in range(KD):
                take_hi(("N", 0, k), aT_h[:, k, :], bank(("N", 0, k))[:, :], par[:, C_ATTN + k:C_ATTN + k + 1])
            split(1)

            for m in (NSA, DIFF, FOX):
                units = units_of(m)
                if m > NSA:
                    nc.scalar.preload_act_table_set(LN_EXP)
                for n in range(1, len(PROJ[m])):
                    prev, name = PROJ[m][n - 1], PROJ[m][n]
                    if m == NSA or n > 1:
                        split(BI[(m, name)] + 1)
                        post(m, prev)
                    post_t(m, prev)
                    if m == NSA:
                        compression(name)
                split(BI[(m, PROJ[m][-1])] + 2)
                post(m, PROJ[m][-1])
                post_t(m, PROJ[m][-1])

                for e in EVENTS[m]:
                    what, j = e[0], e[1]
                    if what == "S":
                        s0, n = span(units[j])
                        b = place[("S", m, j)][0]
                        act.wait_ge(max_ready, unit_no(m, j) + 1)
                        nc.scalar.activation(prob[:, j % 4, 0:n], ps[b][:, 0:n], ACT.Exp, bias=nmx[:, j:j + 1],
                                             accum_out=lsum[:, j:j + 1]).then_inc(psum_free[b], 1)
                    elif what == "A" and pv_index(m, j) % 2 == 1:
                        s0, n = span(units[j])
                        b = place[("A", m, j)][0]
                        full(act, ("A", m, j))
                        nc.scalar.activation(probT[:, 1, 0:n], ps[b][:, 0:n], ACT.Copy).then_inc(psum_free[b], 1)
                    elif what == "G":
                        for f in range(e[1], e[2]):
                            if (f + 1) % GATE_STEPS == 0:
                                c = f // GATE_STEPS
                                full(act, ("G", m, c))
                                if m > NSA:
                                    free(act, ("B", m - 1, c))
                                b = place[("G", m, c)][0]
                                nc.scalar.activation(gate[:, c, :], ps[b][:, :], ACT.Tanh, scale=0.5).then_inc(psum_free[b], 1)
                    elif what == "W":
                        split(j, e[2])
                    elif what == "SC":
                        for k in range(2):
                            free(act, ("SC", j, k))
                        nc.scalar.activation(pc[:, j % 2], pc[:, j % 2], ACT.Exp).then_inc(cexp_ready, 1)
                    elif what == "TC":
                        b = place[("TC", j)][0]
                        full(act, ("TC", j))
                        nc.scalar.activation(pcT[:, :, :], ps[b][:, 0:256].rearrange("p (e t) -> p e t", e=2),
                                             ACT.Copy).then_inc(psum_free[b], 1)
                    elif what == "SUB":
                        last = len(units) // TT * (j + 1) - 1
                        free(act, ("O", m, last - 2))
                        free(act, ("O", m, last))
                        nc.scalar.activation(sq[:, 0, :], otok[:, j % 2, :], ACT.Square).then_inc(sub_sq, 1)
                    elif what == "SUN":
                        act.wait_ge(sub_sums, j + 1)
                        inv_rms(rstd[:, 4 * j:4 * j + 4], hss[:, j, :], P)
                    elif what == "OT":
                        b = place[("OT", m, j)][0]
                        full(act, ("OT", m, j))
                        nc.scalar.activation(oT[:, :, j * P:(j + 1) * P], ps[b][:, :].rearrange("p (k t) -> p k t", k=4), ACT.Copy,
                                             scale=par[:, C_SUBLN:C_SUBLN + 1] if m == DIFF else 1.0).then_inc(psum_free[b], 1)
                        if j == TT - 1:
                            free(act, ("OT", m, j))
                            free(act, ("OT", m, j - 1))
                            for k in range(4):
                                nc.scalar.activation(oT_h[:, k, :], oT[:, k, :], ACT.Copy).then_inc(oT_hi, 1)
                if m < FOX:
                    post(m + 1, PROJ[m + 1][0])
                for c in range(KD):
                    if c % 4 == 3:
                        split(BI[(m, f"br{c // 4}")] + 2)
                    if m == FOX:
                        act.wait_ge(merged_ready, KD + c + 1)
                        nc.scalar.activation(mT_h[:, c, :], merged[:, c, :], ACT.Copy, scale=0.5).then_inc(merged_hi, 1)

            def squares(n):
                for t in range(TT):
                    nc.scalar.activation(sq[:, 0, 0:256], hid[:, t, n * 256:(n + 1) * 256], ACT.Square,
                                         accum_out=sst[:, t, n:n + 1]).then_inc(sst_ready, 1)
                    act.wait_ge(sst_ready, TT * n + t + 1)

            def ffn_hi(k):
                take_hi(("N", 1, k), aT_h[:, k, :], bank(("N", 1, k))[:, :], par[:, C_FFN + k:C_FFN + k + 1])

            nc.scalar.preload_act_table_set(LN_EXP)
            for n in range(4):
                for k in range(max(0, 2 * n - 2), 2 * n):
                    ffn_hi(k)
                if n < 3:
                    for half in range(2):
                        free(act, ("WO", n, half))
                    squares(n)
                    split(BI[("wo", n)] + 2)
            ffn_hi(6)
            ffn_hi(7)
            squares(3)
            act.wait_ge(sums_ready, 1)
            inv_rms(rstd[:, 0:TT], ss[:, :], D)
            split(BI[("wo", 3)] + 2)
            nc.scalar.preload_act_table(ACT.Gelu_apprx_tanh)

            with act.Fori(0, N_UP) as i:
                for c in range(2):
                    act.wait_ge(conv_done, 2 * i + (c + 1))
                    nc.scalar.activation(gl[:, c, :], uc[:, c, :], ACT.Gelu_apprx_tanh).then_inc(gelu_ready, 1)
                    if c == 0:
                        act.wait_ge(psum_full[1], i + (up0[1] + 1))
                        split_hi(0, i + (B_UP // 2 + 2))
                for c in range(2):
                    act.wait_ge(psum_free[2 + c], i + (up0[2 + c] + 1))
                    nc.scalar.activation(actT_h[:, bass.ds(2 * i + c, 1), :].rearrange("p o n -> p (o n)"),
                                         av[:, c, :], ACT.Copy).then_inc(act_hi, 1)
                act.wait_ge(psum_full[3], i + (up0[3] + 1))
                split_hi(1, i + (B_UP // 2 + 2))
            for n in range(2, N_DOWN):
                act.wait_ge(down_used, n - 1)
                split_hi(n % 2, (B_DOWN + n) // 2 + 1)
            for d in range(0, KD, 2):
                full(act, ("Y", d))
                b = place[("Y", d)][0]
                nc.scalar.activation(yT[:, d, :], ps[b][:, :], ACT.Copy).then_inc(psum_free[b], 1)

        @block.vector
        def _(dve):
            links = [0]

            def link(ins):
                links[0] += 1
                ins.then_inc(dve_link, 1)
                dve.wait_ge(dve_link, links[0])

            def split_lo(b, slot):
                dve.wait_ge(hi_ready, 4 * b + 4)
                nc.vector.tensor_tensor(wl[slot][:, :], raw[slot][:, :], wh[slot][:, :].bitcast(f32),
                                        ALU.subtract).then_inc(lo_ready, 1)

            def split(b, piece=None):
                if piece is None:
                    return split_lo(b, b % 2)
                dve.wait_ge(hi_ready, 4 * b + piece + 1)
                cols = slice(piece * 512, piece * 512 + 512)
                ins = nc.vector.tensor_tensor(wl[b % 2][:, cols], raw[b % 2][:, cols], wh[b % 2][:, cols].bitcast(f32), ALU.subtract)
                if piece == 3:
                    ins.then_inc(lo_ready, 1)

            def take_lo(key, dst, hi, src, scale):
                dve.wait_ge(hi_taken, hi_at[key])
                b = place[key][0]
                nc.vector.scalar_tensor_tensor(dst, src, scale, hi.bitcast(f32), ALU.mult, ALU.subtract).then_inc(psum_free[b], 1)

            def post(m, name):
                if name in T_CHUNKS:
                    kv = name in ("slc", "win")
                    w = P if kv else 256
                    nh = w // HD
                    q = NORMS.index(name)
                    for half in range(2):
                        dve.wait_ge(sq_ready, 2 * q + half + 1)
                        nc.vector.tensor_reduce(hss[:, 2 * half:2 * half + 2, 0:nh],
                                                sq[:, half, 0:2 * w].rearrange("p (t h c) -> p t h c", t=2, c=HD),
                                                AX.X, ALU.add).then_inc(hss_ready, 1)
                    if q >= 2:
                        full(dve, ("T", *NORM_JOBS[q - 2], 1))
                    dve.wait_ge(rstd_ready, rs_at[name])
                    for half in range(2):
                        b = place[("P", m, name, half)][0]
                        src = ps[b][:, :].rearrange("p (t h c) -> p t h c", t=2, c=HD)[:, :, 0:nh, :]
                        r = rstd[:, 8 * half:8 * half + 8].rearrange("p (t h) -> p t h", t=2)[:, :, 0:nh].unsqueeze(3).to_broadcast([P, 2, nh, HD])
                        if kv:
                            dst = nrm[q % 2][:, 2 * half:2 * half + 2, :].rearrange("p t (g r c) -> p t g r c", g=2, r=2)
                            nc.vector.tensor_tensor(dst[:, :, :, 0, :], src, r, ALU.mult)
                            ins = nc.vector.tensor_tensor(dst[:, :, :, 1, :], src, r, ALU.mult)
                        else:
                            dst = nrm[q % 2][:, 2 * half:2 * half + 2, :].rearrange("p t (h c) -> p t h c", c=HD)
                            ins = nc.vector.tensor_tensor(dst, src, r, ALU.mult)
                        ins.then_inc(psum_free[b], 1)
                elif name == "cmp":
                    for kv in range(2):
                        key = ("P", m, name, kv)
                        full(dve, key)
                        b = place[key][0]
                        if kv == 1:
                            dve.wait_ge(cpe_ready, 1)
                        for g in range(2):
                            nc.vector.tensor_copy(cx[0:64, g, :], ps[b][64 * g:64 * g + 64, :])
                            ins = nc.vector.tensor_copy(cx[64:128, g, 0:S - 1], ps[b][64 * g:64 * g + 64, 1:S])
                        ins.then_inc(psum_free[b], 1)
                        free(dve, key)
                        nc.vector.memset(cpe[:, kv, :, :, NCMP:NCMP + 1], 0.0)
                        for g in range(2):
                            pairs = cx[:, g, :].rearrange("p (n r two) -> p two r n", r=8, two=2)[:, 0]
                            for r in range(2):
                                c0 = C_PE + 16 * kv + 8 * r
                                pe_ = par[:, c0:c0 + 8].unsqueeze(2).to_broadcast([P, 8, NCMP])
                                ins = nc.vector.tensor_tensor(cpe[:, kv, 8 * r:8 * r + 8, g, 0:NCMP], pairs[:, :, r:r + NCMP],
                                                              pe_, ALU.add)
                        ins.then_inc(cpe_ready, 1)
                elif name == "small":
                    full(dve, ("P", m, name, 0))
                    b = place[("P", m, name, 0)][0]
                    nc.vector.tensor_copy(smallt[:, :, :], ps[b][:, 0:P].rearrange("p (t c) -> p t c", t=TT)).then_inc(psum_free[b], 1)
                    free(dve, ("P", m, name, 0))
                    fb = par[:, C_FOXB:C_FOXB + 8].unsqueeze(1).to_broadcast([P, TT, 8])
                    nc.vector.tensor_tensor(logf[:, :, :], smallt[:, :, 24:32], fb, ALU.add).then_inc(small_v, 1)
                    lv = par[:, C_LAM:C_LAM + 4 * HD].rearrange("p (a b c) -> p a b c", a=2, b=2)
                    nc.vector.tensor_tensor(lprod[:, :, :], lv[:, :, 0, :], lv[:, :, 1, :], ALU.mult).then_inc(small_v, 1)
                    dve.wait_ge(small_v, 2)
                    nc.vector.tensor_reduce(lamt[:, :], lprod[:, :, :], AX.X, ALU.add).then_inc(small_v, 1)
                    dve.wait_ge(small_a, 1)
                    link(nc.vector.tensor_scalar(gsm[:, :, :], gsm[:, :, :], 1.0, None, ALU.add))
                    link(nc.vector.reciprocal(gsm[:, :, :], gsm[:, :, :]))
                    dve.wait_ge(small_a, 2)
                    link(nc.vector.tensor_scalar(lf1[:, :, :], logf[:, :, :], 0.0, None, ALU.min))
                    nc.vector.tensor_tensor(logf[:, :, :], lf1[:, :, :], lf2[:, :, :], ALU.subtract).then_inc(small_v, 1)
                    dve.wait_ge(small_a, 3)
                    link(nc.vector.scalar_tensor_tensor(neglam[:, :], lame[:, 1:2], -LAM_INIT, lame[:, 0:1], ALU.add, ALU.subtract))

            def post_t(m, name):
                for c in T_CHUNKS.get(name, []):
                    g = GAIN[name]
                    k = QK_CHUNK[name] + c
                    take_lo(("T", m, name, c), qk_l[:, k, :], qk_h[:, k, :], bank(("T", m, name, c))[:, :], par[:, g:g + 1])

            def compression(name):
                if name == "nq1":
                    dve.wait_ge(ksq_ready, 1)
                    nc.vector.tensor_reduce(kss[:, :], ksq[:, :], AX.X, ALU.add).then_inc(kss_ready, 1)
                    link(nc.vector.memset(vblk[:, :, :], 0.0))
                    full(dve, ("VC",))
                    b = place[("VC",)][0]
                    for a in range(4):
                        ins = nc.vector.tensor_copy(vblk[32 * a:32 * a + 32, a, :], ps[b][32 * a:32 * a + 32, 0:HD])
                    ins.then_inc(psum_free[b], 1)
                    dve.wait_ge(rstd_ready, rs_at[("KC",)])
                    b = place[("KC",)][0]
                    nc.vector.tensor_scalar(ktok[:, 0, :], ps[b][0:HD, 0:HD], rstd[0:HD, 0:1], None, ALU.mult)
                    nc.vector.tensor_scalar(ktok[:, 1, :], ps[b][0:HD, 0:HD], rstd[0:HD, 0:1], None, ALU.mult).then_inc(psum_free[b], 1)
                    dve.wait_ge(hi_taken, hi_at[("F",)])
                    b = place[("F",)][0]
                    nc.vector.scalar_tensor_tensor(fT[32:40, :], ps[b][0:8, :], -1.0, fT[0:8, :].bitcast(f32), ALU.mult,
                                                   ALU.subtract).then_inc(psum_free[b], 1)
                elif name == "slc":
                    take_lo(("KCT",), kc_l[:, :, :], kc_h[:, :, :], bank(("KCT",))[:, 0:64].rearrange("p (g n) -> p g n", g=2),
                            par[:, C_KG:C_KG + 1])

            nc.vector.memset(epsc[:, :], EPS).then_inc(eps_set, 1)
            for t in (1, 3):
                dve.wait_ge(x_in[t], 16)
                nc.vector.scalar_tensor_tensor(xn0[:, t, :], x0[:, t, :], 1.0, x0[:, t, :], ALU.mult, ALU.mult,
                                               accum_out=ss[:, t:t + 1]).then_inc(x_sums, 1)
            dve.wait_ge(x_sums, 2)
            dve.wait_ge(rstd_ready, 1)
            for t in range(3):
                nc.vector.tensor_scalar(xn0[:, t, :], x0[:, t, :], rstd[:, t:t + 1], None, ALU.mult).then_inc(xn_ready, 1)
            dve.wait_ge(par_in, 16)
            link(nc.vector.tensor_scalar(par[:, C_QG:C_QG + 3], par[:, C_QG:C_QG + 3], HD ** -0.5, None, ALU.mult))
            link(nc.vector.tensor_scalar(par[:, C_SUBLN:C_SUBLN + 1], par[:, C_SUBLN:C_SUBLN + 1], 1.0 - LAM_INIT, None, ALU.mult))
            split(0)
            for k in range(KD):
                take_lo(("N", 0, k), aT_l[:, k, :], aT_h[:, k, :], bank(("N", 0, k))[:, :], par[:, C_ATTN + k:C_ATTN + k + 1])
            split(1)
            dve.wait_ge(const_in, 32)
            nc.vector.tensor_copy(valid[:, :], stage[:, K_VALID:K_VALID + 1])
            nc.vector.tensor_copy(identr[:, :], stage[:, K_ID:K_ID + P])
            nc.vector.tensor_copy(distD[:, :], stage[:, K_D:K_D + S])
            nc.vector.tensor_copy(distW[:, :], stage[:, K_W:K_W + S])
            nc.vector.tensor_copy(causal[:, :], stage[:, K_M:K_M + P])
            nc.vector.tensor_copy(distC[:, :, :].rearrange("p t n -> p (t n)"), stage[:, K_DC:K_DC + P])
            nc.vector.tensor_copy(sel[:, :, :].rearrange("p h n -> p (h n)"), stage[:, K_SEL:K_SEL + 1024])
            nc.vector.memset(fT[:, :].bitcast(f32), 0.0)
            for h in range(8):
                ins = nc.vector.tensor_scalar(slopeI[:, h, :], stage[:, K_ID:K_ID + P], SLOPES8[h], None, ALU.mult)
            link(ins)

            for m in (NSA, DIFF, FOX):
                units = units_of(m)
                for n in range(1, len(PROJ[m])):
                    prev, name = PROJ[m][n - 1], PROJ[m][n]
                    if m == NSA or n > 1:
                        split(BI[(m, name)] + 1)
                        post(m, prev)
                    post_t(m, prev)
                    if m == NSA:
                        compression(name)
                split(BI[(m, PROJ[m][-1])] + 2)
                post(m, PROJ[m][-1])
                post_t(m, PROJ[m][-1])

                for e in EVENTS[m]:
                    what, j = e[0], e[1]
                    if what in ("S", "C", "A", "O"):
                        kind, h, c, i = units[j]
                        s0, n = span(units[j])
                    if what == "S":
                        full(dve, ("S", m, j))
                        nc.vector.tensor_reduce(nmx[:, j:j + 1], bank(("S", m, j))[:, 0:n], AX.X, ALU.max, negate=True).then_inc(max_ready, 1)
                    elif what == "C":
                        free(dve, ("S", m, j))
                        if m == DIFF:
                            free(dve, ("S", m, j - 1))
                            link(nc.vector.reciprocal(rl[:, j - 1:j + 1], lsum[:, j - 1:j + 1]))
                            link(nc.vector.tensor_scalar(coef[:, j:j + 1], rl[:, j:j + 1], neglam[:, 0:1], None, ALU.mult))
                            dst = prob[:, 4 + (j // 2) % 2, 0:n]
                            link(nc.vector.tensor_scalar(dst, prob[:, (j - 1) % 4, 0:n], rl[:, j - 1:j], None, ALU.mult))
                            nc.vector.scalar_tensor_tensor(dst, prob[:, j % 4, 0:n], coef[:, j:j + 1], dst, ALU.mult, ALU.add).then_inc(comb_ready, 1)
                        else:
                            link(nc.vector.reciprocal(rl[:, j:j + 1], lsum[:, j:j + 1]))
                            if m == NSA:
                                gi = 8 * (1 if kind == "slc" else 2) + h
                                link(nc.vector.tensor_scalar(coef[:, j:j + 1], rl[:, j:j + 1], gsm[:, i, gi:gi + 1], None, ALU.mult))
                    elif what == "A" and pv_index(m, j) % 2 == 0:
                        b = place[("A", m, j)][0]
                        full(dve, ("A", m, j))
                        nc.vector.tensor_copy(probT[:, 0, 0:n], ps[b][:, 0:n]).then_inc(psum_free[b], 1)
                    elif what == "O":
                        b = place[("O", m, j)][0]
                        full(dve, ("O", m, j))
                        dst = otok[:, i % 2, h * HD:(h + 1) * HD]
                        if m == NSA:
                            free(dve, ("OC", i, h % 2) if kind == "slc" else ("O", m, j - 1))
                            nc.vector.scalar_tensor_tensor(dst, ps[b][:, 0:HD], coef[:, j:j + 1], dst, ALU.mult, ALU.add).then_inc(psum_free[b], 1)
                        elif m == DIFF:
                            nc.vector.tensor_copy(otok[:, i % 2, h * P:(h + 1) * P], ps[b][:, 0:P]).then_inc(psum_free[b], 1)
                        else:
                            nc.vector.tensor_scalar(dst, ps[b][:, 0:HD], rl[:, j:j + 1], None, ALU.mult).then_inc(psum_free[b], 1)
                    elif what == "W":
                        split(j, e[2])
                    elif what == "SC":
                        for k in range(2):
                            full(dve, ("SC", j, k))
                            b = place[("SC", j, k)][0]
                            src = ps[b][:, 0:P].rearrange("p (a n) -> p a n", a=4)
                            link(nc.vector.tensor_reduce(cmx[:, 4 * k:4 * k + 4], src, AX.X, ALU.max))
                            nc.vector.tensor_tensor(pc[:, j % 2, k], src, cmx[:, 4 * k:4 * k + 4].unsqueeze(2).to_broadcast([P, 4, 32]),
                                                    ALU.subtract).then_inc(psum_free[b], 1)
                    elif what == "TC":
                        dve.wait_ge(cexp_ready, j + 1)
                        pv = pc[:, j % 2].rearrange("p e a n -> p (e a) n")
                        link(nc.vector.tensor_reduce(csum[:, :], pv, AX.X, ALU.add))
                        link(nc.vector.reciprocal(crl[:, :], csum[:, :]))
                        if j == 0:
                            link(nc.vector.tensor_scalar(crl[:, :], crl[:, :], valid[:, 0:1], None, ALU.mult))
                        link(nc.vector.tensor_tensor(ccoef[:, :].rearrange("p (e a) -> p e a", e=2), crl[:, :].rearrange("p (e a) -> p e a", e=2),
                                                     gsm[:, j, 0:8].rearrange("p (a e) -> p e a", e=2), ALU.mult))
                        nc.vector.tensor_tensor(pv, pv, ccoef[:, :].unsqueeze(2).to_broadcast([P, 8, 32]), ALU.mult).then_inc(pc_ready, 1)
                    elif what == "OC":
                        for k in range(2):
                            full(dve, ("OC", j, k))
                            b = place[("OC", j, k)][0]
                            dst = otok[:, j % 2, :].rearrange("p (a e c) -> p e a c", e=2, c=HD)[:, k]
                            nc.vector.tensor_copy(dst, ps[b][:, 0:256].rearrange("p (a c) -> p a c", a=4)).then_inc(psum_free[b], 1)
                    elif what == "SUB":
                        dve.wait_ge(sub_sq, j + 1)
                        nc.vector.tensor_reduce(hss[:, j, :], sq[:, 0, :].rearrange("p (h c) -> p h c", c=P), AX.X, ALU.add).then_inc(sub_sums, 1)
                    elif what == "SUN":
                        dve.wait_ge(rstd_ready, rs_at[("SUB", j)])
                        v = otok[:, j % 2, :].rearrange("p (h c) -> p h c", c=P)
                        nc.vector.tensor_tensor(v, v, rstd[:, 4 * j:4 * j + 4].unsqueeze(2).to_broadcast([P, 4, P]), ALU.mult).then_inc(sub_ready, 1)
                    elif what == "OT" and j == TT - 1:
                        for k in range(4):
                            dve.wait_ge(oT_hi, 4 * m + k + 1)
                            nc.vector.tensor_tensor(oT_l[:, k, :], oT[:, k, :], oT_h[:, k, :].bitcast(f32), ALU.subtract).then_inc(oT_lo, 1)
                if m < FOX:
                    post(m + 1, PROJ[m + 1][0])
                for c in range(KD):
                    if c % 4 == 3:
                        split(BI[(m, f"br{c // 4}")] + 2)
                    free(dve, ("G", m, c))
                    full(dve, ("B", m, c))
                    pb = place[("B", m, c)][0]
                    dst = merged[:, c, :] if m == NSA else bt[:, c % 2, :]
                    nc.vector.scalar_tensor_tensor(dst, gate[:, c, :], 1.0, ps[pb][:, :], ALU.add, ALU.mult).then_inc(psum_free[pb], 1)
                    if m > NSA:
                        free(dve, ("B", m, c))
                        free(dve, ("B", NSA, c))
                        if m == FOX:
                            dve.wait_ge(merged_ready, c + 1)
                        nc.vector.tensor_tensor(merged[:, c, :], merged[:, c, :], bt[:, c % 2, :], ALU.add).then_inc(merged_ready, 1)
                    if m == FOX:
                        dve.wait_ge(merged_hi, c + 1)
                        nc.vector.scalar_tensor_tensor(mT_l[:, c, :], merged[:, c, :], 0.5, mT_h[:, c, :].bitcast(f32), ALU.mult,
                                                       ALU.subtract).then_inc(merged_lo, 1)

            def ffn_lo(k):
                take_lo(("N", 1, k), aT_l[:, k, :], aT_h[:, k, :], bank(("N", 1, k))[:, :], par[:, C_FFN + k:C_FFN + k + 1])

            nc.vector.memset(ones[:, :], 1.0).then_inc(diag_ready, 1)
            dve.wait_ge(h_in, 16)
            for n in range(4):
                for half in range(2):
                    full(dve, ("WO", n, half))
                    b = place[("WO", n, half)][0]
                    dst = hid[:, 2 * half:2 * half + 2, n * 256:(n + 1) * 256]
                    nc.vector.tensor_tensor(dst, ps[b][:, :].rearrange("p (t c) -> p t c", t=2), dst, ALU.add).then_inc(psum_free[b], 1)
                for k in range(max(0, 2 * n - 2), 2 * n):
                    ffn_lo(k)
                if n < 3:
                    split(BI[("wo", n)] + 2)
            ffn_lo(6)
            ffn_lo(7)
            dve.wait_ge(sst_ready, 4 * TT)
            nc.vector.tensor_reduce(ss[:, :], sst[:, :, :], AX.X, ALU.add).then_inc(sums_ready, 1)
            dve.wait_ge(rstd_ready, rs_at[("N", 1)])
            for t in range(TT):
                nc.vector.tensor_scalar(diag[:, t, :], ident[:, :], rstd[:, t:t + 1], None, ALU.mult).then_inc(diag_ready, 1)
            split(BI[("wo", 3)] + 2)
            full(dve, ("R",))
            nc.vector.tensor_copy(rstdT[:, :], bank(("R",))[:, :]).then_inc(psum_free[6], 1)
            free(dve, ("R",))

            with dve.Fori(0, N_UP) as i:
                for c in range(2):
                    dve.wait_ge(psum_full[c], i + (up0[c] + 1))
                    nc.vector.tensor_tensor(un[:, c, :], rstdT[:, :], ps[c][:, :], ALU.mult).then_inc(psum_free[c], 1)
                    dve.wait_ge(psum_free[c], i + (up0[c] + 1))

                    def tap(j):
                        return par[:, bass.ds(6 * i + (C_CONVW + 3 * c + j), 1)]

                    nc.vector.tensor_scalar(uc[:, c, :], un[:, c, :], tap(2), par[:, bass.ds(2 * i + (C_CONVB + c), 1)],
                                            ALU.mult, ALU.add).then_inc(conv_step, 1)
                    dve.wait_ge(conv_step, 4 * i + (2 * c + 1))
                    nc.vector.scalar_tensor_tensor(uc[:, c, 1:S], un[:, c, 0:S - 1], tap(1), uc[:, c, 1:S], ALU.mult,
                                                   ALU.add).then_inc(conv_step, 1)
                    dve.wait_ge(conv_step, 4 * i + (2 * c + 2))
                    nc.vector.scalar_tensor_tensor(uc[:, c, 2:S], un[:, c, 0:S - 2], tap(0), uc[:, c, 2:S], ALU.mult,
                                                   ALU.add).then_inc(conv_done, 1)
                dve.wait_ge(conv_done, 2 * i + 2)
                split_lo(B_UP + 2 * i + 2, 0)
                for c in range(2):
                    dve.wait_ge(psum_full[2 + c], i + (up0[2 + c] + 1))
                    dve.wait_ge(glr_ready, 2 * i + (c + 1))
                    nc.vector.tensor_tensor(av[:, c, :], gl[:, c, :], ps[2 + c][:, :], ALU.mult).then_inc(psum_free[2 + c], 1)
                for c in range(2):
                    dve.wait_ge(act_hi, 2 * i + (c + 1))
                    k = bass.ds(2 * i + c, 1)
                    nc.vector.tensor_tensor(actT_l[:, k, :].rearrange("p o n -> p (o n)"), av[:, c, :],
                                            actT_h[:, k, :].rearrange("p o n -> p (o n)").bitcast(f32), ALU.subtract).then_inc(act_lo, 1)
                split_lo(B_UP + 2 * i + 3, 1)
            for n in range(2, N_DOWN):
                split(B_DOWN + n)

            def finish(d):
                full(dve, ("YT", d))
                cols = slice(d * P, (d + 1) * P)
                nc.vector.tensor_tensor(outt[:, :, cols], bank(("YT", d))[:, :].rearrange("p (t c) -> p t c", t=TT), hid[:, :, cols],
                                        ALU.add).then_inc(out_ready, 1)

            for d in range(KD):
                if d % 2 == 1:
                    full(dve, ("Y", d))
                    b = place[("Y", d)][0]
                    nc.vector.tensor_copy(yT[:, d, :], ps[b][:, :]).then_inc(psum_free[b], 1)
                if d >= 2:
                    finish(d - 2)
            finish(KD - 2)
            finish(KD - 1)

        @block.gpsimd
        def _(pool):
            pool.wait_ge(psum_free[6], place[("R",)][1] + 1)
            with pool.Fori(0, N_UP) as i:
                for c in range(2):
                    pool.wait_ge(gelu_ready, 2 * i + (c + 1))
                    nc.gpsimd.tensor_tensor(gl[:, c, :], gl[:, c, :], rstdT[:, :], ALU.mult).then_inc(glr_ready, 1)

        @block.tensor
        def _(pe):
            def begin(key):
                b, r = place[key]
                if r:
                    pe.wait_ge(psum_free[b], r)
                return ps[b]

            def done(key, ins):
                ins.then_inc(psum_full[place[key][0]], 1)

            def passes(dst, a_h, a_l, b_h, b_l, start, stop):
                nc.tensor.matmul(dst, a_h, b_h, start=start, stop=False)
                nc.tensor.matmul(dst, a_h, b_l, start=False, stop=False)
                return nc.tensor.matmul(dst, a_l, b_h, start=False, stop=stop)

            def weights(b, k, cols):
                pe.wait_ge(lo_ready, b + 1)
                return [w[b % 2][:, 0:k * cols].rearrange("p (k c) -> p k c", k=k) for w in (wh, wl)]

            def project(b, keys, cols, tiles, half=None):
                h, l = weights(b, KD, cols)
                for n, key in enumerate(keys):
                    bk = begin(key)
                    for t in range(tiles):
                        tt = (n if half is None else half) * tiles + t
                        rows = slice(tt * P, (tt + 1) * P)
                        for k in range(KD):
                            ins = passes(bk[:, t * cols:(t + 1) * cols], aT_h[:, k, rows], aT_l[:, k, rows], h[:, k], l[:, k],
                                         k == 0, k == KD - 1)
                    done(key, ins)

            def transposes(key, blocks):
                bk = begin(key)
                for n, src in enumerate(blocks):
                    ins = nc.tensor.transpose(bk[:, n * P:(n + 1) * P], src, ident[:, :])
                done(key, ins)

            def post_t(m, name):
                if name not in T_CHUNKS:
                    return
                for half in range(2):
                    free(pe, ("P", m, name, half))
                q = NORMS.index(name)
                for c in T_CHUNKS[name]:
                    transposes(("T", m, name, c), [nrm[q % 2][:, t, c * P:(c + 1) * P] for t in range(TT)])

            def compression(name):
                if name == "nq0":
                    pe.wait_ge(cw_in, 32)
                    for kv in range(2):
                        pe.wait_ge(cpe_ready, kv + 1)
                        bk = begin(("H", kv))
                        for r in range(16):
                            ins = nc.tensor.matmul(bk[:, 0:64], w1_sb[:, kv, r, :], cpe[:, kv, r], start=r == 0, stop=r == 15)
                        done(("H", kv), ins)
                elif name == "nq1":
                    free(pe, ("H", 0))
                    bk = begin(("KC",))
                    done(("KC",), nc.tensor.matmul(bk[0:HD, 0:HD], chid[:, 0, 0:64], w2_sb[:, 0, :], start=True, stop=True))
                    free(pe, ("H", 1))
                    bk = begin(("VC",))
                    done(("VC",), nc.tensor.matmul(bk[:, 0:HD], chid[:, 1, :], w2_sb[:, 1, :], start=True, stop=True))
                    pe.wait_ge(small_v, 4)
                    bk = begin(("F",))
                    for i in range(TT):
                        ins = nc.tensor.matmul(bk[0:8, :], logf[:, i, :], later[:, 384 - P * i:384 - P * i + S], start=i == 0, stop=i == TT - 1)
                    done(("F",), ins)
                elif name == "slc":
                    free(pe, ("KC",))
                    bk = begin(("KCT",))
                    done(("KCT",), nc.tensor.transpose(bk[:, 0:64], ktok[:, :, :].rearrange("n r c -> n (r c)"), ident[0:HD, 0:HD]))

            pe.wait_ge(id_in, 16)
            pe.wait_ge(xn_ready, 3)
            pe.wait_ge(xn_act, 1)
            for k in range(KD):
                transposes(("N", 0, k), [xn0[:, t, k * P:(k + 1) * P] for t in range(TT)])

            for m in (NSA, DIFF, FOX):
                units = units_of(m)
                for n, name in enumerate(PROJ[m]):
                    b = BI[(m, name)]
                    if name == "cmp":
                        h, l = weights(b, KD, 256)
                        for c in range(2):
                            key = ("P", m, name, c)
                            bk = begin(key)
                            for k in range(KD):
                                if c == 0:
                                    free(pe, ("N", 0, k))
                                cols = slice(c * P, (c + 1) * P)
                                ins = passes(bk[:, :], h[:, k, cols], l[:, k, cols], aT_h[:, k], aT_l[:, k], k == 0, k == KD - 1)
                            done(key, ins)
                    elif name == "small":
                        project(b, [("P", m, name, 0)], 32, TT)
                    elif m == NSA or n > 0:
                        project(b, [("P", m, name, c) for c in range(2)], 256, 2)
                    if n > 0:
                        post_t(m, PROJ[m][n - 1])
                    if m == NSA:
                        compression(name)
                post_t(m, PROJ[m][-1])

                for name in PROJ[m]:
                    for c in T_CHUNKS.get(name, []):
                        free(pe, ("T", m, name, c))
                if m == NSA:
                    for key in (("VC",), ("KCT",), ("F",)):
                        free(pe, key)

                def scores(j):
                    u = units[j]
                    kind, h, c, i = u
                    s0, n = span(u)
                    rows, qc, kc = operands(m, u)
                    bk = begin(("S", m, j))
                    dst = bk[:, 0:n]
                    if kind == "fox":
                        nc.tensor.matmul(dst, sel[:, h, :], fT[:, 0:n], start=True, stop=False)
                        nc.tensor.matmul(bk[:, n - P:n], identr[:, :], causal[:, :], start=False, stop=False)
                    else:
                        dist = distW if kind == "win" else distD
                        sl = h if kind != "diff" else 2 * h + 1
                        c0 = 384 - P * i + s0
                        nc.tensor.matmul(dst, slopeI[:, sl, :], dist[:, c0:c0 + n], start=True, stop=False)
                    t = slice(i * P, (i + 1) * P)
                    done(("S", m, j), passes(dst, qk_h[rows, qc, t], qk_l[rows, qc, t], qk_h[rows, kc, s0:s0 + n], qk_l[rows, kc, s0:s0 + n],
                                             False, True))

                def values(q):
                    u = units[q]
                    s0, n = span(u)
                    v0, vw = v_cols(u)
                    free(pe, ("A", m, q))
                    for name in PROJ[m]:
                        if name[1] == "v":
                            free(pe, ("P", m, name, 0))
                            free(pe, ("P", m, name, 1))
                    bk = begin(("O", m, q))
                    for kb in range(n // P):
                        ins = nc.tensor.matmul(bk[:, 0:vw], probT[:, pv_index(m, q) % 2, kb * P:(kb + 1) * P],
                                               V[:, s0 // P + kb, v0:v0 + vw], start=kb == 0, stop=kb == n // P - 1)
                    done(("O", m, q), ins)

                def gate_step(f):
                    c, k, p = f // GATE_STEPS, f % GATE_STEPS // 3, f % 3
                    b = BI[(m, f"gate{c // 2}")]
                    if f % GATE_STEPS == 0:
                        weights(b, KD, 256)
                    h, l = [w[b % 2][:, :].rearrange("p (k c) -> p k c", k=KD) for w in (wh, wl)]
                    key = ("G", m, c)
                    bk = begin(key) if f % GATE_STEPS == 0 else ps[place[key][0]]
                    cols = slice(c % 2 * P, c % 2 * P + P)
                    ins = nc.tensor.matmul(bk[:, :], (l if p == 2 else h)[:, k, cols], (aT_l if p == 1 else aT_h)[:, k],
                                           start=f % GATE_STEPS == 0, stop=f % GATE_STEPS == GATE_STEPS - 1)
                    if f % GATE_STEPS == GATE_STEPS - 1:
                        done(key, ins)

                for e in EVENTS[m]:
                    what, j = e[0], e[1]
                    if what == "S":
                        scores(j)
                    elif what == "G":
                        for f in range(e[1], e[2]):
                            gate_step(f)
                    elif what == "A":
                        if m == DIFF:
                            pe.wait_ge(comb_ready, j // 2 + 1)
                        else:
                            free(pe, ("S", m, j))
                        s0, n = span(units[j])
                        slot = 4 + (j // 2) % 2 if m == DIFF else j % 4
                        transposes(("A", m, j), [prob[:, slot, kb * P:(kb + 1) * P] for kb in range(n // P)])
                    elif what == "O":
                        values(j)
                    elif what == "SC":
                        rows = slice(j * P, (j + 1) * P)
                        for k in range(2):
                            bk = begin(("SC", j, k))
                            hd_ = slice(64 * k, 64 * k + 64)
                            for a in range(4):
                                dst = bk[:, 32 * a:32 * a + 32]
                                nc.tensor.matmul(dst, slopeI[:, 2 * a + k, :], distC[:, j, :], start=True, stop=False)
                                ins = passes(dst, qk_h[hd_, a, rows], qk_l[hd_, a, rows], kc_h[hd_, a // 2], kc_l[hd_, a // 2], False, True)
                            done(("SC", j, k), ins)
                    elif what == "TC":
                        pe.wait_ge(pc_ready, j + 1)
                        transposes(("TC", j), [pc[:, j % 2, k].rearrange("p a n -> p (a n)") for k in range(2)])
                    elif what == "OC":
                        free(pe, ("TC", j))
                        for k in range(2):
                            bk = begin(("OC", j, k))
                            done(("OC", j, k), nc.tensor.matmul(bk[:, 0:256], pcT[:, k, :], vblk[:, :, :].rearrange("p a c -> p (a c)"),
                                                                start=True, stop=True))
                    elif what == "OT":
                        last = len(units) // TT * (j + 1) - 1
                        if m == DIFF:
                            pe.wait_ge(sub_ready, j + 1)
                        else:
                            free(pe, ("O", m, last - 1))
                            free(pe, ("O", m, last))
                        transposes(("OT", m, j), [otok[:, j % 2, k * P:(k + 1) * P] for k in range(4)])
                    elif what == "P":
                        name = PROJ[m + 1][0]
                        project(BI[(m + 1, name)], [("P", m + 1, name, j)], 256, 2, half=j)

                for c in range(KD):
                    h, l = weights(BI[(m, f"br{c // 4}")], 4, S)
                    bk = begin(("B", m, c))
                    cols = slice(c % 4 * P, c % 4 * P + P)
                    for k in range(4):
                        pe.wait_ge(oT_lo, 4 * m + k + 1)
                        ins = passes(bk[:, :], h[:, k, cols], l[:, k, cols], oT_h[:, k], oT_l[:, k], k == 0, k == 3)
                    done(("B", m, c), ins)

            def ffn_transposes(k):
                free(pe, ("WO", k // 2, 0))
                free(pe, ("WO", k // 2, 1))
                transposes(("N", 1, k), [hid[:, t, k * P:(k + 1) * P] for t in range(TT)])

            for n in range(4):
                h, l = weights(BI[("wo", n)], KD, 256)
                for half in range(2):
                    key = ("WO", n, half)
                    bk = begin(key)
                    for t in range(2):
                        rows = slice((2 * half + t) * P, (2 * half + t + 1) * P)
                        for k in range(KD):
                            pe.wait_ge(merged_lo, k + 1)
                            ins = passes(bk[:, t * 256:(t + 1) * 256], mT_h[:, k, rows], mT_l[:, k, rows], h[:, k], l[:, k], k == 0, k == KD - 1)
                    done(key, ins)
                for k in range(max(0, 2 * n - 2), 2 * n):
                    ffn_transposes(k)
            ffn_transposes(6)
            ffn_transposes(7)

            def up_chunk(i, b, c, first=False):
                h, l = [w[b][:, :].rearrange("p (k c) -> p k c", k=KD) for w in (wh, wl)]
                bk = 2 * b + c
                pe.wait_ge(psum_free[bk], i + up0[bk])
                cols = slice(c * P, (c + 1) * P)
                for k in range(KD):
                    if first:
                        free(pe, ("N", 1, k))
                    ins = passes(ps[bk][:, :], h[:, k, cols], l[:, k, cols], aT_h[:, k], aT_l[:, k], k == 0, k == KD - 1)
                ins.then_inc(psum_full[bk], 1)

            for b in range(2):
                pe.wait_ge(lo_ready, B_UP + b + 1)
                for c in range(2):
                    up_chunk(0, b, c, first=(b, c) == (0, 0))
                    if (b, c) == (0, 0):
                        pe.wait_ge(diag_ready, TT + 1)
                        bk = begin(("R",))
                        for t in range(TT):
                            ins = nc.tensor.matmul(bk[:, t * P:(t + 1) * P], ones[:, :], diag[:, t, :], start=True, stop=True)
                        done(("R",), ins)
            with pe.Fori(1, N_UP) as i:
                for b in range(2):
                    pe.wait_ge(lo_ready, 2 * i + (B_UP + b + 1))
                    for c in range(2):
                        up_chunk(i, b, c)

            def finish(d):
                free(pe, ("Y", d))
                transposes(("YT", d), [yT[:, d, t * P:(t + 1) * P] for t in range(TT)])

            def down(n, slot, first, last):
                pe.wait_ge(lo_ready, n + (B_DOWN + 1))
                pe.wait_ge(act_lo, 2 * n + 2)
                h, l = [w[slot][:, :].rearrange("p (k c) -> p k c", k=2) for w in (wh, wl)]
                acts = [[t[:, bass.ds(2 * n + k, 1), :].rearrange("p o n -> p (o n)") for t in (actT_h, actT_l)] for k in range(2)]
                for d in range(KD):
                    if first:
                        begin(("Y", d))
                    cols = slice(d * P, (d + 1) * P)
                    for k in range(2):
                        ins = passes(ps[d][:, :], h[:, k, cols], l[:, k, cols], acts[k][0], acts[k][1], first and k == 0, last and k == 1)
                    if last:
                        done(("Y", d), ins)
                        if d >= 2:
                            finish(d - 2)
                if not last:
                    ins.then_inc(down_used, 1)

            down(0, 0, True, False)
            with pe.Fori(1, N_DOWN - 2, 2) as n:
                down(n, 1, False, False)
                down(n + 1, 0, False, False)
            down(N_DOWN - 2, 1, False, False)
            down(N_DOWN - 1, 0, False, True)
            finish(KD - 2)
            finish(KD - 1)


def pack_params(np, a):
    def cols(v):
        return v.reshape(-1, P).T

    def twice(v):
        return np.concatenate([v, v])[:, None]

    conv = a["conv_w"][0].reshape(3, NF, P).transpose(2, 1, 0).reshape(P, 3 * NF)
    pe = [a["cmp_pe"][0, i].reshape(16, P).T for i in range(2)]
    rows = [np.broadcast_to(v.reshape(1, -1), (P, v.size)) for v in (a["diff_lam"][0], a["fox_b"][0])]
    gains = [a["nsa_q_g"][0], a["diff_q_g"][0], a["fox_q_g"][0], a["nsa_k_g"][0, 0], a["nsa_k_g"][0, 1], a["nsa_k_g"][0, 2],
             a["diff_k_g"][0], a["fox_k_g"][0]]
    parts = [cols(a["attn_norm_g"][0]), cols(a["ffn_norm_g"][0]), conv, cols(a["conv_b"][0]), cols(a["diff_subln_g"][0])]
    out = np.concatenate(parts + [twice(g) for g in gains] + pe + rows, axis=1)
    assert out.shape == (P, C_END)
    return np.ascontiguousarray(out)


def pack_constants(np):
    far = -1e30
    c = np.zeros((P, K_END), np.float32)
    p = np.arange(P)[:, None]
    col = np.arange(S)[None, :]
    c[:, K_ID:K_ID + P] = np.eye(P)
    dist = 384 + p - col
    c[:, K_D:K_D + S] = np.where(dist >= 0, -dist, far)
    c[:, K_W:K_W + S] = np.where((dist >= 0) & (dist < 256), -dist, far)
    c[:, K_M:K_M + P] = np.where(np.arange(P)[None, :] <= p, 0.0, far)
    for i in range(TT):
        dc = i * P + p - (16 * np.arange(32)[None, :] + 31)
        c[:, K_DC + 32 * i:K_DC + 32 * i + 32] = np.where(dc >= 0, -dc, far)
    for h in range(8):
        c[h, K_SEL + P * h:K_SEL + P * (h + 1)] = 1.0
        c[32 + h, K_SEL + P * h:K_SEL + P * (h + 1)] = 1.0
    c[:, K_U:K_U + 896] = np.arange(896)[None, :] - 384 >= p
    c[:, K_VALID] = np.arange(P) >= 31
    return c


def pack_weights(np, a):
    w_in, w_br, w_o, w_up, w_down = (a[n][0] for n in ("w_in", "w_br", "w_o", "w_up", "w_down"))
    col = {"nq": 0, "cmp": 512, "slc": 768, "win": 1024, "ngate": 1280, "dq": 1304, "dk": 1816, "dv": 2328,
           "fq": 2840, "fk": 3352, "fv": 3864, "ff": 4376, "mg": 4384}

    def rows_of(w, k):
        return w.reshape(k, P, -1).transpose(1, 0, 2).reshape(P, -1)

    out = np.zeros((N_BLOCKS, P, BLOCK), np.float32)
    for n, (m, name) in enumerate(BLOCKS):
        if m == "wo":
            out[n] = rows_of(w_o[:, 256 * name:256 * name + 256], KD)
        elif name == "small":
            w = np.concatenate([w_in[:, col["ngate"]:col["ngate"] + 24], w_in[:, col["ff"]:col["ff"] + 8]], axis=1)
            out[n][:, 0:KD * 32] = rows_of(w, KD)
        elif name.startswith("gate"):
            c = col["mg"] + D * m + 256 * int(name[4])
            out[n] = rows_of(w_in[:, c:c + 256], KD)
        elif name.startswith("br"):
            h = int(name[2])
            out[n] = rows_of(w_br[m][:, S * h:S * h + S], 4)
        else:
            c = col[name] if name in col else col[name[:2]] + 256 * int(name[2])
            out[n] = rows_of(w_in[:, c:c + 256], KD)
    for i in range(N_UP):
        out[B_UP + 2 * i] = rows_of(w_up[:, 256 * i:256 * i + 256], KD)
        out[B_UP + 2 * i + 1] = rows_of(w_up[:, D_FF + 256 * i:D_FF + 256 * i + 256], KD)
    for n in range(N_DOWN):
        out[B_DOWN + n] = rows_of(w_down[256 * n:256 * n + 256], 2)
    return out


def kernel(**inputs):
    import numpy as np
    import concourse.bacc as bacc
    from concourse.bass_utils import run_bass_kernel_spmd

    a = {k: np.asarray(v) for k, v in inputs.items()}
    arrays = {
        "x": a["x"],
        "wblk": pack_weights(np, a),
        "w1": np.ascontiguousarray(a["cmp_w1"][0].reshape(2, 16, P, P).transpose(2, 0, 1, 3)),
        "w2": np.ascontiguousarray(a["cmp_w2"][0].transpose(1, 0, 2)),
        "params": pack_params(np, a),
        "consts": pack_constants(np),
    }
    nc = bacc.Bacc("TRN2", target_bir_lowering=False, num_devices=1)
    args = [nc.dram_tensor(n, v.shape, mybir.dt.from_np(v.dtype), kind="ExternalInput").ap() for n, v in arrays.items()]
    args.append(nc.dram_tensor("out", (1, S, D), mybir.dt.float32, kind="ExternalOutput").ap())
    build(nc, *args)
    r = run_bass_kernel_spmd(nc, [arrays], core_ids=[0])
    return r.results[0]["out"]
```

```python
import concourse.bass as bass
from concourse import mybir
from contextlib import ExitStack

P = 128
S = 512
D = 1024
HD = 64
TT = S // P
KD = D // P
D_FF = 2816
NF = D_FF // P
NCMP = 31
EPS = 1e-6
LAM_INIT = 0.2
BLOCK = 2048

C_ATTN, C_FFN = 0, 8
C_CONVW = 16
C_CONVB = C_CONVW + 3 * NF
C_SUBLN = C_CONVB + NF
C_QG = C_SUBLN + 1
C_KG = C_QG + 3
C_PE = C_KG + 5
C_LAM = C_PE + 32
C_FOXB = C_LAM + 4 * HD
C_END = C_FOXB + 8
K_ID, K_D, K_W, K_M, K_DC, K_SEL, K_VALID, K_U = 0, 128, 640, 1152, 1280, 1408, 2432, 2433
K_END = 3329

NSA, DIFF, FOX = 0, 1, 2
PROJ = {NSA: ["cmp", "small", "nq0", "nq1", "slc", "win"],
        DIFF: ["dq0", "dq1", "dk0", "dk1", "dv0", "dv1"],
        FOX: ["fq0", "fq1", "fk0", "fk1", "fv0", "fv1"]}
BLOCKS = [(NSA, PROJ[NSA][0])]
for _m in (NSA, DIFF, FOX):
    BLOCKS += [(_m, n) for n in PROJ[_m][1:]] + [(_m, f"gate{n}") for n in range(4)]
    BLOCKS += [(_m + 1, PROJ[_m + 1][0])] if _m < FOX else []
    BLOCKS += [(_m, f"br{n}") for n in range(2)]
BLOCKS += [("wo", n) for n in range(4)]
BI = {n: i for i, n in enumerate(BLOCKS)}
B_UP = len(BLOCKS)
N_UP = D_FF // 256
B_DOWN = B_UP + 2 * N_UP
N_DOWN = NF // 2
N_BLOCKS = B_DOWN + N_DOWN
assert B_UP % 2 == 0

LN_EXP = "natural_log_exp_and_others"
SLOPES8 = [2.0 ** -(h + 1) for h in range(8)]


def units_of(m):
    if m == NSA:
        return [(k, h, 0, i) for i in range(TT) for h in range(8) for k in ("slc", "win")]
    if m == DIFF:
        return [("diff", h, c, i) for i in range(TT) for h in range(4) for c in range(2)]
    return [("fox", h, 0, i) for i in range(TT) for h in range(8)]


def span(u):
    kind, h, c, i = u
    s0 = max(0, i - 2) * P if kind == "win" else 0
    return s0, (i + 1) * P - s0


GATE_STEPS = KD * 3
FILL = KD * GATE_STEPS
HEAD_FILL = {NSA: 24, DIFF: 4, FOX: 4}


def has_pv(m, q):
    return m != DIFF or q % 2 == 1


def pv_index(m, q):
    return q // 2 if m == DIFF else q


def attention_events(m):
    U = len(units_of(m))
    per = U // TT
    t_lag, o_lag = (3, 4) if m == DIFF else (2, 3)
    at = {}

    def put(j, *event):
        at.setdefault(j, []).append(event)

    tail = 20 if m == FOX else 0
    head = HEAD_FILL[m]
    slots = U + o_lag
    for piece in range(4):
        put(piece, "W", BI[(m, "gate1")], piece)
        put(piece + 1, "WL", BI[(m, "gate1")], piece)

    def put_fill(j, f0, f1):
        put(j, "G", f0, f1)
        for f in range(f0, f1):
            if (f + 1) % (2 * GATE_STEPS) == 0:
                b = BI[(m, "gate0")] + f // (2 * GATE_STEPS) + 2
                for piece in range(4):
                    if m < FOX or b < BI[(m, "gate3")] + 2:
                        put(j + 1 + piece, "W", b, piece)
                        put(j + 2 + piece, "WL", b, piece)

    if m == NSA:
        put(-2, "SC", 0)
        put(-1, "G", head, head + 8)
        put(1, "CN", 0)
        put(2, "TC", 0)
        put(3, "OC", 0)
        for i in range(1, TT):
            put(per * i - 12, "SC", i)
            put(per * i - 10, "CN", i)
            put(per * i - 8, "TC", i)
            put(per * i - 6, "OC", i)
        head += 8
    for j in range(slots):
        n = FILL - tail - head
        put_fill(j, head + n * j // slots, head + n * (j + 1) // slots)
        if j < U:
            put(j, "S", j)
    for q in range(U):
        if has_pv(m, q):
            put(q + 1, "C", q)
            put(q + t_lag, "A", q)
            put(q + o_lag, "O", q)
    for i in range(TT):
        last = per * (i + 1) - 1 + o_lag
        if m == DIFF:
            put(last, "SUB", i)
            put(last + 1, "SUN", i)
            if i < TT - 1:
                put(last + 3, "OT", i)
        elif i < TT - 1:
            put(last + 1, "OT", i)
    order = {k: n for n, k in enumerate(("S", "C", "CN", "TC", "OC", "G", "SC", "A", "O", "SUB", "SUN", "OT", "WL", "W"))}
    out = [e for j in sorted(at) for e in sorted(at[j], key=lambda e: order[e[0]])]
    first = [("G", 0, HEAD_FILL[m]), ("T",)]
    if m == FOX:
        out += [("G", FILL - tail, FILL - 8), ("OT", TT - 1), ("G", FILL - 8, FILL), ("W", BI[(m, "gate3")] + 2, None), ("WL", BI[(m, "gate3")] + 2, None)]
    else:
        out += [("P", 0, 0), ("P", 0, 1), ("OT", TT - 1), ("P", 1, 0), ("P", 1, 1)]
    return first + out


def build(nc, x, wblk, w1, w2, params, consts, out):
    f32, f32r = mybir.dt.float32, mybir.dt.float32r
    ACT, ALU, AX = mybir.ActivationFunctionType, mybir.AluOpType, mybir.AxisListType
    KB = 1024

    place, results = {}, [0] * 8

    def plan(key, bank):
        place[key] = (bank, results[bank])
        results[bank] += 1

    turn = 0

    def plan_t(key):
        nonlocal turn
        plan(key, 4 + turn % 2)
        turn += 1

    T_CHUNKS = {n: [0, 1] for n in ("nq0", "nq1", "slc", "win", "dq0", "dq1", "dk0", "dk1", "fq0", "fq1", "fk0", "fk1")}
    EVENTS = {m: attention_events(m) for m in (NSA, DIFF, FOX)}

    def plan_p(m, name):
        for half in range(1 if name == "small" else 2):
            plan(("P", m, name, half), 6 + half if name == "nq0" else (BI[(m, name)] % 2) * 2 + half)

    for k in range(KD):
        plan(("N", 0, k), k)
    for m in (NSA, DIFF, FOX):
        for n, name in enumerate(PROJ[m]):
            if m == NSA or n > 0:
                plan_p(m, name)
            if n > 0:
                for c in T_CHUNKS.get(PROJ[m][n - 1], []):
                    plan_t(("T", m, PROJ[m][n - 1], c))
            if name == "nq0":
                plan_t(("ST",))
                plan(("H", 0), 0)
                plan(("H", 1), 1)
            if name == "nq1":
                plan(("KC",), 6)
                plan(("VC",), 7)
            if name == "slc":
                plan(("KCT",), 7)
                plan(("F",), 6)
        for e in EVENTS[m]:
            if e[0] == "T":
                for c in T_CHUNKS.get(PROJ[m][-1], []):
                    plan_t(("T", m, PROJ[m][-1], c))
            elif e[0] == "S":
                plan(("S", m, e[1]), 6 + e[1] % 2)
            elif e[0] == "G":
                for f in range(e[1], e[2]):
                    if f % GATE_STEPS == 0:
                        plan(("G", m, f // GATE_STEPS), f // GATE_STEPS % 2)
            elif e[0] == "A":
                plan_t(("A", m, e[1]))
            elif e[0] == "O":
                plan(("O", m, e[1]), 2 + pv_index(m, e[1]) % 2)
            elif e[0] == "SC":
                plan(("SC", e[1]), 7)
            elif e[0] == "TC":
                plan_t(("TC", e[1]))
            elif e[0] == "OC":
                plan(("OC", e[1], 0), 2)
                plan(("OC", e[1], 1), 3)
            elif e[0] == "OT":
                plan_t(("OT", m, e[1]))
            elif e[0] == "P":
                name = PROJ[m + 1][0]
                if e[2] == 0:
                    plan(("P", m + 1, name, e[1]), (BI[(m + 1, name)] % 2) * 2 + e[1])
        for c in range(KD):
            plan(("B", m, c), (2, 3, 6, 7, 4, 5, 0, 1)[c])
    for n in range(4):
        for half in range(2):
            plan(("WO", n, half), (n % 2) * 2 + half)
        for k in range(2 * n - 2, 2 * n):
            if k >= 0:
                plan(("N", 1, k), 4 + k % 2)
    plan(("N", 1, 6), 4)
    plan(("N", 1, 7), 5)
    plan(("R",), 6)
    up0 = list(results)
    for b in range(4):
        results[b] += N_UP
    for d in range(KD):
        plan(("Y", d), d)
    for d in range(KD):
        plan(("YT", d), d)

    with ExitStack() as ctx:
        base = -(-nc.sbuf_base // 64) * 64
        used = [0]

        def at(name, shape, dt, off):
            size = 4
            for s in shape[1:]:
                size *= s
            used[0] = max(used[0], off + size)
            return nc.alloc_sbuf_tensor_at(name, shape, dt, offset=base + off)

        aT_h = at("aT_h", [P, KD, S], f32r, 0)
        aT_l = at("aT_l", [P, KD, S], f32r, 16 * KB)
        raw = [at(f"raw{i}", [P, BLOCK], f32, (32 + 8 * i) * KB) for i in range(2)]
        wh = [at(f"wh{i}", [P, BLOCK], f32r, (48 + 8 * i) * KB) for i in range(2)]
        wl = [at(f"wl{i}", [P, BLOCK], f32r, (64 + 8 * i) * KB) for i in range(2)]
        RX = 80 * KB
        x0 = at("x0", [P, TT, D], f32, RX)
        nrm = [at(f"nrm{i}", [P, TT, 256], f32, RX + 4 * KB * i) for i in range(2)]
        prob = at("prob", [P, 6, S], f32, RX)
        probT = at("probT", [P, 2, S], f32, RX + 12 * KB)
        bt = at("bt", [P, 2, S], f32, RX + 12 * KB)
        hid = at("hid", [P, TT, D], f32, RX)
        RA = 96 * KB
        stage = at("stage", [P, K_U], f32, RA)
        xn0 = at("xn0", [P, TT, D], f32, RA + 16 * KB)
        q_hl = at("q_hl", [P, 8, S], f32r, RA)
        k_hh = at("k_hh", [P, 8, S], f32r, RA + 16 * KB)
        k_l = at("k_l", [P, 4, S], f32r, RA + 32 * KB)
        oT_h = at("oT_h", [P, 4, S], f32r, RA)
        oT_l = at("oT_l", [P, 4, S], f32r, RA + 8 * KB)
        mT_h = at("mT_h", [P, KD, S], f32r, RA + 16 * KB)
        mT_l = at("mT_l", [P, KD, S], f32r, RA + 32 * KB)
        V = at("V", [P, TT, S], f32, RA + 40 * KB)
        biasC = at("biasC", [P, TT, 8, 32], f32r, RA + 24 * KB)
        smT = at("smT", [32, S], f32, RX + 12 * KB)
        gate = at("gate", [P, KD, S], f32, RA + 48 * KB)
        w1_sb = at("w1_sb", [P, 2, 16, P], f32, RA + 48 * KB)
        merged = at("merged", [P, KD, S], f32, RA + 64 * KB)
        RM = RA + 64 * KB
        cx = at("cx", [P, 2, S], f32, RM)
        cpe = at("cpe", [P, 2, 16, 2, 32], f32, RM + 4 * KB)
        pc = at("pc", [P, 2, 2, 4, 32], f32, RM)
        pcT = at("pcT", [P, 2, P], f32, RM + 2 * KB)
        w2_sb = at("w2_sb", [P, 2, HD], f32, RM + 12 * KB)
        chid = at("chid", [P, 2, P], f32, RM + 12 * KB + 512)
        ktok = at("ktok", [HD, 2, HD], f32, RM + 13 * KB + 512)
        ksq = at("ksq", [HD, HD], f32, RM + 11 * KB)
        kc_hh = at("kc_hh", [P, 2, 32], f32r, RM + 14 * KB)
        kc_l = at("kc_l", [P, 2, 2, 32], f32r, RM + 14 * KB + 512)
        vblk = at("vblk", [P, 4, HD], f32, RM + 15 * KB)
        sq = at("sq", [P, 2, S], f32, RA + 80 * KB)
        RC = RA + 84 * KB
        slopeI = at("slopeI", [P, 8, P], f32r, RC)
        distD = at("distD", [P, S], f32r, RC + 4 * KB)
        distW = at("distW", [P, S], f32r, RC + 6 * KB)
        causal = at("causal", [P, P], f32r, RC + 8 * KB)
        sel = at("sel", [P, 8, P], f32r, RC + 9 * KB)
        later = at("later", [P, 896], f32, RC + 13 * KB)
        otok = at("otok", [P, 2, S], f32, RC + 13 * KB)
        fT = at("fT", [P, S], f32r, RC + 17 * KB)
        rstdT = at("rstdT", [P, S], f32, RC + 16 * KB)
        ones = at("ones", [P, P], f32, RC + 18 * KB)
        diag = at("diag", [P, TT, P], f32, RA + 82 * KB)
        actT_h = at("actT_h", [P, NF, S], f32r, RA)
        actT_l = at("actT_l", [P, NF, S], f32r, RA + 44 * KB)
        uc = at("uc", [P, 2, S], f32, RA + 88 * KB)
        gl = at("gl", [P, 2, S], f32, RA + 92 * KB)
        av = at("av", [P, 2, S], f32, RA + 96 * KB)
        yT = at("yT", [P, KD, S], f32, 0)
        outt = at("outt", [P, TT, D], f32, 32 * KB)
        RK = RC + 19 * KB
        ident = at("ident", [P, P], f32, RK)
        identr = at("identr", [P, P], f32r, RK + 512)
        par = at("par", [P, C_END], f32, RK + KB)
        RS = RK + KB + -(-4 * C_END // 32) * 32
        so = [RS]

        def small(name, shape, dt=f32):
            t = at(name, shape, dt, so[0])
            n = 4
            for s in shape[1:]:
                n *= s
            so[0] += -(-n // 32) * 32
            return t

        ss = small("ss", [P, TT])
        xss = small("xss", [P, TT, 2])
        sst = small("sst", [P, TT, 4])
        lnv = small("lnv", [P, 16])
        rstd = small("rstd", [P, 16])
        hss = small("hss", [P, TT, 4])
        epsc = small("epsc", [P, 1])
        un = at("un", [P, 2, S], f32, so[0])
        nmx = small("nmx", [P, 64])
        lsum = small("lsum", [P, 64])
        rl = small("rl", [P, 64])
        coef = small("coef", [P, 64])
        cmx = small("cmx", [P, 8])
        csum = small("csum", [P, 8])
        crl = small("crl", [P, 8])
        ccoef = small("ccoef", [P, 8])
        smallt = small("smallt", [P, TT, 32])
        gsm = small("gsm", [P, TT, 24])
        logf = small("logf", [P, TT, 8])
        lf1 = small("lf1", [P, TT, 8])
        lf2 = small("lf2", [P, TT, 8])
        lprod = small("lprod", [P, 2, HD])
        lamt = small("lamt", [P, 2])
        lame = small("lame", [P, 2])
        neglam = small("neglam", [P, 1])
        valid = small("valid", [P, 1])
        kss = small("kss", [HD, 1])
        assert base + used[0] <= nc.sbuf_usable_end, (base + used[0], nc.sbuf_usable_end)

        ps = [ctx.enter_context(nc.psum_tensor(f"ps{i}", [P, S], f32)) for i in range(8)]

        def sem(name):
            return ctx.enter_context(nc.semaphore(name))

        psum_full = [sem(f"psum_full{i}") for i in range(8)]
        psum_free = [sem(f"psum_free{i}") for i in range(8)]
        raw_in = [sem(f"raw_in{i}") for i in range(2)]
        hi_ready = sem("hi_ready")
        lo_ready = sem("lo_ready")
        down_used = sem("down_used")
        x_in = [sem(f"x_in{t}") for t in range(TT)]
        id_in, par_in, const_in, cw_in, h_in = (sem(n) for n in ("id_in", "par_in", "const_in", "cw_in", "h_in"))
        x_sums = sem("x_sums")
        xsq_ready = sem("xsq_ready")
        first_lo = sem("first_lo")
        eps_set = sem("eps_set")
        pc_ready = sem("pc_ready")
        oT_hi = sem("oT_hi")
        sub_sums = sem("sub_sums")
        diag_ready = sem("diag_ready")
        glr_ready = sem("glr_ready")
        act_link, dve_link = sem("act_link"), sem("dve_link")
        xn_ready = sem("xn_ready")
        hi_taken = sem("hi_taken")
        sq_ready = sem("sq_ready")
        hss_ready = sem("hss_ready")
        rstd_ready = sem("rstd_ready")
        max_ready = sem("max_ready")
        comb_ready = sem("comb_ready")
        cexp_ready = sem("cexp_ready")
        small_v, small_a = sem("small_v"), sem("small_a")
        const_ready = sem("const_ready")
        cpe_ready = sem("cpe_ready")
        ksq_ready, kss_ready = sem("ksq_ready"), sem("kss_ready")
        sub_sq = sem("sub_sq")
        sst_ready, sums_ready = sem("sst_ready"), sem("sums_ready")
        conv_done = sem("conv_done")
        sub_ready = sem("sub_ready")
        conv_step = sem("conv_step")
        gelu_ready, act_hi = sem("gelu_ready"), sem("act_hi")
        act_lo = sem("act_lo")
        merged_ready = sem("merged_ready")
        merged_hi, merged_lo = sem("merged_hi"), sem("merged_lo")
        out_ready, out_done = sem("out_ready"), sem("out_done")

        def free(eng, key):
            b, r = place[key]
            eng.wait_ge(psum_free[b], r + 1)

        def full(eng, key):
            b, r = place[key]
            eng.wait_ge(psum_full[b], r + 1)

        last_result = {}
        for m in (NSA, DIFF, FOX):
            for name in PROJ[m]:
                last_result[BI[(m, name)]] = ("P", m, name, 0 if name == "small" else 1)
            for n in range(4):
                last_result[BI[(m, f"gate{n}")]] = ("G", m, 2 * n + 1)
            for n in range(2):
                last_result[BI[(m, f"br{n}")]] = ("B", m, 4 * n + 3)
        for n in range(4):
            last_result[BI[("wo", n)]] = ("WO", n, 1)

        def bank(key):
            return ps[place[key][0]]

        hi_order = [("N", 0, k) for k in range(KD)]
        for m in (NSA, DIFF, FOX):
            for n, name in enumerate(PROJ[m]):
                if n > 0:
                    hi_order += [("T", m, PROJ[m][n - 1], c) for c in T_CHUNKS.get(PROJ[m][n - 1], [])]
                if name == "slc":
                    hi_order += [("KCT",), ("F",)]
            hi_order += [("T", m, PROJ[m][-1], c) for c in T_CHUNKS.get(PROJ[m][-1], [])]
        hi_order += [("N", 1, k) for k in range(KD)]
        hi_at = {k: n + 1 for n, k in enumerate(hi_order)}

        QK_CHUNK = {"nq0": 0, "nq1": 2, "slc": 4, "win": 6, "dq0": 0, "dq1": 2, "dk0": 4, "dk1": 6,
                    "fq0": 0, "fq1": 2, "fk0": 4, "fk1": 6}
        GAIN = {"nq0": C_QG, "nq1": C_QG, "slc": C_KG + 1, "win": C_KG + 2, "dq0": C_QG + 1, "dq1": C_QG + 1,
                "dk0": C_KG + 3, "dk1": C_KG + 3, "fq0": C_QG + 2, "fq1": C_QG + 2, "fk0": C_KG + 4, "fk1": C_KG + 4}
        NORM_JOBS = [(m, n) for m in (NSA, DIFF, FOX) for n in PROJ[m] if n in T_CHUNKS]
        NORMS = [n for m, n in NORM_JOBS]
        rs_order = [("N", 0), "nq0", ("KC",), "nq1", "slc", "win", "dq0", "dq1", "dk0", "dk1"]
        rs_order += [("SUB", i) for i in range(TT)] + ["fq0", "fq1", "fk0", "fk1", ("N", 1)]
        rs_at = {k: n + TT for n, k in enumerate(rs_order)}

        def operands(m, u):
            kind, h, c, i = u
            if kind in ("slc", "win"):
                kc = (0 if kind == "slc" else 2) + h // 4
                return slice(64 * (h % 2), 64 * (h % 2) + 64), h, kc, kc
            if kind == "diff":
                h = 2 * h + c
            return slice(64 * (h % 2), 64 * (h % 2) + 64), h, h, h // 2

        def unit_no(m, j):
            return sum(len(units_of(q)) for q in range(m)) + j

        def v_cols(u):
            kind, h, c, i = u
            if kind == "slc":
                return h // 4 * 64, 64
            if kind == "win":
                return 128 + h // 4 * 64, 64
            if kind == "diff":
                return h * P, P
            return h * 64, 64

        block = ctx.enter_context(nc.Block())

        @block.sync
        def _(sp):
            xv = x[0].rearrange("(t p) d -> t p d", p=P)
            for t in range(TT):
                sp.dma_start(x0[:, t, :], xv[t]).then_inc(x_in[t], 16)
            sp.dma_start(ident[:, :], consts[:, K_ID:K_ID + P]).then_inc(id_in, 16)

            def load(b, slot, first):
                if not first:
                    sp.wait_ge(lo_ready, b - 1)
                sp.dma_start(raw[slot][:, :], wblk[bass.ds(b, 1)].rearrange("o p n -> p (o n)")).then_inc(raw_in[slot], 16)

            load(0, 0, True)
            sp.dma_start(par[:, :], params).then_inc(par_in, 16)
            sp.dma_start(raw[1][:, 0:KD * 32], wblk[1, :, 0:KD * 32]).then_inc(raw_in[1], 16)
            sp.dma_start(stage[:, :], consts[:, 0:K_U]).then_inc(const_in, 16)
            sp.dma_start(later[:, :], consts[:, K_U:K_U + 896]).then_inc(const_in, 16)
            load(2, 0, False)
            load(3, 1, False)
            sp.dma_start(w1_sb[:, :, :, :], w1).then_inc(cw_in, 16)
            sp.dma_start(w2_sb[:, :, :], w2).then_inc(cw_in, 16)
            with sp.Fori(4, BI[("wo", 2)], 2) as i:
                load(i, 0, False)
                load(i + 1, 1, False)
            sp.wait_ge(merged_ready, 2 * KD)
            sp.dma_start(hid[:, :, :], x[0].rearrange("(t p) d -> p t d", p=P)).then_inc(h_in, 16)
            with sp.Fori(BI[("wo", 2)], N_BLOCKS - 1, 2) as i:
                load(i, 0, False)
                load(i + 1, 1, False)
            load(N_BLOCKS - 1, (N_BLOCKS - 1) % 2, False)
            outv = out[0].rearrange("(t p) d -> p t d", p=P)
            for n in range(4):
                sp.wait_ge(out_ready, 2 * n + 2)
                sp.dma_start(outv[:, :, n * 256:(n + 1) * 256], outt[:, :, n * 256:(n + 1) * 256]).then_inc(out_done, 16)
            sp.wait_ge(out_done, 64)

        @block.scalar
        def _(act):
            links = [0]

            def link(ins):
                links[0] += 1
                ins.then_inc(act_link, 1)
                act.wait_ge(act_link, links[0])

            def split_hi(slot, fills):
                act.wait_ge(raw_in[slot], fills * 16)
                nc.scalar.activation(wh[slot][:, :], raw[slot][:, :], ACT.Copy).then_inc(hi_ready, 4)

            def split(b, piece=None):
                if b >= 2 and piece in (None, 0):
                    full(act, last_result[b - 2])
                if b == BI[(NSA, "small")]:
                    act.wait_ge(raw_in[1], 16)
                    nc.scalar.activation(wh[1][:, 0:KD * 32], raw[1][:, 0:KD * 32], ACT.Copy).then_inc(hi_ready, 4)
                    return
                if piece is None:
                    return split_hi(b % 2, b // 2 + 1)
                if piece == 0:
                    act.wait_ge(raw_in[b % 2], (b // 2 + 1) * 16)
                cols = slice(piece * 512, piece * 512 + 512)
                nc.scalar.activation(wh[b % 2][:, cols], raw[b % 2][:, cols], ACT.Copy).then_inc(hi_ready, 1)

            def take_hi(key, dst, src, scale):
                full(act, key)
                nc.scalar.activation(dst, src, ACT.Copy, scale=scale).then_inc(hi_taken, 1)

            def inv_rms(dst, src, width):
                rows, n = src.shape[0], src.shape[1]
                link(nc.scalar.activation(lnv[0:rows, 0:n], src, ACT.Ln, scale=1.0 / width, bias=epsc[0:rows, :]))
                nc.scalar.activation(dst, lnv[0:rows, 0:n], ACT.Exp, scale=-0.5).then_inc(rstd_ready, 1)

            def post(m, name):
                if name in T_CHUNKS:
                    w = P if name in ("slc", "win") else 256
                    n = NORMS.index(name)
                    for half in range(2):
                        full(act, ("P", m, name, half))
                        src = bank(("P", m, name, half))[:, :].rearrange("p (t c) -> p t c", t=2)
                        if name in ("slc", "win"):
                            vc = 0 if name == "slc" else P
                            nc.scalar.activation(V[:, 2 * half:2 * half + 2, vc:vc + P], src[:, :, P:], ACT.Copy)
                        nc.scalar.activation(sq[:, half, 0:2 * w].rearrange("p (t c) -> p t c", t=2), src[:, :, 0:w],
                                             ACT.Square).then_inc(sq_ready, 1)
                    act.wait_ge(hss_ready, 2 * (n + 1))
                    inv_rms(rstd[:, :], hss[:, :, :].rearrange("p t h -> p (t h)"), HD)
                elif name in ("dv0", "dv1", "fv0", "fv1"):
                    vc = 256 * int(name[2])
                    for half in range(2):
                        full(act, ("P", m, name, half))
                        b = place[("P", m, name, half)][0]
                        nc.scalar.activation(V[:, 2 * half:2 * half + 2, vc:vc + 256],
                                             ps[b][:, :].rearrange("p (t c) -> p t c", t=2), ACT.Copy).then_inc(psum_free[b], 1)

            def post_t(m, name):
                if name == "small":
                    act.wait_ge(const_ready, 1)
                    free(act, ("ST",))
                    nc.scalar.activation(gsm[:, :, :], smallt[:, :, 0:24], ACT.Exp, scale=-1.0).then_inc(small_a, 1)
                    act.wait_ge(small_v, 1)
                    link(nc.scalar.activation(lf1[:, :, :], logf[:, :, :], ACT.Abs))
                    link(nc.scalar.activation(lf1[:, :, :], lf1[:, :, :], ACT.Exp, scale=-1.0))
                    nc.scalar.activation(lf2[:, :, :], lf1[:, :, :], ACT.Ln, bias=1.0).then_inc(small_a, 1)
                    act.wait_ge(small_v, 3)
                    nc.scalar.activation(lame[:, :], lamt[:, :], ACT.Exp).then_inc(small_a, 1)
                for c in T_CHUNKS.get(name, []):
                    g = GAIN[name]
                    chunk = QK_CHUNK[name] + c
                    key = ("T", m, name, c)
                    if name in ("slc", "win"):
                        take_hi(key, k_hh[:, chunk - 4, :], bank(key)[:, :], par[:, g:g + 1])
                        continue
                    full(act, key)
                    for e in range(2):
                        home = slice(64 * e, 64 * e + 64)
                        src, gain = bank(key)[home, :], par[home, g:g + 1]
                        if chunk < 4:
                            ins = nc.scalar.activation(q_hl[home, 2 * chunk + e, :], src, ACT.Copy, scale=gain)
                        else:
                            for r in range(2):
                                dst = k_hh[64 * r:64 * r + 64, 2 * (chunk - 4) + e, :]
                                ins = nc.scalar.activation(dst, src, ACT.Copy, scale=gain)
                    ins.then_inc(hi_taken, 1)

            def compression(name):
                if name == "nq0":
                    full(act, ("H", 0))
                    b = place[("H", 0)][0]
                    nc.scalar.activation(chid[:, 0, 0:64], ps[b][:, 0:64], ACT.Gelu_apprx_tanh).then_inc(psum_free[b], 1)
                    full(act, ("H", 1))
                    b = place[("H", 1)][0]
                    hv = chid[:, 1, :].rearrange("p (g r n) -> p g r n", g=2, r=2)
                    for r in range(2):
                        ins = nc.scalar.activation(hv[:, :, r, :], ps[b][:, 0:64].rearrange("p (g n) -> p g n", g=2), ACT.Gelu_apprx_tanh)
                    ins.then_inc(psum_free[b], 1)
                    nc.scalar.preload_act_table_set(LN_EXP)
                elif name == "nq1":
                    full(act, ("KC",))
                    nc.scalar.activation(ksq[:, :], bank(("KC",))[0:HD, 0:HD], ACT.Square).then_inc(ksq_ready, 1)
                    act.wait_ge(kss_ready, 1)
                    inv_rms(rstd[0:HD, 0:1], kss[:, :], HD)
                elif name == "slc":
                    take_hi(("KCT",), kc_hh[:, :, :], bank(("KCT",))[:, 0:64].rearrange("p (g n) -> p g n", g=2), par[:, C_KG:C_KG + 1])
                    full(act, ("F",))
                    nc.scalar.activation(fT[0:8, :], bank(("F",))[0:8, :], ACT.Copy, scale=-1.0).then_inc(hi_taken, 1)

            nc.scalar.preload_act_table_set(LN_EXP)
            act.wait_ge(eps_set, 1)
            for t in range(TT):
                act.wait_ge(x_in[t], 16)
                nc.scalar.activation(xn0[:, t, 0:S], x0[:, t, 0:S], ACT.Square, accum_out=xss[:, t, 0:1]).then_inc(xsq_ready, 1)
                act.wait_ge(x_sums, t + 1)
                link(nc.scalar.activation(lnv[:, t:t + 1], ss[:, t:t + 1], ACT.Ln, scale=1.0 / D, bias=epsc[:, :]))
                nc.scalar.activation(rstd[:, t:t + 1], lnv[:, t:t + 1], ACT.Exp, scale=-0.5).then_inc(rstd_ready, 1)
            act.wait_ge(par_in, 16)
            for k in range(KD):
                if k % 2 == 0:
                    split(0, k // 2)
                take_hi(("N", 0, k), aT_h[:, k, :], bank(("N", 0, k))[:, :], par[:, C_ATTN + k:C_ATTN + k + 1])
            split(1)

            for m in (NSA, DIFF, FOX):
                units = units_of(m)
                if m > NSA:
                    nc.scalar.preload_act_table_set(LN_EXP)
                for n in range(1, len(PROJ[m])):
                    prev, name = PROJ[m][n - 1], PROJ[m][n]
                    if m == NSA or n > 1:
                        split(BI[(m, name)] + 1)
                        post(m, prev)
                    post_t(m, prev)
                    if m == NSA:
                        compression(name)
                post(m, PROJ[m][-1])

                if m == FOX:
                    act.wait_ge(merged_ready, KD)
                for e in EVENTS[m]:
                    what, j = e[0], e[1] if len(e) > 1 else None
                    if what == "T":
                        post_t(m, PROJ[m][-1])
                    if what == "S":
                        s0, n = span(units[j])
                        b = place[("S", m, j)][0]
                        act.wait_ge(max_ready, unit_no(m, j) + 1)
                        nc.scalar.activation(prob[:, j % 4, 0:n], ps[b][:, 0:n], ACT.Exp, bias=nmx[:, j:j + 1],
                                             accum_out=lsum[:, j:j + 1]).then_inc(psum_free[b], 1)
                    elif what == "A" and pv_index(m, j) % 2 == 1:
                        s0, n = span(units[j])
                        b = place[("A", m, j)][0]
                        full(act, ("A", m, j))
                        nc.scalar.activation(probT[:, 1, 0:n], ps[b][:, 0:n], ACT.Copy).then_inc(psum_free[b], 1)
                    elif what == "G":
                        for f in range(e[1], e[2]):
                            if (f + 1) % GATE_STEPS == 0:
                                c = f // GATE_STEPS
                                full(act, ("G", m, c))
                                if m > NSA:
                                    free(act, ("B", m - 1, c))
                                b = place[("G", m, c)][0]
                                nc.scalar.activation(gate[:, c, :], ps[b][:, :], ACT.Tanh, scale=0.5).then_inc(psum_free[b], 1)
                    elif what == "W":
                        split(j, e[2])
                    elif what == "SC":
                        free(act, ("SC", j))
                        nc.scalar.activation(pc[:, j % 2], pc[:, j % 2], ACT.Exp).then_inc(cexp_ready, 1)
                    elif what == "TC":
                        b = place[("TC", j)][0]
                        full(act, ("TC", j))
                        nc.scalar.activation(pcT[:, :, :], ps[b][:, 0:256].rearrange("p (e t) -> p e t", e=2),
                                             ACT.Copy).then_inc(psum_free[b], 1)
                    elif what == "SUB":
                        last = len(units) // TT * (j + 1) - 1
                        free(act, ("O", m, last - 2))
                        free(act, ("O", m, last))
                        nc.scalar.activation(sq[:, 0, :], otok[:, j % 2, :], ACT.Square).then_inc(sub_sq, 1)
                        nc.scalar.preload_act_table_set(LN_EXP)
                    elif what == "SUN":
                        act.wait_ge(sub_sums, j + 1)
                        inv_rms(rstd[:, 4 * j:4 * j + 4], hss[:, j, :], P)
                    elif what == "OT":
                        b = place[("OT", m, j)][0]
                        full(act, ("OT", m, j))
                        nc.scalar.activation(oT_h[:, :, j * P:(j + 1) * P], ps[b][:, :].rearrange("p (k t) -> p k t", k=4), ACT.Copy,
                                             scale=par[:, C_SUBLN:C_SUBLN + 1] if m == DIFF else 1.0).then_inc(oT_hi, 1)
                if m < FOX:
                    post(m + 1, PROJ[m + 1][0])
                    split(BI[(m, "br1")])
                for c in range(KD):
                    if m == FOX:
                        act.wait_ge(merged_ready, KD + c + 1)
                        nc.scalar.activation(mT_h[:, c, :], merged[:, c, :], ACT.Copy, scale=0.5).then_inc(merged_hi, 1)
                    if c % 4 == 3:
                        split(BI[(m, f"br{c // 4}")] + 2)

            def squares(n):
                for t in range(TT):
                    nc.scalar.activation(sq[:, 0, 0:256], hid[:, t, n * 256:(n + 1) * 256], ACT.Square,
                                         accum_out=sst[:, t, n:n + 1]).then_inc(sst_ready, 1)
                    act.wait_ge(sst_ready, TT * n + t + 1)

            def ffn_hi(k):
                take_hi(("N", 1, k), aT_h[:, k, :], bank(("N", 1, k))[:, :], par[:, C_FFN + k:C_FFN + k + 1])

            nc.scalar.preload_act_table_set(LN_EXP)
            for n in range(4):
                for k in range(max(0, 2 * n - 2), 2 * n):
                    ffn_hi(k)
                if n < 3:
                    for half in range(2):
                        free(act, ("WO", n, half))
                    squares(n)
                    split(BI[("wo", n)] + 2)
            ffn_hi(6)
            ffn_hi(7)
            squares(3)
            act.wait_ge(sums_ready, 1)
            inv_rms(rstd[:, 0:TT], ss[:, :], D)
            split(BI[("wo", 3)] + 2)
            nc.scalar.preload_act_table(ACT.Gelu_apprx_tanh)

            with act.Fori(0, N_UP) as i:
                for c in range(2):
                    act.wait_ge(conv_done, 2 * i + (c + 1))
                    nc.scalar.activation(gl[:, c, :], uc[:, c, :], ACT.Gelu_apprx_tanh).then_inc(gelu_ready, 1)
                    if c == 0:
                        act.wait_ge(psum_full[1], i + (up0[1] + 1))
                        split_hi(0, i + (B_UP // 2 + 2))
                for c in range(2):
                    act.wait_ge(psum_free[2 + c], i + (up0[2 + c] + 1))
                    nc.scalar.activation(actT_h[:, bass.ds(2 * i + c, 1), :].rearrange("p o n -> p (o n)"),
                                         av[:, c, :], ACT.Copy).then_inc(act_hi, 1)
                act.wait_ge(psum_full[3], i + (up0[3] + 1))
                split_hi(1, i + (B_UP // 2 + 2))
            for n in range(2, N_DOWN):
                act.wait_ge(down_used, n - 1)
                split_hi(n % 2, (B_DOWN + n) // 2 + 1)
            for d in range(0, KD, 2):
                full(act, ("Y", d))
                b = place[("Y", d)][0]
                nc.scalar.activation(yT[:, d, :], ps[b][:, :], ACT.Copy).then_inc(psum_free[b], 1)

        @block.vector
        def _(dve):
            links = [0]

            def link(ins):
                links[0] += 1
                ins.then_inc(dve_link, 1)
                dve.wait_ge(dve_link, links[0])

            def split_lo(b, slot):
                dve.wait_ge(hi_ready, 4 * b + 4)
                nc.vector.tensor_tensor(wl[slot][:, :], raw[slot][:, :], wh[slot][:, :].bitcast(f32),
                                        ALU.subtract).then_inc(lo_ready, 1)

            def split(b, piece=None):
                if b == BI[(NSA, "small")]:
                    dve.wait_ge(hi_ready, 4 * b + 4)
                    nc.vector.tensor_tensor(wl[1][:, 0:KD * 32], raw[1][:, 0:KD * 32], wh[1][:, 0:KD * 32].bitcast(f32),
                                            ALU.subtract).then_inc(lo_ready, 1)
                    return
                if piece is None:
                    return split_lo(b, b % 2)
                dve.wait_ge(hi_ready, 4 * b + piece + 1)
                cols = slice(piece * 512, piece * 512 + 512)
                ins = nc.vector.tensor_tensor(wl[b % 2][:, cols], raw[b % 2][:, cols], wh[b % 2][:, cols].bitcast(f32), ALU.subtract)
                if piece == 3:
                    ins.then_inc(lo_ready, 1)
                elif b == 0:
                    ins.then_inc(first_lo, 1)

            def take_lo(key, dst, hi, src, scale):
                dve.wait_ge(hi_taken, hi_at[key])
                b = place[key][0]
                nc.vector.scalar_tensor_tensor(dst, src, scale, hi.bitcast(f32), ALU.mult, ALU.subtract).then_inc(psum_free[b], 1)

            def post(m, name):
                if name in T_CHUNKS:
                    kv = name in ("slc", "win")
                    w = P if kv else 256
                    nh = w // HD
                    q = NORMS.index(name)
                    for half in range(2):
                        dve.wait_ge(sq_ready, 2 * q + half + 1)
                        nc.vector.tensor_reduce(hss[:, 2 * half:2 * half + 2, 0:nh],
                                                sq[:, half, 0:2 * w].rearrange("p (t h c) -> p t h c", t=2, c=HD),
                                                AX.X, ALU.add).then_inc(hss_ready, 1)
                    if q >= 2:
                        full(dve, ("T", *NORM_JOBS[q - 2], 1))
                    dve.wait_ge(rstd_ready, rs_at[name])
                    for half in range(2):
                        b = place[("P", m, name, half)][0]
                        src = ps[b][:, :].rearrange("p (t h c) -> p t h c", t=2, c=HD)[:, :, 0:nh, :]
                        r = rstd[:, 8 * half:8 * half + 8].rearrange("p (t h) -> p t h", t=2)[:, :, 0:nh].unsqueeze(3).to_broadcast([P, 2, nh, HD])
                        if kv:
                            dst = nrm[q % 2][:, 2 * half:2 * half + 2, :].rearrange("p t (g r c) -> p t g r c", g=2, r=2)
                            nc.vector.tensor_tensor(dst[:, :, :, 0, :], src, r, ALU.mult)
                            ins = nc.vector.tensor_tensor(dst[:, :, :, 1, :], src, r, ALU.mult)
                        else:
                            dst = nrm[q % 2][:, 2 * half:2 * half + 2, :].rearrange("p t (h c) -> p t h c", c=HD)
                            ins = nc.vector.tensor_tensor(dst, src, r, ALU.mult)
                        ins.then_inc(psum_free[b], 1)
                elif name == "cmp":
                    for kv in range(2):
                        key = ("P", m, name, kv)
                        full(dve, key)
                        b = place[key][0]
                        if kv == 1:
                            dve.wait_ge(cpe_ready, 1)
                        for g in range(2):
                            nc.vector.tensor_copy(cx[0:64, g, :], ps[b][64 * g:64 * g + 64, :])
                            ins = nc.vector.tensor_copy(cx[64:128, g, 0:S - 1], ps[b][64 * g:64 * g + 64, 1:S])
                        ins.then_inc(psum_free[b], 1)
                        free(dve, key)
                        nc.vector.memset(cpe[:, kv, :, :, NCMP:NCMP + 1], 0.0)
                        for g in range(2):
                            pairs = cx[:, g, :].rearrange("p (n r two) -> p two r n", r=8, two=2)[:, 0]
                            for r in range(2):
                                c0 = C_PE + 16 * kv + 8 * r
                                pe_ = par[:, c0:c0 + 8].unsqueeze(2).to_broadcast([P, 8, NCMP])
                                ins = nc.vector.tensor_tensor(cpe[:, kv, 8 * r:8 * r + 8, g, 0:NCMP], pairs[:, :, r:r + NCMP],
                                                              pe_, ALU.add)
                        ins.then_inc(cpe_ready, 1)
                elif name == "small":
                    full(dve, ("P", m, name, 0))
                    b = place[("P", m, name, 0)][0]
                    nc.vector.tensor_copy(smT[:, :], ps[b][0:32, :]).then_inc(psum_free[b], 1)

            def post_t(m, name):
                if name == "small":
                    dve.wait_ge(const_ready, 1)
                    full(dve, ("ST",))
                    b = place[("ST",)][0]
                    nc.vector.tensor_copy(smallt[:, :, :], ps[b][:, 0:P].rearrange("p (t c) -> p t c", t=TT)).then_inc(psum_free[b], 1)
                    free(dve, ("ST",))
                    fb = par[:, C_FOXB:C_FOXB + 8].unsqueeze(1).to_broadcast([P, TT, 8])
                    nc.vector.tensor_tensor(logf[:, :, :], smallt[:, :, 24:32], fb, ALU.add).then_inc(small_v, 1)
                    lv = par[:, C_LAM:C_LAM + 4 * HD].rearrange("p (a b c) -> p a b c", a=2, b=2)
                    nc.vector.tensor_tensor(lprod[:, :, :], lv[:, :, 0, :], lv[:, :, 1, :], ALU.mult).then_inc(small_v, 1)
                    dve.wait_ge(small_v, 2)
                    nc.vector.tensor_reduce(lamt[:, :], lprod[:, :, :], AX.X, ALU.add).then_inc(small_v, 1)
                    dve.wait_ge(small_a, 1)
                    link(nc.vector.tensor_scalar(gsm[:, :, :], gsm[:, :, :], 1.0, None, ALU.add))
                    link(nc.vector.reciprocal(gsm[:, :, :], gsm[:, :, :]))
                    dve.wait_ge(small_a, 2)
                    link(nc.vector.tensor_scalar(lf1[:, :, :], logf[:, :, :], 0.0, None, ALU.min))
                    nc.vector.tensor_tensor(logf[:, :, :], lf1[:, :, :], lf2[:, :, :], ALU.subtract).then_inc(small_v, 1)
                    dve.wait_ge(small_a, 3)
                    link(nc.vector.scalar_tensor_tensor(neglam[:, :], lame[:, 1:2], -LAM_INIT, lame[:, 0:1], ALU.add, ALU.subtract))
                for c in T_CHUNKS.get(name, []):
                    g = GAIN[name]
                    chunk = QK_CHUNK[name] + c
                    key = ("T", m, name, c)
                    if name in ("slc", "win"):
                        take_lo(key, k_l[:, chunk - 4, :], k_hh[:, chunk - 4, :], bank(key)[:, :], par[:, g:g + 1])
                        continue
                    dve.wait_ge(hi_taken, hi_at[key])
                    for e in range(2):
                        home, other = slice(64 * e, 64 * e + 64), slice(64 - 64 * e, 128 - 64 * e)
                        if chunk < 4:
                            dst, hi = q_hl[other, 2 * chunk + e, :], q_hl[home, 2 * chunk + e, :]
                        else:
                            dst, hi = k_l[home, chunk - 4, :], k_hh[home, 2 * (chunk - 4) + e, :]
                        ins = nc.vector.scalar_tensor_tensor(dst, bank(key)[home, :], par[home, g:g + 1], hi.bitcast(f32), ALU.mult, ALU.subtract)
                    ins.then_inc(psum_free[place[key][0]], 1)

            def compression(name):
                if name == "nq1":
                    dve.wait_ge(ksq_ready, 1)
                    nc.vector.tensor_reduce(kss[:, :], ksq[:, :], AX.X, ALU.add).then_inc(kss_ready, 1)
                    link(nc.vector.memset(vblk[:, :, :], 0.0))
                    full(dve, ("VC",))
                    b = place[("VC",)][0]
                    for a in range(4):
                        ins = nc.vector.tensor_copy(vblk[32 * a:32 * a + 32, a, :], ps[b][32 * a:32 * a + 32, 0:HD])
                    ins.then_inc(psum_free[b], 1)
                    dve.wait_ge(rstd_ready, rs_at[("KC",)])
                    b = place[("KC",)][0]
                    nc.vector.tensor_scalar(ktok[:, 0, :], ps[b][0:HD, 0:HD], rstd[0:HD, 0:1], None, ALU.mult)
                    nc.vector.tensor_scalar(ktok[:, 1, :], ps[b][0:HD, 0:HD], rstd[0:HD, 0:1], None, ALU.mult).then_inc(psum_free[b], 1)
                elif name == "slc":
                    dve.wait_ge(hi_taken, hi_at[("KCT",)])
                    for e in range(2):
                        home = slice(64 * e, 64 * e + 64)
                        src = bank(("KCT",))[home, 0:64].rearrange("p (g n) -> p g n", g=2)
                        ins = nc.vector.scalar_tensor_tensor(kc_l[home, :, e, :], src, par[home, C_KG:C_KG + 1], kc_hh[home, :, :].bitcast(f32),
                                                             ALU.mult, ALU.subtract)
                    ins.then_inc(psum_free[place[("KCT",)][0]], 1)
                    dve.wait_ge(hi_taken, hi_at[("F",)])
                    b = place[("F",)][0]
                    nc.vector.scalar_tensor_tensor(fT[32:40, :], ps[b][0:8, :], -1.0, fT[0:8, :].bitcast(f32), ALU.mult,
                                                   ALU.subtract).then_inc(psum_free[b], 1)

            nc.vector.memset(epsc[:, :], EPS).then_inc(eps_set, 1)
            for t in range(TT):
                dve.wait_ge(x_in[t], 16)
                nc.vector.scalar_tensor_tensor(xn0[:, t, S:D], x0[:, t, S:D], 1.0, x0[:, t, S:D], ALU.mult, ALU.mult,
                                               accum_out=xss[:, t, 1:2]).then_inc(xsq_ready, 1)
                dve.wait_ge(xsq_ready, 2 * t + 2)
                nc.vector.tensor_tensor(ss[:, t:t + 1], xss[:, t, 0:1], xss[:, t, 1:2], ALU.add).then_inc(x_sums, 1)
                dve.wait_ge(rstd_ready, t + 1)
                nc.vector.tensor_scalar(xn0[:, t, :], x0[:, t, :], rstd[:, t:t + 1], None, ALU.mult).then_inc(xn_ready, 1)
            dve.wait_ge(par_in, 16)
            link(nc.vector.tensor_scalar(par[:, C_QG:C_QG + 3], par[:, C_QG:C_QG + 3], HD ** -0.5, None, ALU.mult))
            link(nc.vector.tensor_scalar(par[:, C_SUBLN:C_SUBLN + 1], par[:, C_SUBLN:C_SUBLN + 1], 1.0 - LAM_INIT, None, ALU.mult))
            for k in range(KD):
                if k % 2 == 0:
                    split(0, k // 2)
                take_lo(("N", 0, k), aT_l[:, k, :], aT_h[:, k, :], bank(("N", 0, k))[:, :], par[:, C_ATTN + k:C_ATTN + k + 1])
            split(1)
            for m in (NSA, DIFF, FOX):
                units = units_of(m)
                for n in range(1, len(PROJ[m])):
                    prev, name = PROJ[m][n - 1], PROJ[m][n]
                    if m == NSA or n > 1:
                        split(BI[(m, name)] + 1)
                        post(m, prev)
                    post_t(m, prev)
                    if m == NSA:
                        compression(name)
                post(m, PROJ[m][-1])

                if m == FOX:
                    dve.wait_ge(merged_ready, KD)
                for e in EVENTS[m]:
                    what, j = e[0], e[1] if len(e) > 1 else None
                    if what == "T":
                        post_t(m, PROJ[m][-1])
                    if what in ("S", "C", "A", "O"):
                        kind, h, c, i = units[j]
                        s0, n = span(units[j])
                    if what == "S":
                        full(dve, ("S", m, j))
                        nc.vector.tensor_reduce(nmx[:, j:j + 1], bank(("S", m, j))[:, 0:n], AX.X, ALU.max, negate=True).then_inc(max_ready, 1)
                    elif what == "C":
                        free(dve, ("S", m, j))
                        if m == DIFF:
                            free(dve, ("S", m, j - 1))
                            link(nc.vector.reciprocal(rl[:, j - 1:j + 1], lsum[:, j - 1:j + 1]))
                            link(nc.vector.tensor_scalar(coef[:, j:j + 1], rl[:, j:j + 1], neglam[:, 0:1], None, ALU.mult))
                            dst = prob[:, 4 + (j // 2) % 2, 0:n]
                            link(nc.vector.tensor_scalar(dst, prob[:, (j - 1) % 4, 0:n], rl[:, j - 1:j], None, ALU.mult))
                            nc.vector.scalar_tensor_tensor(dst, prob[:, j % 4, 0:n], coef[:, j:j + 1], dst, ALU.mult, ALU.add).then_inc(comb_ready, 1)
                        else:
                            link(nc.vector.reciprocal(rl[:, j:j + 1], lsum[:, j:j + 1]))
                            if m == NSA:
                                gi = 8 * (1 if kind == "slc" else 2) + h
                                link(nc.vector.tensor_scalar(coef[:, j:j + 1], rl[:, j:j + 1], gsm[:, i, gi:gi + 1], None, ALU.mult))
                    elif what == "A" and pv_index(m, j) % 2 == 0:
                        b = place[("A", m, j)][0]
                        full(dve, ("A", m, j))
                        nc.vector.tensor_copy(probT[:, 0, 0:n], ps[b][:, 0:n]).then_inc(psum_free[b], 1)
                    elif what == "O":
                        b = place[("O", m, j)][0]
                        full(dve, ("O", m, j))
                        dst = otok[:, i % 2, h * HD:(h + 1) * HD]
                        if m == NSA:
                            free(dve, ("OC", i, h % 2) if kind == "slc" else ("O", m, j - 1))
                            nc.vector.scalar_tensor_tensor(dst, ps[b][:, 0:HD], coef[:, j:j + 1], dst, ALU.mult, ALU.add).then_inc(psum_free[b], 1)
                        elif m == DIFF:
                            nc.vector.tensor_copy(otok[:, i % 2, h * P:(h + 1) * P], ps[b][:, 0:P]).then_inc(psum_free[b], 1)
                        else:
                            nc.vector.tensor_scalar(dst, ps[b][:, 0:HD], rl[:, j:j + 1], None, ALU.mult).then_inc(psum_free[b], 1)
                    elif what == "WL":
                        split(j, e[2])
                    elif what == "SC":
                        full(dve, ("SC", j))
                        b = place[("SC", j)][0]
                        src = ps[b][:, 0:256].rearrange("p (a e n) -> p e a n", a=4, e=2)
                        cm = cmx[:, :].rearrange("p (e a) -> p e a", e=2)
                        link(nc.vector.tensor_reduce(cm, src, AX.X, ALU.max))
                        nc.vector.tensor_tensor(pc[:, j % 2], src, cm.unsqueeze(3).to_broadcast([P, 2, 4, 32]), ALU.subtract).then_inc(psum_free[b], 1)
                    elif what == "CN":
                        dve.wait_ge(cexp_ready, j + 1)
                        pv = pc[:, j % 2].rearrange("p e a n -> p (e a) n")
                        link(nc.vector.tensor_reduce(csum[:, :], pv, AX.X, ALU.add))
                        link(nc.vector.reciprocal(crl[:, :], csum[:, :]))
                        if j == 0:
                            link(nc.vector.tensor_scalar(crl[:, :], crl[:, :], valid[:, 0:1], None, ALU.mult))
                        link(nc.vector.tensor_tensor(ccoef[:, :].rearrange("p (e a) -> p e a", e=2), crl[:, :].rearrange("p (e a) -> p e a", e=2),
                                                     gsm[:, j, 0:8].rearrange("p (a e) -> p e a", e=2), ALU.mult))
                        nc.vector.tensor_tensor(pv, pv, ccoef[:, :].unsqueeze(2).to_broadcast([P, 8, 32]), ALU.mult).then_inc(pc_ready, 1)
                    elif what == "OC":
                        for k in range(2):
                            full(dve, ("OC", j, k))
                            b = place[("OC", j, k)][0]
                            dst = otok[:, j % 2, :].rearrange("p (a e c) -> p e a c", e=2, c=HD)[:, k]
                            nc.vector.tensor_copy(dst, ps[b][:, 0:256].rearrange("p (a c) -> p a c", a=4)).then_inc(psum_free[b], 1)
                    elif what == "SUB":
                        dve.wait_ge(sub_sq, j + 1)
                        nc.vector.tensor_reduce(hss[:, j, :], sq[:, 0, :].rearrange("p (h c) -> p h c", c=P), AX.X, ALU.add).then_inc(sub_sums, 1)
                    elif what == "SUN":
                        dve.wait_ge(rstd_ready, rs_at[("SUB", j)])
                        v = otok[:, j % 2, :].rearrange("p (h c) -> p h c", c=P)
                        nc.vector.tensor_tensor(v, v, rstd[:, 4 * j:4 * j + 4].unsqueeze(2).to_broadcast([P, 4, P]), ALU.mult).then_inc(sub_ready, 1)
                    elif what == "OT":
                        dve.wait_ge(oT_hi, TT * m + j + 1)
                        b = place[("OT", m, j)][0]
                        nc.vector.scalar_tensor_tensor(oT_l[:, :, j * P:(j + 1) * P], ps[b][:, :].rearrange("p (k t) -> p k t", k=4),
                                                       par[:, C_SUBLN:C_SUBLN + 1] if m == DIFF else 1.0,
                                                       oT_h[:, :, j * P:(j + 1) * P].bitcast(f32), ALU.mult, ALU.subtract).then_inc(psum_free[b], 1)
                if m < FOX:
                    post(m + 1, PROJ[m + 1][0])
                    split(BI[(m, "br1")])
                def merged_part(c):
                    dve.wait_ge(merged_hi, c + 1)
                    nc.vector.scalar_tensor_tensor(mT_l[:, c, :], merged[:, c, :], 0.5, mT_h[:, c, :].bitcast(f32), ALU.mult,
                                                   ALU.subtract).then_inc(merged_lo, 1)

                for c in range(KD):
                    free(dve, ("G", m, c))
                    full(dve, ("B", m, c))
                    pb = place[("B", m, c)][0]
                    dst = merged[:, c, :] if m == NSA else bt[:, c % 2, :]
                    if m > NSA and c >= 2:
                        dve.wait_ge(merged_ready, (m - 1) * KD + c - 1)
                    nc.vector.scalar_tensor_tensor(dst, gate[:, c, :], 1.0, ps[pb][:, :], ALU.add, ALU.mult).then_inc(psum_free[pb], 1)
                    if m == FOX and c > 0:
                        merged_part(c - 1)
                    if m == FOX and c == KD - 1:
                        merged_part(c)
                    if c % 4 == 3:
                        split(BI[(m, f"br{c // 4}")] + 2)

            def ffn_lo(k):
                take_lo(("N", 1, k), aT_l[:, k, :], aT_h[:, k, :], bank(("N", 1, k))[:, :], par[:, C_FFN + k:C_FFN + k + 1])

            nc.vector.memset(ones[:, :], 1.0).then_inc(diag_ready, 1)
            dve.wait_ge(h_in, 16)
            for n in range(4):
                for half in range(2):
                    full(dve, ("WO", n, half))
                    b = place[("WO", n, half)][0]
                    dst = hid[:, 2 * half:2 * half + 2, n * 256:(n + 1) * 256]
                    nc.vector.tensor_tensor(dst, ps[b][:, :].rearrange("p (t c) -> p t c", t=2), dst, ALU.add).then_inc(psum_free[b], 1)
                for k in range(max(0, 2 * n - 2), 2 * n):
                    ffn_lo(k)
                if n < 3:
                    split(BI[("wo", n)] + 2)
            ffn_lo(6)
            ffn_lo(7)
            dve.wait_ge(sst_ready, 4 * TT)
            nc.vector.tensor_reduce(ss[:, :], sst[:, :, :], AX.X, ALU.add).then_inc(sums_ready, 1)
            dve.wait_ge(rstd_ready, rs_at[("N", 1)])
            for t in range(TT):
                nc.vector.tensor_scalar(diag[:, t, :], ident[:, :], rstd[:, t:t + 1], None, ALU.mult).then_inc(diag_ready, 1)
            split(BI[("wo", 3)] + 2)
            full(dve, ("R",))
            nc.vector.tensor_copy(rstdT[:, :], bank(("R",))[:, :]).then_inc(psum_free[6], 1)
            free(dve, ("R",))

            with dve.Fori(0, N_UP) as i:
                for c in range(2):
                    dve.wait_ge(psum_full[c], i + (up0[c] + 1))
                    nc.vector.tensor_tensor(un[:, c, :], rstdT[:, :], ps[c][:, :], ALU.mult).then_inc(psum_free[c], 1)
                    dve.wait_ge(psum_free[c], i + (up0[c] + 1))

                    def tap(j):
                        return par[:, bass.ds(6 * i + (C_CONVW + 3 * c + j), 1)]

                    nc.vector.tensor_scalar(uc[:, c, :], un[:, c, :], tap(2), par[:, bass.ds(2 * i + (C_CONVB + c), 1)],
                                            ALU.mult, ALU.add).then_inc(conv_step, 1)
                    dve.wait_ge(conv_step, 4 * i + (2 * c + 1))
                    nc.vector.scalar_tensor_tensor(uc[:, c, 1:S], un[:, c, 0:S - 1], tap(1), uc[:, c, 1:S], ALU.mult,
                                                   ALU.add).then_inc(conv_step, 1)
                    dve.wait_ge(conv_step, 4 * i + (2 * c + 2))
                    nc.vector.scalar_tensor_tensor(uc[:, c, 2:S], un[:, c, 0:S - 2], tap(0), uc[:, c, 2:S], ALU.mult,
                                                   ALU.add).then_inc(conv_done, 1)
                dve.wait_ge(conv_done, 2 * i + 2)
                split_lo(B_UP + 2 * i + 2, 0)
                for c in range(2):
                    dve.wait_ge(psum_full[2 + c], i + (up0[2 + c] + 1))
                    dve.wait_ge(glr_ready, 2 * i + (c + 1))
                    nc.vector.tensor_tensor(av[:, c, :], gl[:, c, :], ps[2 + c][:, :], ALU.mult).then_inc(psum_free[2 + c], 1)
                for c in range(2):
                    dve.wait_ge(act_hi, 2 * i + (c + 1))
                    k = bass.ds(2 * i + c, 1)
                    nc.vector.tensor_tensor(actT_l[:, k, :].rearrange("p o n -> p (o n)"), av[:, c, :],
                                            actT_h[:, k, :].rearrange("p o n -> p (o n)").bitcast(f32), ALU.subtract).then_inc(act_lo, 1)
                split_lo(B_UP + 2 * i + 3, 1)
            for n in range(2, N_DOWN):
                split(B_DOWN + n)

            def finish(d):
                full(dve, ("YT", d))
                cols = slice(d * P, (d + 1) * P)
                nc.vector.tensor_tensor(outt[:, :, cols], bank(("YT", d))[:, :].rearrange("p (t c) -> p t c", t=TT), hid[:, :, cols],
                                        ALU.add).then_inc(out_ready, 1)

            for d in range(KD):
                if d % 2 == 1:
                    full(dve, ("Y", d))
                    b = place[("Y", d)][0]
                    nc.vector.tensor_copy(yT[:, d, :], ps[b][:, :]).then_inc(psum_free[b], 1)
                if d >= 2:
                    finish(d - 2)
            finish(KD - 2)
            finish(KD - 1)

        @block.gpsimd
        def _(pool):
            pool.wait_ge(const_in, 32)
            pool.wait_ge(psum_full[7], 1)
            nc.gpsimd.tensor_copy(valid[:, :], stage[:, K_VALID:K_VALID + 1])
            nc.gpsimd.tensor_copy(identr[:, :], stage[:, K_ID:K_ID + P])
            nc.gpsimd.tensor_copy(distD[:, :], stage[:, K_D:K_D + S])
            nc.gpsimd.tensor_copy(distW[:, :], stage[:, K_W:K_W + S])
            nc.gpsimd.tensor_copy(causal[:, :], stage[:, K_M:K_M + P])
            for h in range(8):
                nc.gpsimd.tensor_scalar(biasC[:, :, h, :], stage[:, K_DC:K_DC + P].rearrange("p (t n) -> p t n", t=TT), SLOPES8[h], None, ALU.mult)
            nc.gpsimd.memset(kc_l[:, :, :, :].bitcast(f32), 0.0)
            nc.gpsimd.tensor_copy(sel[:, :, :].rearrange("p h n -> p (h n)"), stage[:, K_SEL:K_SEL + 1024])
            nc.gpsimd.memset(fT[:, :].bitcast(f32), 0.0)
            for h in range(8):
                ins = nc.gpsimd.tensor_scalar(slopeI[:, h, :], stage[:, K_ID:K_ID + P], SLOPES8[h], None, ALU.mult)
            ins.then_inc(const_ready, 1)

            for m in (DIFF, FOX):
                for c in range(KD):
                    free(pool, ("B", m, c))
                    free(pool, ("B", NSA, c))
                    if m == FOX:
                        pool.wait_ge(merged_ready, c + 1)
                    nc.gpsimd.tensor_tensor(merged[:, c, :], merged[:, c, :], bt[:, c % 2, :], ALU.add).then_inc(merged_ready, 1)
            pool.wait_ge(psum_free[6], place[("R",)][1] + 1)
            with pool.Fori(0, N_UP) as i:
                for c in range(2):
                    pool.wait_ge(gelu_ready, 2 * i + (c + 1))
                    nc.gpsimd.tensor_tensor(gl[:, c, :], gl[:, c, :], rstdT[:, :], ALU.mult).then_inc(glr_ready, 1)

        @block.tensor
        def _(pe):
            def begin(key):
                b, r = place[key]
                if r:
                    pe.wait_ge(psum_free[b], r)
                return ps[b]

            def done(key, ins):
                ins.then_inc(psum_full[place[key][0]], 1)

            def passes(dst, a_h, a_l, b_h, b_l, start, stop):
                nc.tensor.matmul(dst, a_h, b_h, start=start, stop=False)
                nc.tensor.matmul(dst, a_h, b_l, start=False, stop=False)
                return nc.tensor.matmul(dst, a_l, b_h, start=False, stop=stop)

            def weights(b, k, cols):
                pe.wait_ge(lo_ready, b + 1)
                return [w[b % 2][:, 0:k * cols].rearrange("p (k c) -> p k c", k=k) for w in (wh, wl)]

            def project(b, keys, tiles=(0, 1)):
                h, l = weights(b, KD, 256)
                for key in keys:
                    half = key[3]
                    bk = begin(key) if 0 in tiles else bank(key)
                    for t in tiles:
                        rows = slice((2 * half + t) * P, (2 * half + t + 1) * P)
                        for k in range(KD):
                            ins = passes(bk[:, t * 256:(t + 1) * 256], aT_h[:, k, rows], aT_l[:, k, rows], h[:, k], l[:, k],
                                         k == 0, k == KD - 1)
                    if 1 in tiles:
                        done(key, ins)

            def transposes(key, blocks):
                bk = begin(key)
                for n, src in enumerate(blocks):
                    ins = nc.tensor.transpose(bk[:, n * P:(n + 1) * P], src, ident[:, :])
                done(key, ins)

            def post_t(m, name):
                if name == "small":
                    free(pe, ("P", NSA, "small", 0))
                    bk = begin(("ST",))
                    for t in range(TT):
                        ins = nc.tensor.transpose(bk[:, 32 * t:32 * t + 32], smT[:, t * P:(t + 1) * P], ident[0:32, 0:32])
                    done(("ST",), ins)
                if name not in T_CHUNKS:
                    return
                for half in range(2):
                    free(pe, ("P", m, name, half))
                q = NORMS.index(name)
                for c in T_CHUNKS[name]:
                    transposes(("T", m, name, c), [nrm[q % 2][:, t, c * P:(c + 1) * P] for t in range(TT)])

            def compression(name):
                if name == "nq0":
                    pe.wait_ge(cw_in, 32)
                    for kv in range(2):
                        pe.wait_ge(cpe_ready, kv + 1)
                        bk = begin(("H", kv))
                        for r in range(16):
                            ins = nc.tensor.matmul(bk[:, 0:64], w1_sb[:, kv, r, :], cpe[:, kv, r], start=r == 0, stop=r == 15)
                        done(("H", kv), ins)
                elif name == "nq1":
                    free(pe, ("H", 0))
                    bk = begin(("KC",))
                    done(("KC",), nc.tensor.matmul(bk[0:HD, 0:HD], chid[:, 0, 0:64], w2_sb[:, 0, :], start=True, stop=True))
                    free(pe, ("H", 1))
                    bk = begin(("VC",))
                    done(("VC",), nc.tensor.matmul(bk[:, 0:HD], chid[:, 1, :], w2_sb[:, 1, :], start=True, stop=True))
                elif name == "slc":
                    free(pe, ("KC",))
                    bk = begin(("KCT",))
                    done(("KCT",), nc.tensor.transpose(bk[:, 0:64], ktok[:, :, :].rearrange("n r c -> n (r c)"), ident[0:HD, 0:HD]))
                    pe.wait_ge(small_v, 4)
                    bk = begin(("F",))
                    for i in range(TT):
                        ins = nc.tensor.matmul(bk[0:8, i * P:S], logf[:, i, :], later[:, 384:384 + S - P * i], start=i == 0, stop=i == TT - 1)
                    done(("F",), ins)

            pe.wait_ge(id_in, 16)
            for t in range(TT):
                for k in range(KD):
                    if k == 0:
                        pe.wait_ge(xn_ready, t + 1)
                    ins = nc.tensor.transpose(ps[k][:, t * P:(t + 1) * P], xn0[:, t, k * P:(k + 1) * P], ident[:, :])
                    if t == TT - 1:
                        done(("N", 0, k), ins)

            for m in (NSA, DIFF, FOX):
                units = units_of(m)
                for n, name in enumerate(PROJ[m]):
                    b = BI[(m, name)]
                    if name == "cmp":
                        h, l = [w[0][:, :].rearrange("p (k c) -> p k c", k=KD) for w in (wh, wl)]
                        for k in range(KD):
                            if k % 2 == 0:
                                pe.wait_ge(*((first_lo, k // 2 + 1) if k < 6 else (lo_ready, 1)))
                            free(pe, ("N", 0, k))
                            for c in range(2):
                                key = ("P", m, name, c)
                                bk = begin(key) if k == 0 else bank(key)
                                cols = slice(c * P, (c + 1) * P)
                                ins = passes(bk[:, :], h[:, k, cols], l[:, k, cols], aT_h[:, k], aT_l[:, k], k == 0, k == KD - 1)
                                if k == KD - 1:
                                    done(key, ins)
                    elif name == "small":
                        h, l = weights(b, KD, 32)
                        bk = begin(("P", m, name, 0))
                        for k in range(KD):
                            ins = passes(bk[0:32, :], h[:, k], l[:, k], aT_h[:, k], aT_l[:, k], k == 0, k == KD - 1)
                        done(("P", m, name, 0), ins)
                    elif m == NSA or n > 0:
                        project(b, [("P", m, name, c) for c in range(2)])
                    if n > 0:
                        post_t(m, PROJ[m][n - 1])
                    if m == NSA:
                        compression(name)

                def scores(j):
                    u = units[j]
                    kind, h, c, i = u
                    s0, n = span(u)
                    home, qh, kh, kl = operands(m, u)
                    bk = begin(("S", m, j))
                    dst = bk[:, 0:n]
                    if kind == "fox":
                        nc.tensor.matmul(dst, sel[:, h, :], fT[:, 0:n], start=True, stop=False)
                        nc.tensor.matmul(bk[:, n - P:n], identr[:, :], causal[:, :], start=False, stop=False)
                    else:
                        dist = distW if kind == "win" else distD
                        sl = h if kind != "diff" else 2 * h + 1
                        c0 = 384 - P * i + s0
                        nc.tensor.matmul(dst, slopeI[:, sl, :], dist[:, c0:c0 + n], start=True, stop=False)
                    t = slice(i * P, (i + 1) * P)
                    nc.tensor.matmul(dst, q_hl[:, qh, t], k_hh[:, kh, s0:s0 + n], start=False, stop=False)
                    done(("S", m, j), nc.tensor.matmul(dst, q_hl[home, qh, t], k_l[home, kl, s0:s0 + n], start=False, stop=True))

                def values(q):
                    u = units[q]
                    s0, n = span(u)
                    v0, vw = v_cols(u)
                    free(pe, ("A", m, q))
                    for name in PROJ[m]:
                        if name[1] == "v":
                            free(pe, ("P", m, name, 0))
                            free(pe, ("P", m, name, 1))
                    bk = begin(("O", m, q))
                    for kb in range(n // P):
                        ins = nc.tensor.matmul(bk[:, 0:vw], probT[:, pv_index(m, q) % 2, kb * P:(kb + 1) * P],
                                               V[:, s0 // P + kb, v0:v0 + vw], start=kb == 0, stop=kb == n // P - 1)
                    done(("O", m, q), ins)

                def gate_step(f):
                    c, k, p = f // GATE_STEPS, f % GATE_STEPS // 3, f % 3
                    b = BI[(m, f"gate{c // 2}")]
                    if f % GATE_STEPS == 0:
                        weights(b, KD, 256)
                    h, l = [w[b % 2][:, :].rearrange("p (k c) -> p k c", k=KD) for w in (wh, wl)]
                    key = ("G", m, c)
                    bk = begin(key) if f % GATE_STEPS == 0 else ps[place[key][0]]
                    cols = slice(c % 2 * P, c % 2 * P + P)
                    ins = nc.tensor.matmul(bk[:, :], (l if p == 2 else h)[:, k, cols], (aT_l if p == 1 else aT_h)[:, k],
                                           start=f % GATE_STEPS == 0, stop=f % GATE_STEPS == GATE_STEPS - 1)
                    if f % GATE_STEPS == GATE_STEPS - 1:
                        done(key, ins)

                for e in EVENTS[m]:
                    what, j = e[0], e[1] if len(e) > 1 else None
                    if what == "T":
                        post_t(m, PROJ[m][-1])
                    elif what == "S":
                        if j == 0:
                            for name in PROJ[m]:
                                for c in T_CHUNKS.get(name, []):
                                    free(pe, ("T", m, name, c))
                        scores(j)
                    elif what == "G":
                        for f in range(e[1], e[2]):
                            gate_step(f)
                    elif what == "A":
                        if m == DIFF:
                            pe.wait_ge(comb_ready, j // 2 + 1)
                        else:
                            free(pe, ("S", m, j))
                        s0, n = span(units[j])
                        slot = 4 + (j // 2) % 2 if m == DIFF else j % 4
                        transposes(("A", m, j), [prob[:, slot, kb * P:(kb + 1) * P] for kb in range(n // P)])
                    elif what == "O":
                        values(j)
                    elif what == "SC":
                        rows = slice(j * P, (j + 1) * P)
                        if j == 0:
                            pe.wait_ge(const_ready, 1)
                            for name in ("nq0", "nq1"):
                                for c in range(2):
                                    free(pe, ("T", m, name, c))
                            for key in (("VC",), ("KCT",), ("F",)):
                                free(pe, key)
                        bk = begin(("SC", j))
                        nc.tensor.matmul(bk[:, 0:256], identr[:, :], biasC[:, j].rearrange("p h n -> p (h n)"), start=True, stop=False)
                        for h in range(8):
                            dst = bk[:, 32 * h:32 * h + 32]
                            nc.tensor.matmul(dst, q_hl[:, h, rows], kc_hh[:, h // 4], start=False, stop=False)
                            ins = nc.tensor.matmul(dst, q_hl[:, h, rows], kc_l[:, h // 4, h % 2], start=False, stop=h == 7)
                        done(("SC", j), ins)
                    elif what == "TC":
                        pe.wait_ge(pc_ready, j + 1)
                        transposes(("TC", j), [pc[:, j % 2, k].rearrange("p a n -> p (a n)") for k in range(2)])
                    elif what == "OC":
                        free(pe, ("TC", j))
                        for k in range(2):
                            bk = begin(("OC", j, k))
                            done(("OC", j, k), nc.tensor.matmul(bk[:, 0:256], pcT[:, k, :], vblk[:, :, :].rearrange("p a c -> p (a c)"),
                                                                start=True, stop=True))
                    elif what == "OT":
                        last = len(units) // TT * (j + 1) - 1
                        if m == DIFF:
                            pe.wait_ge(sub_ready, j + 1)
                        else:
                            free(pe, ("O", m, last - 1))
                            free(pe, ("O", m, last))
                        transposes(("OT", m, j), [otok[:, j % 2, k * P:(k + 1) * P] for k in range(4)])
                    elif what == "P":
                        name = PROJ[m + 1][0]
                        project(BI[(m + 1, name)], [("P", m + 1, name, j)], (e[2],))

                for c in range(KD):
                    h, l = weights(BI[(m, f"br{c // 4}")], 4, S)
                    bk = begin(("B", m, c))
                    cols = slice(c % 4 * P, c % 4 * P + P)
                    if c == 0:
                        free(pe, ("OT", m, TT - 2))
                        free(pe, ("OT", m, TT - 1))
                    for k in range(4):
                        ins = passes(bk[:, :], h[:, k, cols], l[:, k, cols], oT_h[:, k], oT_l[:, k], k == 0, k == 3)
                    done(("B", m, c), ins)

            def ffn_transposes(k):
                free(pe, ("WO", k // 2, 0))
                free(pe, ("WO", k // 2, 1))
                transposes(("N", 1, k), [hid[:, t, k * P:(k + 1) * P] for t in range(TT)])

            for n in range(4):
                h, l = weights(BI[("wo", n)], KD, 256)
                steps = [(half, t, range(KD)) for half in range(2) for t in range(2)]
                if n == 0:
                    steps = [(0, 0, range(6)), (1, 0, range(6)), (0, 0, (6, 7)), (1, 0, (6, 7)), (0, 1, range(KD)), (1, 1, range(KD))]
                for half, t, ks in steps:
                    key = ("WO", n, half)
                    bk = begin(key) if t == 0 and ks[0] == 0 else bank(key)
                    rows = slice((2 * half + t) * P, (2 * half + t + 1) * P)
                    for k in ks:
                        pe.wait_ge(merged_lo, k + 1)
                        ins = passes(bk[:, t * 256:(t + 1) * 256], mT_h[:, k, rows], mT_l[:, k, rows], h[:, k], l[:, k], k == 0, k == KD - 1)
                    if t == 1:
                        done(key, ins)
                for k in range(max(0, 2 * n - 2), 2 * n):
                    ffn_transposes(k)

            def up_chunk(i, b, c, ks=range(KD), first=False):
                h, l = [w[b][:, :].rearrange("p (k c) -> p k c", k=KD) for w in (wh, wl)]
                bk = 2 * b + c
                if ks[0] == 0:
                    pe.wait_ge(psum_free[bk], i + up0[bk])
                cols = slice(c * P, (c + 1) * P)
                for k in ks:
                    if first:
                        free(pe, ("N", 1, k))
                    ins = passes(ps[bk][:, :], h[:, k, cols], l[:, k, cols], aT_h[:, k], aT_l[:, k], k == 0, k == KD - 1)
                if ks[-1] == KD - 1:
                    ins.then_inc(psum_full[bk], 1)

            pe.wait_ge(lo_ready, B_UP + 1)
            up_chunk(0, 0, 0, range(6), first=True)
            ffn_transposes(6)
            ffn_transposes(7)
            up_chunk(0, 0, 1, range(6))
            up_chunk(0, 0, 0, (6, 7), first=True)
            up_chunk(0, 0, 1, (6, 7))
            pe.wait_ge(diag_ready, TT + 1)
            bk = begin(("R",))
            for t in range(TT):
                ins = nc.tensor.matmul(bk[:, t * P:(t + 1) * P], ones[:, :], diag[:, t, :], start=True, stop=True)
            done(("R",), ins)
            pe.wait_ge(lo_ready, B_UP + 2)
            for c in range(2):
                up_chunk(0, 1, c)
            with pe.Fori(1, N_UP) as i:
                for b in range(2):
                    pe.wait_ge(lo_ready, 2 * i + (B_UP + b + 1))
                    for c in range(2):
                        up_chunk(i, b, c)

            def finish(d):
                free(pe, ("Y", d))
                transposes(("YT", d), [yT[:, d, t * P:(t + 1) * P] for t in range(TT)])

            def down(n, slot, first, last):
                pe.wait_ge(lo_ready, n + (B_DOWN + 1))
                pe.wait_ge(act_lo, 2 * n + 2)
                h, l = [w[slot][:, :].rearrange("p (k c) -> p k c", k=2) for w in (wh, wl)]
                acts = [[t[:, bass.ds(2 * n + k, 1), :].rearrange("p o n -> p (o n)") for t in (actT_h, actT_l)] for k in range(2)]
                for d in range(KD):
                    if first:
                        begin(("Y", d))
                    cols = slice(d * P, (d + 1) * P)
                    for k in range(2):
                        ins = passes(ps[d][:, :], h[:, k, cols], l[:, k, cols], acts[k][0], acts[k][1], first and k == 0, last and k == 1)
                    if last:
                        done(("Y", d), ins)
                        if d >= 2:
                            finish(d - 2)
                if not last:
                    ins.then_inc(down_used, 1)

            down(0, 0, True, False)
            with pe.Fori(1, N_DOWN - 2, 2) as n:
                down(n, 1, False, False)
                down(n + 1, 0, False, False)
            down(N_DOWN - 2, 1, False, False)
            down(N_DOWN - 1, 0, False, True)
            finish(KD - 2)
            finish(KD - 1)


def pack_params(np, a):
    def cols(v):
        return v.reshape(-1, P).T

    def twice(v):
        return np.concatenate([v, v])[:, None]

    conv = a["conv_w"][0].reshape(3, NF, P).transpose(2, 1, 0).reshape(P, 3 * NF)
    pe = [a["cmp_pe"][0, i].reshape(16, P).T for i in range(2)]
    rows = [np.broadcast_to(v.reshape(1, -1), (P, v.size)) for v in (a["diff_lam"][0], a["fox_b"][0])]
    gains = [a["nsa_q_g"][0], a["diff_q_g"][0], a["fox_q_g"][0], a["nsa_k_g"][0, 0], a["nsa_k_g"][0, 1], a["nsa_k_g"][0, 2],
             a["diff_k_g"][0], a["fox_k_g"][0]]
    parts = [cols(a["attn_norm_g"][0]), cols(a["ffn_norm_g"][0]), conv, cols(a["conv_b"][0]), cols(a["diff_subln_g"][0])]
    out = np.concatenate(parts + [twice(g) for g in gains] + pe + rows, axis=1)
    assert out.shape == (P, C_END)
    return np.ascontiguousarray(out)


def pack_constants(np):
    far = -1e30
    c = np.zeros((P, K_END), np.float32)
    p = np.arange(P)[:, None]
    col = np.arange(S)[None, :]
    c[:, K_ID:K_ID + P] = np.eye(P)
    dist = 384 + p - col
    c[:, K_D:K_D + S] = np.where(dist >= 0, -dist, far)
    c[:, K_W:K_W + S] = np.where((dist >= 0) & (dist < 256), -dist, far)
    c[:, K_M:K_M + P] = np.where(np.arange(P)[None, :] <= p, 0.0, far)
    for i in range(TT):
        dc = i * P + p - (16 * np.arange(32)[None, :] + 31)
        c[:, K_DC + 32 * i:K_DC + 32 * i + 32] = np.where(dc >= 0, -dc, far)
    for h in range(8):
        c[h, K_SEL + P * h:K_SEL + P * (h + 1)] = 1.0
        c[32 + h, K_SEL + P * h:K_SEL + P * (h + 1)] = 1.0
    c[:, K_U:K_U + 896] = np.arange(896)[None, :] - 384 >= p
    c[:, K_VALID] = np.arange(P) >= 31
    return c


def pack_weights(np, a):
    w_in, w_br, w_o, w_up, w_down = (a[n][0] for n in ("w_in", "w_br", "w_o", "w_up", "w_down"))
    col = {"nq": 0, "cmp": 512, "slc": 768, "win": 1024, "ngate": 1280, "dq": 1304, "dk": 1816, "dv": 2328,
           "fq": 2840, "fk": 3352, "fv": 3864, "ff": 4376, "mg": 4384}

    def rows_of(w, k):
        return w.reshape(k, P, -1).transpose(1, 0, 2).reshape(P, -1)

    out = np.zeros((N_BLOCKS, P, BLOCK), np.float32)
    for n, (m, name) in enumerate(BLOCKS):
        if m == "wo":
            out[n] = rows_of(w_o[:, 256 * name:256 * name + 256], KD)
        elif name == "small":
            w = np.concatenate([w_in[:, col["ngate"]:col["ngate"] + 24], w_in[:, col["ff"]:col["ff"] + 8]], axis=1)
            out[n][:, 0:KD * 32] = rows_of(w, KD)
        elif name.startswith("gate"):
            c = col["mg"] + D * m + 256 * int(name[4])
            out[n] = rows_of(w_in[:, c:c + 256], KD)
        elif name.startswith("br"):
            h = int(name[2])
            out[n] = rows_of(w_br[m][:, S * h:S * h + S], 4)
        else:
            c = col[name] if name in col else col[name[:2]] + 256 * int(name[2])
            out[n] = rows_of(w_in[:, c:c + 256], KD)
    for i in range(N_UP):
        out[B_UP + 2 * i] = rows_of(w_up[:, 256 * i:256 * i + 256], KD)
        out[B_UP + 2 * i + 1] = rows_of(w_up[:, D_FF + 256 * i:D_FF + 256 * i + 256], KD)
    for n in range(N_DOWN):
        out[B_DOWN + n] = rows_of(w_down[256 * n:256 * n + 256], 2)
    return out


def kernel(**inputs):
    import numpy as np
    import concourse.bacc as bacc
    from concourse.bass_utils import run_bass_kernel_spmd

    a = {k: np.asarray(v) for k, v in inputs.items()}
    arrays = {
        "x": a["x"],
        "wblk": pack_weights(np, a),
        "w1": np.ascontiguousarray(a["cmp_w1"][0].reshape(2, 16, P, P).transpose(2, 0, 1, 3)),
        "w2": np.ascontiguousarray(a["cmp_w2"][0].transpose(1, 0, 2)),
        "params": pack_params(np, a),
        "consts": pack_constants(np),
    }
    nc = bacc.Bacc("TRN2", target_bir_lowering=False, num_devices=1)
    args = [nc.dram_tensor(n, v.shape, mybir.dt.from_np(v.dtype), kind="ExternalInput").ap() for n, v in arrays.items()]
    args.append(nc.dram_tensor("out", (1, S, D), mybir.dt.float32, kind="ExternalOutput").ap())
    build(nc, *args)
    r = run_bass_kernel_spmd(nc, [arrays], core_ids=[0])
    return r.results[0]["out"]
```
